# Optimizing a Trainium2 kernel written in Bass

```python
import math
import jax, jax.numpy as jnp
from jax import lax
import numpy as np

D_MODEL = 2048
BATCH = 1
SEQ = 256
DEPTH = 1

HEAD_DIM = 128
MIX_WIDTH = D_MODEL
DIFF_WIDTH = MIX_WIDTH // 4
DIL_WIDTH = MIX_WIDTH - DIFF_WIDTH
N_DIL_HEADS = DIL_WIDTH // HEAD_DIM
DIL_CONFIGS = ((128, 1), (512, 4), (2048, 16))
DIL_BLOCK = 64
DIFF_QK_DIM = 64
DIFF_V_DIM = 2 * DIFF_QK_DIM
N_DIFF_HEADS = DIFF_WIDTH // DIFF_V_DIM
DIFF_QK_WIDTH = N_DIFF_HEADS * 2 * DIFF_QK_DIM
IN_WIDTH = 3 * DIL_WIDTH + 2 * DIFF_QK_WIDTH + DIFF_WIDTH
Q_BLOCK = 128
ROPE_THETA = 500000.0
ROPE_FRACTION = 4
PEER_HEADS = 8
PEER_N_KEYS = 128
PEER_N_EXPERTS = PEER_N_KEYS * PEER_N_KEYS
PEER_KEY_DIM = 256
PEER_TOPK = 16
PEER_TOKEN_BLOCK = 64
LN_EPS = 1e-5
NEG_BIG = -1e30
DEEPNORM_ALPHA = (2.0 * DEPTH) ** 0.25
DEEPNORM_BETA = (8.0 * DEPTH) ** -0.25

kernel_name = "hybrid_dilated_diffattn_peer_encoder_layer"

def layer_norm(x, g, b):
    xf = x.astype(jnp.float32)
    mu = jnp.mean(xf, -1, keepdims=True)
    xc = xf - mu
    var = jnp.mean(xc * xc, -1, keepdims=True)
    return (xc * lax.rsqrt(var + LN_EPS) * g.astype(jnp.float32) + b.astype(jnp.float32)).astype(x.dtype)

def head_rms(t, g):
    return t * lax.rsqrt(jnp.mean(t * t, -1, keepdims=True) + LN_EPS) * g.astype(jnp.float32)

def rope_tables(seq, rot_dim):
    inv_freq = 1.0 / (ROPE_THETA ** (jnp.arange(0, rot_dim, 2, dtype=jnp.float32) / rot_dim))
    ang = jnp.arange(seq, dtype=jnp.float32)[:, None] * inv_freq[None, :]
    return jnp.cos(ang), jnp.sin(ang)

def partial_rope(t, cos, sin):
    half = cos.shape[-1]
    shp = (1, t.shape[1]) + (1,) * (t.ndim - 3) + (half,)
    c = cos.reshape(shp).astype(t.dtype)
    s = sin.reshape(shp).astype(t.dtype)
    t1 = t[..., :half]
    t2 = t[..., half:2 * half]
    return jnp.concatenate([t1 * c - t2 * s, t1 * s + t2 * c, t[..., 2 * half:]], axis=-1)

def dilated_window_attention(q, k, v, window, dilation):
    B, S, H, dh = q.shape
    L = S // dilation
    half = window // (2 * dilation)
    blk = DIL_BLOCK
    nb = -(-L // blk)
    Lp = nb * blk

    def strided(t):
        t = t.reshape(B, L, dilation, H, dh).transpose(0, 2, 1, 3, 4)
        return jnp.pad(t, ((0, 0), (0, 0), (0, Lp - L), (0, 0), (0, 0)))

    def neighbours(t):
        tp = jnp.pad(t, ((0, 0), (0, 0), (blk, blk), (0, 0), (0, 0))).reshape(B, dilation, nb + 2, blk, H, dh)
        return jnp.concatenate([tp[:, :, :-2], tp[:, :, 1:-1], tp[:, :, 2:]], axis=3)

    qb = strided(q).reshape(B, dilation, nb, blk, H, dh)
    kn = neighbours(strided(k))
    vn = neighbours(strided(v)).astype(jnp.float32)
    s = jnp.einsum('brnqhd,brnkhd->brnhqk', qb, kn).astype(jnp.float32) * (dh ** -0.5)
    qi = jnp.arange(blk)[:, None]
    kj = jnp.arange(3 * blk)[None, :]
    kpos = (jnp.arange(nb)[:, None, None] - 1) * blk + kj[None]
    mask = (jnp.abs(blk + qi - kj) <= half)[None] & (kpos >= 0) & (kpos < L)
    s = jnp.where(mask[None, None, :, None], s, NEG_BIG)
    m = jnp.max(s, -1, keepdims=True)
    p = jnp.exp(s - m)
    den = jnp.sum(p, -1)
    o = jnp.einsum('brnhqk,brnkhd->brnqhd', p, vn) / jnp.swapaxes(den, -1, -2)[..., None]
    lse = jnp.swapaxes(m[..., 0] + jnp.log(den), -1, -2)

    def unstride(t):
        t = t.reshape((B, dilation, Lp) + t.shape[4:])[:, :, :L]
        t = jnp.moveaxis(t, 1, 2)
        return t.reshape((B, S) + t.shape[3:])

    return unstride(o), unstride(lse)

def differential_attention(q, k, v, lam):
    B, S, H, _, dq = q.shape
    nqb = S // Q_BLOCK
    qb = jnp.moveaxis(q.reshape(B, nqb, Q_BLOCK, H, 2, dq), 1, 0)
    vf = v.astype(jnp.float32)
    scale = dq ** -0.5

    def one_block(qblk):
        s = jnp.einsum('bqhmd,bkhmd->bhmqk', qblk, k).astype(jnp.float32) * scale
        p = jax.nn.softmax(s, axis=-1)
        a = p[:, :, 0] - lam * p[:, :, 1]
        return jnp.einsum('bhqk,bkhd->bqhd', a, vf)

    o = lax.map(one_block, qb)
    return jnp.moveaxis(o, 0, 1).reshape(B, S, H, v.shape[-1])

def hybrid_mixer(h, w_in, dil_norm_g, lambda_q1, lambda_k1, lambda_q2, lambda_k2, subln_g, w_out,
                 lam_init, rope_dil, rope_diff):
    B, S, _ = h.shape
    proj = jnp.einsum('bsd,de->bse', h, w_in)
    splits = [DIL_WIDTH, 2 * DIL_WIDTH, 3 * DIL_WIDTH,
              3 * DIL_WIDTH + DIFF_QK_WIDTH, 3 * DIL_WIDTH + 2 * DIFF_QK_WIDTH]
    qa, ka, va, qd, kd, vd = jnp.split(proj, splits, axis=-1)

    qa = partial_rope(qa.reshape(B, S, N_DIL_HEADS, HEAD_DIM), *rope_dil)
    ka = partial_rope(ka.reshape(B, S, N_DIL_HEADS, HEAD_DIM), *rope_dil)
    va = va.reshape(B, S, N_DIL_HEADS, HEAD_DIM)
    outs, lses = [], []
    for window, dilation in DIL_CONFIGS:
        o, l = dilated_window_attention(qa, ka, va, window, dilation)
        outs.append(o)
        lses.append(l)
    wts = jax.nn.softmax(jnp.stack(lses), axis=0)
    dil_out = jnp.sum(wts[..., None] * jnp.stack(outs), axis=0)
    dil_out = head_rms(dil_out, dil_norm_g).reshape(B, S, DIL_WIDTH)

    qd = partial_rope(qd.reshape(B, S, N_DIFF_HEADS, 2, DIFF_QK_DIM), *rope_diff)
    kd = partial_rope(kd.reshape(B, S, N_DIFF_HEADS, 2, DIFF_QK_DIM), *rope_diff)
    vd = vd.reshape(B, S, N_DIFF_HEADS, DIFF_V_DIM)
    lam = (jnp.exp(jnp.sum(lambda_q1.astype(jnp.float32) * lambda_k1.astype(jnp.float32)))
           - jnp.exp(jnp.sum(lambda_q2.astype(jnp.float32) * lambda_k2.astype(jnp.float32)))
           + lam_init)
    od = differential_attention(qd, kd, vd, lam)
    od = head_rms(od, subln_g) * (1.0 - lam_init)

    mixed = jnp.concatenate([dil_out, od.reshape(B, S, DIFF_WIDTH)], axis=-1).astype(h.dtype)
    return jnp.einsum('bse,ed->bsd', mixed, w_out)

def peer_ffn(h, w_query, sub_keys, expert_u, expert_v):
    B, S, D = h.shape
    T = B * S
    xt = h.reshape(T, D)
    q = jnp.einsum('td,de->te', xt, w_query).reshape(T, PEER_HEADS, 2, PEER_KEY_DIM // 2)
    s = jnp.einsum('thcd,hcnd->thcn', q, sub_keys).astype(jnp.float32)
    sv, si = lax.top_k(s, PEER_TOPK)
    cand = (sv[:, :, 0, :, None] + sv[:, :, 1, None, :]).reshape(T, PEER_HEADS, PEER_TOPK * PEER_TOPK)
    cand_idx = (si[:, :, 0, :, None] * PEER_N_KEYS + si[:, :, 1, None, :]).reshape(T, PEER_HEADS, PEER_TOPK * PEER_TOPK)
    top_s, pos = lax.top_k(cand, PEER_TOPK)
    idx = jnp.take_along_axis(cand_idx, pos, axis=-1)
    g = jax.nn.softmax(top_s, axis=-1)

    nblk = T // PEER_TOKEN_BLOCK
    xs = xt.reshape(nblk, PEER_TOKEN_BLOCK, D)
    idxs = idx.reshape(nblk, PEER_TOKEN_BLOCK, PEER_HEADS * PEER_TOPK)
    gs = g.reshape(nblk, PEER_TOKEN_BLOCK, PEER_HEADS * PEER_TOPK)

    def block(args):
        xb, ib, gb = args
        u = expert_u[ib]
        a = gb.astype(xb.dtype) * jax.nn.gelu(jnp.einsum('tkd,td->tk', u, xb), approximate=False)
        return jnp.einsum('tk,tkd->td', a, expert_v[ib])

    y = lax.map(block, (xs, idxs, gs))
    return y.reshape(B, S, D)

def setup_inputs(seed: int = 0) -> dict:
    key = jax.random.key(seed)
    ks = jax.random.split(key, 20)
    f32 = jnp.float32

    def nrm(k, shape, scale):
        return jax.random.normal(k, shape, f32) * scale

    col_scale = jnp.concatenate([
        jnp.ones((2 * DIL_WIDTH,), f32), jnp.full((DIL_WIDTH,), DEEPNORM_BETA, f32),
        jnp.ones((2 * DIFF_QK_WIDTH,), f32), jnp.full((DIFF_WIDTH,), DEEPNORM_BETA, f32)])
    return {
        "x": nrm(ks[0], (BATCH, SEQ, D_MODEL), 1.0),
        "ln_emb_g": 1.0 + nrm(ks[1], (D_MODEL,), 0.02),
        "ln_emb_b": nrm(ks[2], (D_MODEL,), 0.02),
        "w_in": nrm(ks[3], (DEPTH, D_MODEL, IN_WIDTH), D_MODEL ** -0.5) * col_scale,
        "dil_norm_g": 1.0 + nrm(ks[4], (DEPTH, HEAD_DIM), 0.02),
        "lambda_q1": nrm(ks[5], (DEPTH, DIFF_QK_DIM), 0.1),
        "lambda_k1": nrm(ks[6], (DEPTH, DIFF_QK_DIM), 0.1),
        "lambda_q2": nrm(ks[7], (DEPTH, DIFF_QK_DIM), 0.1),
        "lambda_k2": nrm(ks[8], (DEPTH, DIFF_QK_DIM), 0.1),
        "subln_g": 1.0 + nrm(ks[9], (DEPTH, DIFF_V_DIM), 0.02),
        "w_out": nrm(ks[10], (DEPTH, MIX_WIDTH, D_MODEL), MIX_WIDTH ** -0.5 * DEEPNORM_BETA),
        "ln1_g": 1.0 + nrm(ks[11], (DEPTH, D_MODEL), 0.02),
        "ln1_b": nrm(ks[12], (DEPTH, D_MODEL), 0.02),
        "peer_w_query": nrm(ks[13], (DEPTH, D_MODEL, PEER_HEADS * PEER_KEY_DIM), D_MODEL ** -0.5),
        "peer_sub_keys": nrm(ks[14], (DEPTH, PEER_HEADS, 2, PEER_N_KEYS, PEER_KEY_DIM // 2), (PEER_KEY_DIM // 2) ** -0.5),
        "peer_u": nrm(ks[15], (DEPTH, PEER_N_EXPERTS, D_MODEL), D_MODEL ** -0.5),
        "peer_v": nrm(ks[16], (DEPTH, PEER_N_EXPERTS, D_MODEL), DEEPNORM_BETA),
        "ln2_g": 1.0 + nrm(ks[17], (DEPTH, D_MODEL), 0.02),
        "ln2_b": nrm(ks[18], (DEPTH, D_MODEL), 0.02),
    }

def reference(x, ln_emb_g, ln_emb_b, w_in, dil_norm_g, lambda_q1, lambda_k1, lambda_q2, lambda_k2,
              subln_g, w_out, ln1_g, ln1_b, peer_w_query, peer_sub_keys, peer_u, peer_v, ln2_g, ln2_b):
    S = x.shape[1]
    rope_dil = rope_tables(S, HEAD_DIM // ROPE_FRACTION)
    rope_diff = rope_tables(S, DIFF_QK_DIM // ROPE_FRACTION)
    h = layer_norm(x, ln_emb_g, ln_emb_b)
    for l in range(DEPTH):
        lam_init = 0.8 - 0.6 * math.exp(-0.3 * l)
        mix = hybrid_mixer(h, w_in[l], dil_norm_g[l], lambda_q1[l], lambda_k1[l], lambda_q2[l], lambda_k2[l],
                           subln_g[l], w_out[l], lam_init, rope_dil, rope_diff)
        h = layer_norm(DEEPNORM_ALPHA * h + mix, ln1_g[l], ln1_b[l])
        ffn = peer_ffn(h, peer_w_query[l], peer_sub_keys[l], peer_u[l], peer_v[l])
        h = layer_norm(DEEPNORM_ALPHA * h + ffn, ln2_g[l], ln2_b[l])
    return h


_drawn_inputs = setup_inputs


def setup_inputs(seed=0):
    import zlib

    import numpy as np

    out = dict(_drawn_inputs(seed))
    spreads = {}
    factors = {'lambda_q1': 8.0, 'subln_g': 3.18, 'ln2_g': 2.822, 'ln2_b': 2.841}
    for name, (base, spread) in spreads.items():
        noise = np.random.default_rng([zlib.crc32(name.encode()), seed]).standard_normal(out[name].shape)
        drawn = base * np.exp(spread * noise) if base else spread * noise
        out[name] = __import__('jax').numpy.asarray(drawn.astype(out[name].dtype))
    for name, factor in factors.items():
        out[name] = (out[name] * factor).astype(out[name].dtype)
    return out
```

```python
import math
from contextlib import ExitStack

import numpy as np

import concourse.bass as bass
from concourse import mybir
from concourse.alu_op_type import AluOpType as ALU

F32 = mybir.dt.float32
F32R = mybir.dt.float32r
U32 = mybir.dt.uint32
ACT = mybir.ActivationFunctionType
AX_X = mybir.AxisListType.X
ds = bass.ds

P = 128
D = 2048
S = 256
T = S // P
KT = D // P
DH = 128
DIL_HEADS = 12
DIFF_HEADS = 4
DIFF_DQ = 64
IN_WIDTH = 3 * DIL_HEADS * DH + 3 * DIFF_HEADS * 2 * DIFF_DQ
COL_QD = 3 * DIL_HEADS * DH
COL_KD = COL_QD + DIFF_HEADS * DH
COL_VD = COL_KD + DIFF_HEADS * DH
ROPE_THETA = 500000.0
HALF_DIL = DH // 4 // 2
HALF_DIFF = DIFF_DQ // 4 // 2
DIL_CONFIGS = ((128, 1), (512, 4), (2048, 16))
PEER_HEADS = 8
N_KEYS = 128
TOPK = 16
LN_EPS = 1e-5
ALPHA = 2.0 ** 0.25
LAM_INIT = 0.8 - 0.6 * math.exp(-0.0)
LOWEST = -3.0e38
GROUP = 512
CHUNK_KT = 4
CHUNKS = KT // CHUNK_KT

C_ID = 0
C_IOTA = C_ID + P
C_IOTA16 = C_IOTA + P
C_MASK = C_IOTA16 + TOPK
C_ROPE = C_MASK + T * S
ROPE_W = 2 * HALF_DIL + 2 * HALF_DIFF
C_END = C_ROPE + T * ROPE_W


def shape_constants():
    c = np.zeros((P, C_END), np.float32)
    c[:, C_ID:C_ID + P] = np.eye(P, dtype=np.float32)
    c[:, C_IOTA:C_IOTA + P] = np.arange(P, dtype=np.float32)
    c[:, C_IOTA16:C_IOTA16 + TOPK] = np.arange(TOPK, dtype=np.float32)
    q, k = np.arange(S)[:, None], np.arange(S)[None, :]
    count = np.zeros((S, S), np.int64)
    for window, dilation in DIL_CONFIGS:
        near = np.abs(q // dilation - k // dilation) <= window // (2 * dilation)
        count += near & (q % dilation == k % dilation)
    log_count = np.where(count > 0, np.log(np.maximum(count, 1)) * DH ** 0.5, -1e30)
    c[:, C_MASK:C_MASK + T * S] = log_count.reshape(T, P, S).transpose(1, 0, 2).reshape(P, T * S)
    rope = []
    for half in (HALF_DIL, HALF_DIFF):
        exponent = np.arange(0, 2 * half, 2, dtype=np.float32) / np.float32(2 * half)
        inv = np.float32(1.0) / np.power(np.float32(ROPE_THETA), exponent)
        angle = np.arange(S, dtype=np.float32)[:, None] * inv[None, :]
        rope += [np.cos(angle), np.sin(angle)]
    rope = np.concatenate(rope, axis=1).astype(np.float32)
    c[:, C_ROPE:] = rope.reshape(T, P, ROPE_W).transpose(1, 0, 2).reshape(P, T * ROPE_W)
    return c


class Chain:

    def __init__(self, sem):
        self.sem, self.n = sem, 0

    def step(self, ins):
        ins.then_inc(self.sem, 1)
        self.n += 1
        return self.n


def encoder_layer(nc, x, ln_emb_g, ln_emb_b, w_in, dil_norm_g, lambda_q1, lambda_k1, lambda_q2, lambda_k2,
                  subln_g, w_out, ln1_g, ln1_b, w_query, sub_keys, peer_u, peer_v, ln2_g, ln2_b,
                  constants, h1_spill, out, blocks=99):
    x_v = x.rearrange("o (t p) d -> p (o t) d", p=P)
    out_v = out.rearrange("o (t p) d -> p (o t) d", p=P)
    spill_v = h1_spill.rearrange("(t p) d -> p t d", p=P)

    BASE = 16512
    at = [BASE]

    def small(name, shape, dt=F32):
        size = 4 * int(np.prod(shape[1:]))
        size += -size % 32
        t = nc.alloc_sbuf_tensor_at(name, shape, dt, offset=at[0])
        at[0] += size
        return t

    def place(name, shape, dt, offset):
        return nc.alloc_sbuf_tensor_at(name, shape, dt, offset=offset)

    cst = small("cst", [P, C_END])
    pickT = small("pickT", [P, 3, S])
    lamv = small("lamv", [P, 4, DIFF_DQ])
    lams = small("lams", [P, 8])
    g_col = small("g_col", [P, 4])
    stats = small("stats", [P, T, 4, 6])
    meanvar = small("meanvar", [P, T, 2])
    rstd = small("rstd", [P, T, 2])
    mhalf = small("mhalf", [P, 32])
    row_max = small("row_max", [P, 16, 4])
    neg_max = small("neg_max", [P, 16, 4])
    den = small("den", [P, 16, 4])
    rden = small("rden", [P, 16, 4])
    lam_rden = small("lam_rden", [P, 4, 2])
    sumsq = small("sumsq", [P, T, 16])
    rms = small("rms", [P, T, 16])
    SMALL_END = BASE + 11 * 1024
    assert at[0] <= SMALL_END, at[0] - BASE
    ident = cst[:, C_ID:C_ID + P]
    KB = 1024
    HT0 = SMALL_END
    R0 = HT0 + 32 * KB
    hT = place("hT", [P, KT, 2 * S], F32R, HT0)
    h = place("h", [P, T, D], F32, R0)
    w_raw = place("w_raw", [P, 4, CHUNK_KT, GROUP], F32, R0 + 16 * KB)
    w_hi = place("w_hi", [P, 2, CHUNK_KT, GROUP], F32R, R0 + 48 * KB)
    w_lo = place("w_lo", [P, 2, CHUNK_KT, GROUP], F32R, R0 + 64 * KB)
    ln_gb = place("ln_gb", [P, 2, D], F32, R0 + 80 * KB)
    proj = place("proj", [P, T, IN_WIDTH], F32, R0 + 96 * KB)
    qkT = place("qkT", [P, 32, S], F32, R0 + 48 * KB)
    mixed = place("mixed", [P, T, D], F32, HT0)
    scores = place("scores", [P, 2, T, S], F32, HT0 + 16 * KB)
    probs = place("probs", [P, 2, 2, T, S], F32, HT0 + 20 * KB)
    probsT = place("probsT", [P, 2, T, S], F32, HT0 + 28 * KB)
    rope_tmp = place("rope_tmp", [P, 4, 2 * DIL_HEADS * HALF_DIL], F32, R0 + 144 * KB)
    square = place("square", [P, P], F32, R0 + 150 * KB)
    mixT = place("mixT", [P, KT, 2 * S], F32R, R0 + 96 * KB)
    query = place("query", [P, T, D], F32, R0 + 96 * KB)
    queryT = place("queryT", [P, KT, S], F32, R0 + 112 * KB)
    keys = place("keys", [P, 2 * PEER_HEADS, P], F32, R0 + 80 * KB)
    keysT = place("keysT", [P, 2 * PEER_HEADS, N_KEYS], F32, R0 + 88 * KB)
    key_scores = place("key_scores", [P, T, 2 * PEER_HEADS, N_KEYS], F32, R0)
    TK = R0 + 48 * KB
    top_v = place("top_v", [P, T, 2 * PEER_HEADS, TOPK], F32, TK)
    top_i = place("top_i", [P, T, 2 * PEER_HEADS, TOPK], U32, TK + 2 * KB)
    top_if = place("top_if", [P, T, 2 * PEER_HEADS, TOPK], F32, TK + 4 * KB)
    cand = place("cand", [P, PEER_HEADS, TOPK, TOPK], F32, TK + 6 * KB)
    pick_eq = place("pick_eq", [P, PEER_HEADS, TOPK, TOPK], F32, TK + 14 * KB)
    pick_v = place("pick_v", [P, T, PEER_HEADS, TOPK], F32, TK + 22 * KB)
    pick_pos = place("pick_pos", [P, T, PEER_HEADS, TOPK], U32, TK + 23 * KB)
    pick_ij = place("pick_ij", [P, 2, PEER_HEADS, TOPK], U32, TK + 24 * KB)
    pick_ijf = place("pick_ijf", [P, 2, PEER_HEADS, TOPK], F32, TK + 25 * KB)
    pick = place("pick", [P, T, 3, PEER_HEADS * TOPK], F32, TK + 26 * KB)
    gate_e = place("gate_e", [P, T, PEER_HEADS, TOPK], F32, TK + 29 * KB)
    gate_s = place("gate_s", [P, T, 2, PEER_HEADS], F32, TK + 30 * KB)
    gates = place("gates", [P, N_KEYS, S], F32, R0)
    onehot = place("onehot", [P, 2, 4, 2, P], F32, R0 + 144 * KB)
    e_raw = place("e_raw", [P, 2, D], F32, R0 + 128 * KB)
    uT_hi = place("uT_hi", [P, 4, 4, P], F32R, R0 + 144 * KB)
    uT_lo = place("uT_lo", [P, 4, 4, P], F32R, R0 + 152 * KB)
    act_tmp = place("act_tmp", [P, 2, S], F32, R0 + 160 * KB)
    v_hi = place("v_hi", [P, 2, D], F32R, HT0)
    v_lo = place("v_lo", [P, 2, D], F32R, HT0 + 16 * KB)
    h1 = place("h1", [P, T, D], F32, R0 + 144 * KB)
    a_hi = place("a_hi", [P, 2, S], F32R, R0 + 160 * KB)
    a_lo = place("a_lo", [P, 2, S], F32R, R0 + 162 * KB)
    final = place("final", [P, T, D], F32, R0)
    ln2_gb = place("ln2_gb", [P, 2, D], F32, R0 + 16 * KB)

    sem = nc.alloc_semaphore

    def banks(name, shape):
        return nc.psum_tensor(name, shape, F32)

    def wait_used(eng, s, n):
        if not (isinstance(n, int) and n == 0):
            eng.wait_ge(s, n)

    def broadcast_rows(v):
        return v.rearrange("o d -> (o d)").partition_broadcast(P)

    def f(ap):
        return ap.bitcast(F32)

    def norm_stats(dve, chain, src, ready):
        for t in range(T):
            for c in range(4):
                n = chain.step(nc.vector.bn_stats(stats[:, t, c, :], src[:, t, c * 512:(c + 1) * 512]))
        dve.wait_ge(chain.sem, n)
        for t in range(T):
            n = chain.step(nc.vector.bn_aggr(meanvar[:, t, :], stats[:, t, :, :]))
        dve.wait_ge(chain.sem, n)
        nc.vector.tensor_scalar(rstd[:, :, 0], meanvar[:, :, 1], LN_EPS, None, ALU.add).then_inc(ready, 1)

    def inverse_root(pool, ready, done):
        pool.wait_ge(ready, 1)
        nc.gpsimd.tensor_tensor(rstd[:, :, 1], rstd[:, :, 0], mhalf[:, 0:T], ALU.pow).then_inc(done, 1)

    def norm_apply(dve, chain, buf, gb, done, norm_done):
        dve.wait_ge(done, 1)
        for t in range(T):
            n = chain.step(nc.vector.tensor_scalar(buf[:, t, :], buf[:, t, :], meanvar[:, t, 0:1],
                                                   rstd[:, t, 1:2], ALU.subtract, ALU.mult))
            dve.wait_ge(chain.sem, n)
            n = chain.step(nc.vector.tensor_tensor(buf[:, t, :], buf[:, t, :], gb[:, 0, :], ALU.mult))
            dve.wait_ge(chain.sem, n)
            nc.vector.tensor_tensor(buf[:, t, :], buf[:, t, :], gb[:, 1, :], ALU.add).then_inc(norm_done, 1)

    def turn_pe(pe, tp, src, sem_turned, sem_lo, wait_src):
        for j in range(KT // 2):
            if j >= 2:
                pe.wait_ge(sem_lo, j - 1)
            for t in range(T):
                if j == 0:
                    wait_src(t)
                for k in range(2):
                    kt = 2 * j + k
                    last = nc.tensor.transpose(tp[:, j % 2, k * S + t * P:k * S + (t + 1) * P],
                                               src[:, t, kt * P:(kt + 1) * P], ident)
            last.then_inc(sem_turned, 1)

    def turn_act(act, tp, dst, sem_turned, sem_hi, gain):
        for j in range(KT // 2):
            act.wait_ge(sem_turned, j + 1)
            o = dst[:, 2 * j:2 * j + 2, 0:S]
            i = tp[:, j % 2, :].rearrange("p (k s) -> p k s", k=2)
            g = gain(2 * j)
            if g is None:
                nc.scalar.copy(o, i).then_inc(sem_hi, 1)
            else:
                nc.scalar.activation(o, i, ACT.Copy, scale=g).then_inc(sem_hi, 1)

    def turn_dve(dve, tp, dst, sem_hi, sem_lo, gain):
        for j in range(KT // 2):
            dve.wait_ge(sem_hi, j + 1)
            o = dst[:, 2 * j:2 * j + 2, S:2 * S]
            hi = f(dst[:, 2 * j:2 * j + 2, 0:S])
            i = tp[:, j % 2, :].rearrange("p (k s) -> p k s", k=2)
            g = gain(2 * j)
            if g is None:
                nc.vector.tensor_tensor(o, i, hi, ALU.subtract).then_inc(sem_lo, 1)
            else:
                nc.vector.scalar_tensor_tensor(o, i, g, hi, ALU.mult, ALU.subtract).then_inc(sem_lo, 1)

    class Stream:
        def __init__(self, name, w, groups, acc):
            self.w = w.rearrange("(c k p) (g n) -> p c k g n", k=CHUNK_KT, p=P, n=GROUP)
            self.steps, self.acc = groups // 2, acc
            self.loaded = [sem(f"{name}_loaded{c}") for c in range(CHUNKS)]
            self.hi = [sem(f"{name}_hi{s}") for s in range(2)]
            self.lo = [sem(f"{name}_lo{s}") for s in range(2)]
            self.used = [sem(f"{name}_used{s}") for s in range(2)]
            self.read_out = [sem(f"{name}_read_out{u}") for u in range(2)]

        def load(self, sp, g, c):
            sp.dma_start(w_raw[:, c, :, :].unsqueeze(2), self.w[:, c, :, ds(g, 1), :]).then_inc(self.loaded[c], 16)

        def prefetch(self, sp):
            for c in range(CHUNKS):
                self.load(sp, 0, c)

        def steps_of(self, eng, body):
            body(0, True, self.steps == 1)
            if self.steps > 2:
                with eng.Fori(1, self.steps - 1) as i:
                    body(i, False, False)
            if self.steps > 1:
                body(self.steps - 1, False, True)

        def sp(self, sp):
            def body(i, first, last):
                for u in range(1 if last else 2):
                    for c in range(CHUNKS):
                        sp.wait_ge(self.lo[c % 2], i * 4 + (2 * u + c // 2 + 1))
                        self.load(sp, i * 2 + (u + 1), c)
            self.steps_of(sp, body)

        def split_act(self, act, after_chunk):
            def body(i, first, last):
                for u in range(2):
                    for c in range(CHUNKS):
                        s = c % 2
                        act.wait_ge(self.loaded[c], i * 32 + 16 * (u + 1))
                        if not (first and u == 0 and c < 2):
                            act.wait_ge(self.used[s], i * 4 + (2 * u + c // 2))
                        nc.scalar.copy(w_hi[:, s, :, :], w_raw[:, c, :, :]).then_inc(self.hi[s], 1)
                        after_chunk(i, first, last, u, c)
            self.steps_of(act, body)

        def split_dve(self, dve, after_chunk):
            def body(i, first, last):
                for u in range(2):
                    for c in range(CHUNKS):
                        s = c % 2
                        dve.wait_ge(self.hi[s], i * 4 + (2 * u + c // 2 + 1))
                        nc.vector.tensor_tensor(w_lo[:, s, :, :], w_raw[:, c, :, :], f(w_hi[:, s, :, :]),
                                                ALU.subtract).then_inc(self.lo[s], 1)
                        after_chunk(i, first, last, u, c)
            self.steps_of(dve, body)

        def read_after(self, eng, read):
            def after_chunk(i, first, last, u, c):
                if c == 1 and not (first and u == 0):
                    ip, up = (i, 0) if u == 1 else (i - 1, 1)
                    eng.wait_ge(self.used[1], i * 4 + 2 * u)
                    read(ip * 2 + up, self.acc[:, up, :, :]).then_inc(self.read_out[up], 1)
                if last and u == 1 and c == CHUNKS - 1:
                    eng.wait_ge(self.used[1], i * 4 + 4)
                    read(i * 2 + 1, self.acc[:, 1, :, :]).then_inc(self.read_out[1], 1)
            return after_chunk

        def pe(self, pe, actT):
            def body(i, first, last):
                for u in range(2):
                    for c in range(CHUNKS):
                        s = c % 2
                        pe.wait_ge(self.lo[s], i * 4 + (2 * u + c // 2 + 1))
                        if c == 0 and not first:
                            pe.wait_ge(self.read_out[u], i)
                        for k in range(CHUNK_KT):
                            kt = c * CHUNK_KT + k
                            for t in range(T):
                                hi, lo = (actT[:, kt, b + t * P:b + (t + 1) * P] for b in (0, S))
                                o = self.acc[:, u, t, :]
                                nc.tensor.matmul(o, hi, w_hi[:, s, k, :], start=(kt == 0), stop=False)
                                nc.tensor.matmul(o, hi, w_lo[:, s, k, :], start=False, stop=False)
                                mm = nc.tensor.matmul(o, lo, w_hi[:, s, k, :], start=False, stop=(kt == KT - 1))
                        mm.then_inc(self.used[s], 1)
            self.steps_of(pe, body)

    stream_acc = nc.alloc_psum_tensor("stream_acc", [P, 2, T, GROUP], F32)
    turn_ps = nc.alloc_psum_tensor("turn_ps", [P, 2, 512], F32)
    spare_ps = nc.alloc_psum_tensor("spare_ps", [P, 2, 512], F32)
    in_stream = Stream("w_in", w_in, IN_WIDTH // GROUP, stream_acc)
    out_stream = Stream("w_out", w_out, D // GROUP, stream_acc)
    query_stream = Stream("w_query", w_query, D // GROUP, stream_acc)

    s_const, s_x, s_lng, s_lamv, s_gcol = (sem(n) for n in ("const_in", "x_in", "ln_emb_in", "lambda_in", "gain_in"))
    s_pool = sem("minus_half")
    s_c1, s_var1, s_root1, s_n1 = sem("embed_chain"), sem("embed_var"), sem("embed_root"), sem("embed_normed")
    s_t1, s_h1, s_l1 = sem("embed_turned"), sem("embed_hi"), sem("embed_lo")
    s_lam, s_lame = sem("lambda_sums"), sem("lambda_exps")
    with nc.Block() as block:
        @block.sync
        def _(sp):
            sp.dma_start(h[:], x_v).then_inc(s_x, 16)
            sp.dma_start(cst[:], constants).then_inc(s_const, 16)
            for j, v in enumerate((ln_emb_g, ln_emb_b)):
                sp.dma_start(ln_gb[:, j, :], v.partition_broadcast(P)).then_inc(s_lng, 16)
            in_stream.prefetch(sp)
            for j, v in enumerate((lambda_q1, lambda_k1, lambda_q2, lambda_k2)):
                sp.dma_start(lamv[:, j, :], broadcast_rows(v)).then_inc(s_lamv, 16)
            for j, v in enumerate((dil_norm_g, subln_g)):
                sp.dma_start(g_col[:, j:j + 1], v.rearrange("o d -> d o")).then_inc(s_gcol, 16)

        @block.gpsimd
        def _(pool):
            nc.gpsimd.memset(mhalf[:], -0.5).then_inc(s_pool, 1)
            pool.wait_ge(s_pool, 1)
            inverse_root(pool, s_var1, s_root1)

        @block.vector
        def _(dve):
            chain = Chain(s_c1)
            dve.wait_ge(s_x, 16)
            norm_stats(dve, chain, h, s_var1)
            dve.wait_ge(s_lamv, 64)
            for m in range(2):
                n = chain.step(nc.vector.tensor_tensor(lamv[:, 2 * m, :], lamv[:, 2 * m, :],
                                                       lamv[:, 2 * m + 1, :], ALU.mult))
                dve.wait_ge(chain.sem, n)
                nc.vector.tensor_reduce(lams[:, m:m + 1], lamv[:, 2 * m, :], AX_X, ALU.add).then_inc(s_lam, 1)
            dve.wait_ge(s_gcol, 32)
            n = chain.step(nc.vector.tensor_scalar(g_col[:, 1:2], g_col[:, 1:2], 1.0 - LAM_INIT, None, ALU.mult))
            dve.wait_ge(s_lame, 1)
            n = chain.step(nc.vector.tensor_tensor(lams[:, 4:5], lams[:, 3:4], lams[:, 2:3], ALU.subtract))
            dve.wait_ge(chain.sem, n)
            n = chain.step(nc.vector.tensor_scalar(lams[:, 5:6], lams[:, 4:5], LAM_INIT, None, ALU.subtract))
            dve.wait_ge(s_lng, 32)
            norm_apply(dve, chain, h, ln_gb, s_root1, s_n1)
            turn_dve(dve, turn_ps, hT, s_h1, s_l1, lambda kt: None)

        @block.scalar
        def _(act):
            act.wait_ge(s_lam, 2)
            nc.scalar.activation(lams[:, 2:4], lams[:, 0:2], ACT.Exp).then_inc(s_lame, 1)
            turn_act(act, turn_ps, hT, s_t1, s_h1, lambda kt: None)

        @block.tensor
        def _(pe):
            pe.wait_ge(s_const, 16)
            turn_pe(pe, turn_ps, h, s_t1, s_l1, lambda t: pe.wait_ge(s_n1, t + 1))
    if blocks < 2:
        return

    with nc.Block() as block:
        @block.sync
        def _(sp):
            in_stream.sp(sp)

        @block.scalar
        def _(act):
            in_stream.split_act(act, in_stream.read_after(act, lambda g, acc: nc.scalar.copy(
                proj[:, :, ds(g * GROUP, GROUP)], acc)))

        @block.vector
        def _(dve):
            in_stream.split_dve(dve, lambda *a: None)

        @block.tensor
        def _(pe):
            in_stream.pe(pe, hT)
    if blocks < 3:
        return

    def block_col(b):
        return b * P if b < 24 else COL_QD + (b - 24) * P

    HEADS = DIL_HEADS + DIFF_HEADS
    turn_seq = [b for hd in range(DIL_HEADS) for b in (hd, 12 + hd)] + [b for hd in range(4) for b in (24 + hd, 28 + hd)]
    s_c3, s_rope = sem("rope_chain"), sem("rope_done")
    s_qt, s_qe, = sem("qk_turned"), sem("qk_copied")
    s_s, s_mx, s_e, s_nrm, s_pt, s_pte, s_o, s_oe, s_sq = (sem("att_" + n) for n in (
        "scores", "max", "exp", "normed", "turned", "turned_copied", "out", "out_copied", "squares"))
    s_eps, s_root3, s_rms = sem("rms_eps"), sem("rms_root"), sem("rms_done")
    sc_ps = stream_acc

    def is_diff(u):
        return u >= DIL_HEADS

    def v_col(u):
        return 2 * DIL_HEADS * DH + u * DH if not is_diff(u) else COL_VD + (u - DIL_HEADS) * DH

    with nc.Block() as block:
        @block.sync
        def _(sp):
            out_stream.prefetch(sp)

        @block.vector
        def _(dve):
            chain = Chain(s_c3)

            def rope(t, col, heads, width, half, tab):
                v = proj[:, t, col:col + heads * width].rearrange("p (a w) -> p a w", w=width)
                x1, x2 = v[:, :, 0:half], v[:, :, half:2 * half]
                base = C_ROPE + t * ROPE_W + tab
                cos = cst[:, base:base + half].unsqueeze(1).broadcast_to([P, heads, half])
                sin = cst[:, base + half:base + 2 * half].unsqueeze(1).broadcast_to([P, heads, half])
                tmp = [rope_tmp[:, j, 0:heads * half].rearrange("p (a w) -> p a w", w=half) for j in range(4)]
                for o, a, b in ((tmp[0], x1, cos), (tmp[1], x2, sin), (tmp[2], x1, sin), (tmp[3], x2, cos)):
                    n = chain.step(nc.vector.tensor_tensor(o, a, b, ALU.mult))
                dve.wait_ge(chain.sem, n)
                chain.step(nc.vector.tensor_tensor(x1, tmp[0], tmp[1], ALU.subtract))
                n = chain.step(nc.vector.tensor_tensor(x2, tmp[2], tmp[3], ALU.add))
                dve.wait_ge(chain.sem, n)
                return n
            for t in range(T):
                rope(t, 0, 2 * DIL_HEADS, DH, HALF_DIL, 0)
                rope(t, COL_QD, 4 * DIFF_HEADS, DIFF_DQ, HALF_DIFF, 2 * HALF_DIL)
            nc.vector.memset(lams[:, 6:7], 0.0).then_inc(s_rope, 1)

            def row_maxima(u):
                s = u % 2
                dve.wait_ge(s_s, u + 1)
                if not is_diff(u):
                    if u >= 2:
                        dve.wait_ge(s_e, u - 1)
                    for t in range(T):
                        n = chain.step(nc.vector.tensor_tensor_reduce(
                            scores[:, s, t, :], sc_ps[:, s, 0, t * S:(t + 1) * S],
                            cst[:, C_MASK + t * S:C_MASK + (t + 1) * S], DH ** -0.5, LOWEST, ALU.add, ALU.max,
                            row_max[:, u, t:t + 1]))
                    w, scale = 2, -1.0
                else:
                    n = chain.step(nc.vector.tensor_reduce(
                        row_max[:, u, :], sc_ps[:, s, :, :].rearrange("p m (t k) -> p (m t) k", t=T), AX_X, ALU.max))
                    w, scale = 4, -DIFF_DQ ** -0.5
                dve.wait_ge(chain.sem, n)
                nc.vector.tensor_scalar(neg_max[:, u, 0:w], row_max[:, u, 0:w], scale, None, ALU.mult).then_inc(s_mx, 1)

            def normalise(u):
                s = u % 2
                dve.wait_ge(s_e, u + 1)
                if not is_diff(u):
                    nc.vector.reciprocal(rden[:, u, 0:2], den[:, u, 0:2]).then_inc(s_nrm, 1)
                    return
                j = u - DIL_HEADS
                n = chain.step(nc.vector.reciprocal(rden[:, u, :], den[:, u, :]))
                dve.wait_ge(chain.sem, n)
                n = chain.step(nc.vector.tensor_scalar(lam_rden[:, j, :], rden[:, u, 2:4], lams[:, 5:6], None, ALU.mult))
                for t in range(T):
                    n = chain.step(nc.vector.tensor_scalar(probs[:, s, 0, t, :], probs[:, s, 0, t, :],
                                                           rden[:, u, t:t + 1], None, ALU.mult))
                dve.wait_ge(chain.sem, n)
                for t in range(T):
                    ins = nc.vector.scalar_tensor_tensor(probs[:, s, 0, t, :], probs[:, s, 1, t, :],
                                                         lam_rden[:, j, t:t + 1], probs[:, s, 0, t, :],
                                                         ALU.mult, ALU.add)
                ins.then_inc(s_nrm, 1)

            def outputs(u):
                dve.wait_ge(s_o, u + 1)
                o = mixed[:, :, u * DH:(u + 1) * DH]
                i = spare_ps[:, u % 2, 0:T * DH].rearrange("p (t d) -> p t d", t=T)
                if is_diff(u):
                    nc.vector.tensor_copy(o, i).then_inc(s_oe, 1)
                else:
                    nc.vector.tensor_tensor(o, i, rden[:, u, 0:2].unsqueeze(2).broadcast_to([P, T, DH]),
                                            ALU.mult).then_inc(s_oe, 1)

            for n in range(HEADS + 3):
                if n < HEADS:
                    row_maxima(n)
                if 1 <= n <= HEADS:
                    normalise(n - 1)
                if n >= 3:
                    outputs(n - 3)
            dve.wait_ge(s_sq, HEADS * T)
            nc.vector.tensor_scalar(sumsq[:], sumsq[:], 1.0 / DH, LN_EPS, ALU.mult, ALU.add).then_inc(s_eps, 1)
            dve.wait_ge(s_root3, 1)
            for t in range(T):
                v = mixed[:, t, :].rearrange("p (u d) -> p u d", d=DH)
                nc.vector.tensor_tensor(v, v, rms[:, t, :].unsqueeze(2).broadcast_to([P, HEADS, DH]),
                                        ALU.mult).then_inc(s_rms, 1)

        @block.gpsimd
        def _(pool):
            pool.wait_ge(s_eps, 1)
            nc.gpsimd.tensor_tensor(rms[:].rearrange("p t u -> p (t u)"), sumsq[:].rearrange("p t u -> p (t u)"),
                                    mhalf[:], ALU.pow).then_inc(s_root3, 1)

        @block.scalar
        def _(act):
            for j in range(16):
                act.wait_ge(s_qt, j + 1)
                for k in range(2):
                    ins = nc.scalar.copy(qkT[:, turn_seq[2 * j + k], :], turn_ps[:, j % 2, k * S:(k + 1) * S])
                ins.then_inc(s_qe, 1)

            def exponentials(u):
                s = u % 2
                act.wait_ge(s_mx, u + 1)
                if u >= 2:
                    act.wait_ge(s_pt, u - 1)
                maps = 2 if is_diff(u) else 1
                for m in range(maps):
                    for t in range(T):
                        src = sc_ps[:, s, m, t * S:(t + 1) * S] if is_diff(u) else scores[:, s, t, :]
                        j = m * T + t
                        ins = nc.scalar.activation(probs[:, s, m, t, :], src, ACT.Exp, bias=neg_max[:, u, j:j + 1],
                                                   scale=DIFF_DQ ** -0.5 if is_diff(u) else 1.0,
                                                   accum_out=den[:, u, j:j + 1])
                ins.then_inc(s_e, 1)

            def copy_turned(u):
                act.wait_ge(s_pt, u + 1)
                if u >= 2:
                    act.wait_ge(s_o, u - 1)
                nc.scalar.copy(probsT[:, u % 2, :, :], turn_ps[:, u % 2, :].rearrange("p (k q) -> p k q", k=T)
                               ).then_inc(s_pte, 1)

            def squares(u):
                act.wait_ge(s_oe, u + 1)
                for t in range(T):
                    if u + t > 0:
                        act.wait_ge(s_sq, u * T + t)
                    nc.scalar.activation(square[:], mixed[:, t, u * DH:(u + 1) * DH], ACT.Square,
                                         accum_out=sumsq[:, t, u:u + 1]).then_inc(s_sq, 1)

            for n in range(HEADS + 4):
                if n < HEADS:
                    exponentials(n)
                if 1 <= n <= HEADS:
                    copy_turned(n - 1)
                if n >= 4:
                    squares(n - 4)

        @block.tensor
        def _(pe):
            pe.wait_ge(s_rope, 1)
            for j in range(16):
                if j >= 2:
                    pe.wait_ge(s_qe, j - 1)
                for k in range(2):
                    c = block_col(turn_seq[2 * j + k])
                    for t in range(T):
                        ins = nc.tensor.transpose(turn_ps[:, j % 2, k * S + t * P:k * S + (t + 1) * P],
                                                  proj[:, t, c:c + P], ident)
                ins.then_inc(s_qt, 1)

            def score(u):
                s = u % 2
                if u >= 2:
                    pe.wait_ge(s_mx, u - 1)
                    if is_diff(u - 2):
                        pe.wait_ge(s_e, u - 1)
                if not is_diff(u):
                    for t in range(T):
                        ins = nc.tensor.matmul(sc_ps[:, s, 0, t * S:(t + 1) * S], qkT[:, u, t * P:(t + 1) * P],
                                               qkT[:, 12 + u, :], start=True, stop=True)
                else:
                    j = u - DIL_HEADS
                    for m in range(2):
                        r = slice(m * DIFF_DQ, (m + 1) * DIFF_DQ)
                        for t in range(T):
                            ins = nc.tensor.matmul(sc_ps[:, s, m, t * S:(t + 1) * S],
                                                   qkT[r, 24 + j, t * P:(t + 1) * P], qkT[r, 28 + j, :],
                                                   start=True, stop=True)
                ins.then_inc(s_s, 1)

            def turn(u):
                s = u % 2
                pe.wait_ge(s_nrm, u + 1)
                if u >= 2:
                    pe.wait_ge(s_pte, u - 1)
                for k in range(T):
                    for t in range(T):
                        ins = nc.tensor.transpose(turn_ps[:, s, k * S + t * P:k * S + (t + 1) * P],
                                                  probs[:, s, 0, t, k * P:(k + 1) * P], ident)
                ins.then_inc(s_pt, 1)

            def weigh(u):
                s = u % 2
                pe.wait_ge(s_pte, u + 1)
                if u >= 2:
                    pe.wait_ge(s_oe, u - 1)
                c = v_col(u)
                for t in range(T):
                    for k in range(T):
                        ins = nc.tensor.matmul(spare_ps[:, s, t * DH:(t + 1) * DH],
                                               probsT[:, s, k, t * P:(t + 1) * P], proj[:, k, c:c + DH],
                                               start=(k == 0), stop=(k == T - 1))
                ins.then_inc(s_o, 1)

            pe.wait_ge(s_qe, 16)
            for n in range(HEADS + 2):
                if n < HEADS:
                    score(n)
                if 1 <= n <= HEADS:
                    turn(n - 1)
                if n >= 2:
                    weigh(n - 2)
    if blocks < 4:
        return

    s_lng4, s_c4, s_var4, s_root4, s_n4 = (sem("ln1_" + n) for n in ("gb_in", "chain", "var", "root", "normed"))
    s_mt, s_mh, s_ml = sem("mix_turned"), sem("mix_hi"), sem("mix_lo")
    s_t4, s_h4, s_l4 = sem("h1_turned"), sem("h1_hi"), sem("h1_lo")
    s_spill, s_keys = sem("h1_spilled"), sem("keys_in")

    def mix_gain(kt):
        return g_col[:, 0:1] if kt < DIL_HEADS else g_col[:, 1:2]

    with nc.Block() as block:
        @block.sync
        def _(sp):
            for j, v in enumerate((ln1_g, ln1_b)):
                sp.dma_start(ln_gb[:, j, :], broadcast_rows(v)).then_inc(s_lng4, 16)
            out_stream.sp(sp)
            sp.wait_ge(out_stream.lo[0], 8)
            sp.wait_ge(out_stream.lo[1], 8)
            query_stream.prefetch(sp)
            sp.wait_ge(s_n4, 2)
            sp.dma_start(spill_v, h[:]).then_inc(s_spill, 16)

        @block.gpsimd
        def _(pool):
            inverse_root(pool, s_var4, s_root4)

        @block.scalar
        def _(act):
            turn_act(act, turn_ps, mixT, s_mt, s_mh, mix_gain)
            out_stream.split_act(act, lambda *a: None)
            turn_act(act, turn_ps, hT, s_t4, s_h4, lambda kt: None)

        @block.vector
        def _(dve):
            chain = Chain(s_c4)
            turn_dve(dve, turn_ps, mixT, s_mh, s_ml, mix_gain)
            out_stream.split_dve(dve, out_stream.read_after(dve, lambda g, acc: nc.vector.scalar_tensor_tensor(
                h[:, :, ds(g * GROUP, GROUP)], h[:, :, ds(g * GROUP, GROUP)], ALPHA, acc, ALU.mult, ALU.add)))
            dve.wait_ge(out_stream.read_out[0], 2)
            dve.wait_ge(out_stream.read_out[1], 2)
            norm_stats(dve, chain, h, s_var4)
            dve.wait_ge(s_lng4, 32)
            norm_apply(dve, chain, h, ln_gb, s_root4, s_n4)
            turn_dve(dve, turn_ps, hT, s_h4, s_l4, lambda kt: None)

        @block.tensor
        def _(pe):
            turn_pe(pe, turn_ps, mixed, s_mt, s_ml, lambda t: None)
            pe.wait_ge(s_ml, 8)
            out_stream.pe(pe, mixT)
            turn_pe(pe, turn_ps, h, s_t4, s_l4, lambda t: pe.wait_ge(s_n4, t + 1))
    if blocks < 5:
        return

    HC = 2 * PEER_HEADS
    s_kt, s_kte, s_qt5, s_qe5, s_ks, s_kse = (sem("choice_" + n) for n in (
        "keys_turned", "keys_copied", "q_turned", "q_copied", "scores", "scores_copied"))
    s_c5, s_ge, s_gs, s_pick, s_pkt, s_pke = (sem("pick_" + n) for n in (
        "chain", "exps_in", "exps", "done", "turned", "copied"))
    u_rows = peer_u.rearrange("(a b) d -> a b d", b=N_KEYS)
    v_rows = peer_v.rearrange("(a b) d -> a b d", b=N_KEYS)
    u_loaded = [sem(f"u_loaded{s}") for s in range(2)]
    keys_v = sub_keys.rearrange("h c n d -> n (h c) d")

    with nc.Block() as block:
        @block.sync
        def _(sp):
            sp.dma_start(keys[:], keys_v).then_inc(s_keys, 16)
            query_stream.sp(sp)
            for s in range(2):
                sp.dma_start(e_raw[:, s, :], u_rows[:, s, :]).then_inc(u_loaded[s], 16)
            sp.wait_ge(s_spill, 16)

        @block.scalar
        def _(act):
            for j in range(4):
                act.wait_ge(s_kt, j + 1)
                nc.scalar.copy(keysT[:, 4 * j:4 * j + 4, :], turn_ps[:, j % 2, :].rearrange("p (a n) -> p a n", a=4)
                               ).then_inc(s_kte, 1)
            query_stream.split_act(act, query_stream.read_after(act, lambda g, acc: nc.scalar.copy(
                query[:, :, ds(g * GROUP, GROUP)], acc)))
            for j in range(8):
                act.wait_ge(s_qt5, j + 1)
                nc.scalar.copy(queryT[:, 2 * j:2 * j + 2, :], turn_ps[:, j % 2, :].rearrange("p (k s) -> p k s", k=2)
                               ).then_inc(s_qe5, 1)
            for j in range(8):
                act.wait_ge(s_ks, j + 1)
                t, a = j // 4, 4 * (j % 4)
                if j == 0:
                    act.wait_ge(s_spill, 16)
                nc.scalar.copy(key_scores[:, t, a:a + 4, :], spare_ps[:, j % 2, :].rearrange("p (a n) -> p a n", a=4)
                               ).then_inc(s_kse, 1)
            act.wait_ge(s_ge, 1)
            nc.scalar.activation(gate_e[:], gate_e[:], ACT.Exp).then_inc(s_gs, 1)
            for t in range(T):
                act.wait_ge(s_pkt, t + 1)
                nc.scalar.copy(pickT[:, :, t * P:(t + 1) * P],
                               turn_ps[:, t, 0:3 * P].rearrange("p (a k) -> p a k", a=3)).then_inc(s_pke, 1)

        @block.vector
        def _(dve):
            chain = Chain(s_c5)
            query_stream.split_dve(dve, lambda *a: None)

            def wait(n):
                dve.wait_ge(chain.sem, n)
            for t in range(T):
                for a in range(HC):
                    v = key_scores[:, t, a, :]
                    if a % 4 == 0:
                        dve.wait_ge(s_kse, t * 4 + a // 4 + 1)
                    tv, ti = top_v[:, t, a, :], top_i[:, t, a, :]
                    wait(chain.step(nc.vector.max(tv[:, 0:8], v)))
                    wait(chain.step(nc.vector.max_index(ti[:, 0:8], tv[:, 0:8], v)))
                    wait(chain.step(nc.vector.match_replace(v, tv[:, 0:8], v, LOWEST)))
                    wait(chain.step(nc.vector.max(tv[:, 8:16], v)))
                    n = chain.step(nc.vector.max_index(ti[:, 8:16], tv[:, 8:16], v))
            wait(n)
            n = chain.step(nc.vector.tensor_copy(top_if[:], top_i[:]))
            for t in range(T):
                first = top_v[:, t, 0:HC:2, :].unsqueeze(3).broadcast_to([P, PEER_HEADS, TOPK, TOPK])
                second = top_v[:, t, 1:HC:2, :].unsqueeze(2).broadcast_to([P, PEER_HEADS, TOPK, TOPK])
                wait(chain.step(nc.vector.tensor_tensor(cand[:], first, second, ALU.add)))
                for a in range(PEER_HEADS):
                    v = cand[:, a, :, :].rearrange("p i j -> p (i j)")
                    pv, pp = pick_v[:, t, a, :], pick_pos[:, t, a, :]
                    wait(chain.step(nc.vector.max(pv[:, 0:8], v)))
                    wait(chain.step(nc.vector.max_index(pp[:, 0:8], pv[:, 0:8], v)))
                    wait(chain.step(nc.vector.match_replace(v, pv[:, 0:8], v, LOWEST)))
                    wait(chain.step(nc.vector.max(pv[:, 8:16], v)))
                    n = chain.step(nc.vector.max_index(pp[:, 8:16], pv[:, 8:16], v))
                wait(n)
                chain.step(nc.vector.tensor_scalar(pick_ij[:, 0, :, :], pick_pos[:, t, :, :], 4, None,
                                                   ALU.logical_shift_right))
                wait(chain.step(nc.vector.tensor_scalar(pick_ij[:, 1, :, :], pick_pos[:, t, :, :], TOPK - 1, None,
                                                        ALU.bitwise_and)))
                wait(chain.step(nc.vector.tensor_copy(pick_ijf[:], pick_ij[:])))
                count = cst[:, C_IOTA16:C_IOTA16 + TOPK].unsqueeze(1).unsqueeze(1).broadcast_to(
                    [P, PEER_HEADS, TOPK, TOPK])
                for side in range(2):
                    which = pick_ijf[:, side, :, :].unsqueeze(3).broadcast_to([P, PEER_HEADS, TOPK, TOPK])
                    number = top_if[:, t, side:HC:2, :].unsqueeze(2).broadcast_to([P, PEER_HEADS, TOPK, TOPK])
                    wait(chain.step(nc.vector.tensor_tensor(pick_eq[:], count, which, ALU.is_equal)))
                    wait(chain.step(nc.vector.tensor_tensor(pick_eq[:], pick_eq[:], number, ALU.mult)))
                    n = chain.step(nc.vector.tensor_reduce(
                        pick[:, t, side, :].rearrange("p (a k) -> p a k", k=TOPK), pick_eq[:], AX_X, ALU.add))
                    wait(n)
                n = chain.step(nc.vector.tensor_tensor(
                    gate_e[:, t, :, :], pick_v[:, t, :, :],
                    pick_v[:, t, :, 0:1].broadcast_to([P, PEER_HEADS, TOPK]), ALU.subtract))
            wait(n)
            nc.vector.memset(lams[:, 7:8], 0.0).then_inc(s_ge, 1)
            dve.wait_ge(s_gs, 1)
            wait(chain.step(nc.vector.tensor_reduce(gate_s[:, :, 0, :], gate_e[:], AX_X, ALU.add)))
            wait(chain.step(nc.vector.reciprocal(gate_s[:, :, 1, :], gate_s[:, :, 0, :])))
            for t in range(T):
                nc.vector.tensor_tensor(pick[:, t, 2, :].rearrange("p (a k) -> p a k", k=TOPK), gate_e[:, t, :, :],
                                        gate_s[:, t, 1, :].unsqueeze(2).broadcast_to([P, PEER_HEADS, TOPK]),
                                        ALU.mult).then_inc(s_pick, 1)

        @block.tensor
        def _(pe):
            pe.wait_ge(s_keys, 16)
            for j in range(4):
                if j >= 2:
                    pe.wait_ge(s_kte, j - 1)
                for k in range(4):
                    ins = nc.tensor.transpose(turn_ps[:, j % 2, k * P:(k + 1) * P], keys[:, 4 * j + k, :], ident)
                ins.then_inc(s_kt, 1)
            query_stream.pe(pe, hT)
            pe.wait_ge(query_stream.read_out[0], 2)
            pe.wait_ge(query_stream.read_out[1], 2)
            for j in range(8):
                pe.wait_ge(s_kte, 4)
                if j >= 2:
                    pe.wait_ge(s_qe5, j - 1)
                for k in range(2):
                    kt = 2 * j + k
                    for t in range(T):
                        ins = nc.tensor.transpose(turn_ps[:, j % 2, k * S + t * P:k * S + (t + 1) * P],
                                                  query[:, t, kt * P:(kt + 1) * P], ident)
                ins.then_inc(s_qt5, 1)
            pe.wait_ge(s_qe5, 8)
            for j in range(8):
                t, a = j // 4, 4 * (j % 4)
                if j >= 2:
                    pe.wait_ge(s_kse, j - 1)
                for k in range(4):
                    ins = nc.tensor.matmul(spare_ps[:, j % 2, k * P:(k + 1) * P],
                                           queryT[:, a + k, t * P:(t + 1) * P], keysT[:, a + k, :],
                                           start=True, stop=True)
                ins.then_inc(s_ks, 1)
            for t in range(T):
                pe.wait_ge(s_pick, t + 1)
                for k in range(3):
                    ins = nc.tensor.transpose(turn_ps[:, t, k * P:(k + 1) * P], pick[:, t, k, :], ident)
                ins.then_inc(s_pkt, 1)
    if blocks < 6:
        return

    oh_ready = [sem(f"onehot_ready{a}") for a in range(2)]
    g_made = [sem(f"gates_made{a}") for a in range(2)]
    g_out = [sem(f"gates_copied{a}") for a in range(2)]
    count_row = cst[:, C_IOTA:C_IOTA + P]
    STEPS = S // 8

    def peeled(eng, body):
        body(0)
        with eng.Fori(1, STEPS) as i:
            body(i)

    with nc.Block() as block:
        @block.vector
        def _(dve):
            def body(i):
                for a in range(2):
                    wait_used(dve, g_made[a], i)
                    for j in range(4):
                        tok = i * 8 + (4 * a + j)
                        nc.vector.tensor_scalar(onehot[:, a, j, 0, :], count_row, pickT[:, 0, ds(tok, 1)], None,
                                                ALU.is_equal)
                        ins = nc.vector.tensor_scalar(onehot[:, a, j, 1, :], count_row, pickT[:, 1, ds(tok, 1)],
                                                      pickT[:, 2, ds(tok, 1)], ALU.is_equal, ALU.mult)
                    ins.then_inc(oh_ready[a], 1)
            peeled(dve, body)

        @block.tensor
        def _(pe):
            def body(i):
                for a in range(2):
                    pe.wait_ge(oh_ready[a], i + 1)
                    wait_used(pe, g_out[a], i)
                    for j in range(4):
                        ins = nc.tensor.matmul(turn_ps[:, a, j * P:(j + 1) * P], onehot[:, a, j, 0, :],
                                               onehot[:, a, j, 1, :], start=True, stop=True)
                    ins.then_inc(g_made[a], 1)
            peeled(pe, body)

        @block.scalar
        def _(act):
            def body(i):
                for a in range(2):
                    act.wait_ge(g_made[a], i + 1)
                    nc.scalar.copy(gates[:, :, ds(i * 8 + 4 * a, 4)].rearrange("p n t -> p t n"),
                                   turn_ps[:, a, :].rearrange("p (t n) -> p t n", t=4)).then_inc(g_out[a], 1)
            peeled(act, body)
    if blocks < 7:
        return

    up_turned = [sem(f"u_turned{s}") for s in range(4)]
    up_hi = [sem(f"u_hi{s}") for s in range(4)]
    up_lo = [sem(f"u_lo{s}") for s in range(4)]
    up_used = [sem(f"u_used{s}") for s in range(4)]
    h2_out = [sem(f"score_lo_copied{a}") for a in range(2)]
    h_sum = [sem(f"score_summed{a}") for a in range(2)]
    h_gelu = [sem(f"score_gelu{a}") for a in range(2)]
    h_gated = [sem(f"score_gated{a}") for a in range(2)]
    v_loaded = [sem(f"v_loaded{s}") for s in range(2)]
    STEPS = N_KEYS // 2
    tq = stream_acc[:].rearrange("p a t n -> p (a t) n")

    def steps_of(eng, body):
        body(0, True, False)
        with eng.Fori(1, STEPS - 1) as i:
            body(i, False, False)
        body(STEPS - 1, False, True)

    with nc.Block() as block:
        @block.sync
        def _(sp):
            def body(i, first, last):
                for a in range(2):
                    sp.wait_ge(up_turned[3], i * 2 + (a + 1))
                    if last:
                        sp.dma_start(e_raw[:, a, :], v_rows[:, a, :]).then_inc(v_loaded[a], 16)
                    else:
                        sp.dma_start(e_raw[:, a, :].unsqueeze(1), u_rows[:, ds(i * 2 + (2 + a), 1), :]
                                     ).then_inc(u_loaded[a], 16)
            steps_of(sp, body)

        @block.tensor
        def _(pe):
            def turn(i, k):
                s, a = k % 4, (k // 4) % 2
                if s == 0:
                    pe.wait_ge(u_loaded[a], i * 16 + 16 * (k // 8 + 1))
                wait_used(pe, up_lo[s], i * 2 + k // 4)
                for j in range(4):
                    c = (4 * s + j) * P
                    ins = nc.tensor.transpose(tq[:, s, j * P:(j + 1) * P], e_raw[:, a, c:c + P], ident)
                ins.then_inc(up_turned[s], 1)

            def score(i, k):
                s, a = k % 4, k // 4
                pe.wait_ge(up_lo[s], i * 2 + (k // 4 + 1))
                if s == 0:
                    wait_used(pe, h_sum[a], i)
                for j in range(4):
                    kt = 4 * s + j
                    nc.tensor.matmul(turn_ps[:, a, :], uT_hi[:, s, j, :], hT[:, kt, :],
                                     start=(kt == 0), stop=False)
                    ins = nc.tensor.matmul(turn_ps[:, a, 0:S], uT_lo[:, s, j, :], hT[:, kt, 0:S],
                                           start=False, stop=(kt == KT - 1))
                ins.then_inc(up_used[s], 1)

            turn(0, 0)
            turn(0, 1)

            def body(i, first, last):
                for k in range(8):
                    if not (last and k >= 6):
                        turn(i, k + 2)
                    score(i, k)
            steps_of(pe, body)

        @block.scalar
        def _(act):
            def finish(i, a):
                act.wait_ge(up_used[3], i * 2 + (a + 1))
                wait_used(act, h_gated[a], i)
                nc.scalar.copy(act_tmp[:, a, :], turn_ps[:, a, S:2 * S]).then_inc(h2_out[a], 1)

            def gelu(i, a):
                act.wait_ge(h_sum[a], i + 1)
                nc.scalar.activation(act_tmp[:, a, :], act_tmp[:, a, :], ACT.Gelu).then_inc(h_gelu[a], 1)

            def body(i, first, last):
                for k in range(8):
                    s = k % 4
                    act.wait_ge(up_turned[s], i * 2 + (k // 4 + 1))
                    wait_used(act, up_used[s], i * 2 + k // 4)
                    nc.scalar.copy(uT_hi[:, s, :, :], tq[:, s, :].rearrange("p (j n) -> p j n", j=4)
                                   ).then_inc(up_hi[s], 1)
                    if k == 6:
                        finish(i, 0)
                    if k == 7:
                        gelu(i, 0)
                    if k == 2 and not first:
                        finish(i - 1, 1)
                    if k == 3 and not first:
                        gelu(i - 1, 1)
                if last:
                    finish(i, 1)
                    gelu(i, 1)
            steps_of(act, body)

        @block.vector
        def _(dve):
            def add(i, a):
                dve.wait_ge(h2_out[a], i + 1)
                nc.vector.tensor_tensor(act_tmp[:, a, :], turn_ps[:, a, 0:S], act_tmp[:, a, :], ALU.add
                                        ).then_inc(h_sum[a], 1)

            def gate(i, a):
                dve.wait_ge(h_gelu[a], i + 1)
                g = gates[:, ds(i * 2 + a, 1), :]
                nc.vector.tensor_tensor(g, g, act_tmp[:, a, :].unsqueeze(1), ALU.mult).then_inc(h_gated[a], 1)

            def body(i, first, last):
                for k in range(8):
                    s = k % 4
                    dve.wait_ge(up_hi[s], i * 2 + (k // 4 + 1))
                    nc.vector.tensor_tensor(uT_lo[:, s, :, :], tq[:, s, :].rearrange("p (j n) -> p j n", j=4),
                                            f(uT_hi[:, s, :, :]), ALU.subtract).then_inc(up_lo[s], 1)
                    if k == 6:
                        add(i, 0)
                    if k == 2 and not first:
                        add(i - 1, 1)
                    if k == 3 and not first:
                        gate(i - 1, 1)
                    if k == 7:
                        gate(i, 0)
                if last:
                    add(i, 1)
                    gate(i, 1)
            steps_of(dve, body)
    if blocks < 8:
        return

    s_vhi, s_vlo, s_ahi, s_alo, s_vused = ([sem(f"{n}{s}") for s in range(2)] for n in (
        "v_hi", "v_lo", "a_hi", "a_lo", "v_used"))
    s_h1in, s_gb8, s_c8, s_var8, s_root8, s_n8, s_res, s_done = (sem("ln2_" + n) for n in (
        "h1_in", "gb_in", "chain", "var", "root", "normed", "residual", "stored"))

    def y_bank(t, q):
        if q < 2:
            return stream_acc[:, q, t, :]
        return (turn_ps if q == 2 else spare_ps)[:, t, :]

    with nc.Block() as block:
        @block.sync
        def _(sp):
            sp.dma_start(h1[:], spill_v).then_inc(s_h1in, 16)

            def body(i, first, last):
                for a in range(2):
                    sp.wait_ge(s_vlo[a], i + 1)
                    if not last:
                        sp.dma_start(e_raw[:, a, :].unsqueeze(1), v_rows[:, ds(i * 2 + (2 + a), 1), :]
                                     ).then_inc(v_loaded[a], 16)
            steps_of(sp, body)
            for j, v in enumerate((ln2_g, ln2_b)):
                sp.dma_start(ln2_gb[:, j, :], broadcast_rows(v)).then_inc(s_gb8, 16)
            for t in range(T):
                sp.wait_ge(s_n8, t + 1)
                sp.dma_start(out_v[:, t, :], final[:, t, :]).then_inc(s_done, 16)
            sp.wait_ge(s_done, 32)

        @block.gpsimd
        def _(pool):
            inverse_root(pool, s_var8, s_root8)

        @block.scalar
        def _(act):
            def body(i, first, last):
                for a in range(2):
                    act.wait_ge(v_loaded[a], i * 16 + 16)
                    wait_used(act, s_vused[a], i)
                    nc.scalar.copy(a_hi[:, a, :].unsqueeze(1), gates[:, ds(i * 2 + a, 1), :]).then_inc(s_ahi[a], 1)
                    nc.scalar.copy(v_hi[:, a, :], e_raw[:, a, :]).then_inc(s_vhi[a], 1)
            steps_of(act, body)

        @block.vector
        def _(dve):
            def body(i, first, last):
                for a in range(2):
                    dve.wait_ge(s_ahi[a], i + 1)
                    nc.vector.tensor_tensor(a_lo[:, a, :].unsqueeze(1), gates[:, ds(i * 2 + a, 1), :],
                                            f(a_hi[:, a, :]).unsqueeze(1), ALU.subtract).then_inc(s_alo[a], 1)
                    dve.wait_ge(s_vhi[a], i + 1)
                    nc.vector.tensor_tensor(v_lo[:, a, :], e_raw[:, a, :], f(v_hi[:, a, :]), ALU.subtract
                                            ).then_inc(s_vlo[a], 1)
            steps_of(dve, body)
            chain = Chain(s_c8)
            dve.wait_ge(s_h1in, 16)
            dve.wait_ge(s_vused[1], STEPS)
            for t in range(T):
                for q in range(4):
                    n = chain.step(nc.vector.scalar_tensor_tensor(
                        final[:, t, q * 512:(q + 1) * 512], h1[:, t, q * 512:(q + 1) * 512], ALPHA, y_bank(t, q),
                        ALU.mult, ALU.add))
            dve.wait_ge(chain.sem, n)
            norm_stats(dve, chain, final, s_var8)
            dve.wait_ge(s_gb8, 32)
            norm_apply(dve, chain, final, ln2_gb, s_root8, s_n8)

        @block.tensor
        def _(pe):
            def body(i, first, last):
                for a in range(2):
                    pe.wait_ge(s_vlo[a], i + 1)
                    pe.wait_ge(s_alo[a], i + 1)
                    for t in range(T):
                        hi, lo = a_hi[:, a, t * P:(t + 1) * P], a_lo[:, a, t * P:(t + 1) * P]
                        start, stop = first and a == 0, last and a == 1
                        for q in range(4):
                            nc.tensor.matmul(y_bank(t, q), hi, v_hi[:, a, q * 512:(q + 1) * 512],
                                             start=start, stop=False)
                        for q in range(4):
                            nc.tensor.matmul(y_bank(t, q), hi, v_lo[:, a, q * 512:(q + 1) * 512],
                                             start=False, stop=False)
                        for q in range(4):
                            ins = nc.tensor.matmul(y_bank(t, q), lo, v_hi[:, a, q * 512:(q + 1) * 512],
                                                   start=False, stop=stop)
                    ins.then_inc(s_vused[a], 1)
            steps_of(pe, body)


_INS = ["x", "ln_emb_g", "ln_emb_b", "w_in", "dil_norm_g", "lambda_q1", "lambda_k1", "lambda_q2", "lambda_k2",
        "subln_g", "w_out", "ln1_g", "ln1_b", "peer_w_query", "peer_sub_keys", "peer_u", "peer_v", "ln2_g", "ln2_b"]
_LAYERED = {"w_in", "w_out", "peer_w_query", "peer_sub_keys", "peer_u", "peer_v"}


def kernel(**inputs):
    import concourse.bacc as _bacc
    from concourse.bass_utils import run_bass_kernel_spmd as _run

    nc = _bacc.Bacc("TRN2", target_bir_lowering=False, num_devices=1)
    arrays, args = {}, []
    for name in _INS:
        a = np.ascontiguousarray(inputs[name])
        if name in _LAYERED:
            a = a[0]
        arrays[f"in_{name}_dram"] = a
        args.append(nc.dram_tensor(f"in_{name}_dram", a.shape, F32, kind="ExternalInput").ap())
    arrays["constants_dram"] = shape_constants()
    args.append(nc.dram_tensor("constants_dram", (P, C_END), F32, kind="ExternalInput").ap())
    args.append(nc.dram_tensor("h1_spill", (S, D), F32, kind="Internal").ap())
    args.append(nc.dram_tensor("out_0_dram", (1, S, D), F32, kind="ExternalOutput").ap())
    encoder_layer(nc, *args)
    r = _run(nc, [arrays], core_ids=[0])
    return r.results[0]["out_0_dram"]
```

```python
import math
from contextlib import ExitStack

import numpy as np

import concourse.bass as bass
from concourse import mybir
from concourse.alu_op_type import AluOpType as ALU

F32 = mybir.dt.float32
F32R = mybir.dt.float32r
U32 = mybir.dt.uint32
ACT = mybir.ActivationFunctionType
AX_X = mybir.AxisListType.X
ds = bass.ds

P = 128
D = 2048
S = 256
T = S // P
KT = D // P
DH = 128
DIL_HEADS = 12
DIFF_HEADS = 4
DIFF_DQ = 64
IN_WIDTH = 3 * DIL_HEADS * DH + 3 * DIFF_HEADS * 2 * DIFF_DQ
COL_QD = 3 * DIL_HEADS * DH
COL_KD = COL_QD + DIFF_HEADS * DH
COL_VD = COL_KD + DIFF_HEADS * DH
ROPE_THETA = 500000.0
HALF_DIL = DH // 4 // 2
HALF_DIFF = DIFF_DQ // 4 // 2
DIL_CONFIGS = ((128, 1), (512, 4), (2048, 16))
PEER_HEADS = 8
N_KEYS = 128
TOPK = 16
LN_EPS = 1e-5
ALPHA = 2.0 ** 0.25
LAM_INIT = 0.8 - 0.6 * math.exp(-0.0)
LOWEST = -3.0e38
GROUP = 512
CHUNK_KT = 4
CHUNKS = KT // CHUNK_KT

C_ID = 0
C_IOTA = C_ID + P
C_IOTA16 = C_IOTA + P
C_KEPT = C_IOTA16 + TOPK
C_MASK = C_KEPT
C_ROPE = C_MASK + T * S
ROPE_W = 2 * HALF_DIL + 2 * HALF_DIFF
C_END = C_ROPE + T * ROPE_W


def shape_constants():
    c = np.zeros((P, C_END), np.float32)
    c[:, C_ID:C_ID + P] = np.eye(P, dtype=np.float32)
    c[:, C_IOTA:C_IOTA + P] = np.arange(P, dtype=np.float32)
    c[:, C_IOTA16:C_IOTA16 + TOPK] = np.arange(TOPK, dtype=np.float32)
    q, k = np.arange(S)[:, None], np.arange(S)[None, :]
    count = np.zeros((S, S), np.int64)
    for window, dilation in DIL_CONFIGS:
        near = np.abs(q // dilation - k // dilation) <= window // (2 * dilation)
        count += near & (q % dilation == k % dilation)
    log_count = np.where(count > 0, np.log(np.maximum(count, 1)) * DH ** 0.5, -1e30)
    c[:, C_MASK:C_MASK + T * S] = log_count.reshape(T, P, S).transpose(1, 0, 2).reshape(P, T * S)
    rope = []
    for half in (HALF_DIL, HALF_DIFF):
        exponent = np.arange(0, 2 * half, 2, dtype=np.float32) / np.float32(2 * half)
        inv = np.float32(1.0) / np.power(np.float32(ROPE_THETA), exponent)
        angle = np.arange(S, dtype=np.float32)[:, None] * inv[None, :]
        rope += [np.cos(angle), np.sin(angle)]
    rope = np.concatenate(rope, axis=1).astype(np.float32)
    c[:, C_ROPE:] = rope.reshape(T, P, ROPE_W).transpose(1, 0, 2).reshape(P, T * ROPE_W)
    return c


class Chain:

    def __init__(self, sem):
        self.sem, self.n = sem, 0

    def step(self, ins):
        ins.then_inc(self.sem, 1)
        self.n += 1
        return self.n


def encoder_layer(nc, x, ln_emb_g, ln_emb_b, w_in, dil_norm_g, lambda_q1, lambda_k1, lambda_q2, lambda_k2,
                  subln_g, w_out, ln1_g, ln1_b, w_query, sub_keys, peer_u, peer_v, ln2_g, ln2_b,
                  constants, h1_spill, out, blocks=99):
    x_v = x.rearrange("o (t p) d -> p (o t) d", p=P)
    out_v = out.rearrange("o (t p) d -> p (o t) d", p=P)
    spill_v = h1_spill.rearrange("(t p) d -> p t d", p=P)

    BASE = 16512
    at = [BASE]

    def small(name, shape, dt=F32):
        size = 4 * int(np.prod(shape[1:]))
        size += -size % 32
        t = nc.alloc_sbuf_tensor_at(name, shape, dt, offset=at[0])
        at[0] += size
        return t

    def place(name, shape, dt, offset):
        return nc.alloc_sbuf_tensor_at(name, shape, dt, offset=offset)

    cst = small("cst", [P, C_KEPT])
    pickT = small("pickT", [P, 3, S])
    lams = small("lams", [P, 8])
    stats = small("stats", [P, T, 4, 6])
    meanvar = small("meanvar", [P, T, 2])
    rstd = small("rstd", [P, T, 2])
    mhalf = small("mhalf", [P, 32])
    pick_v = small("pick_v", [P, 16])
    ONEHOT0 = at[0]
    att_cst = small("att_cst", [P, C_END - C_KEPT])
    lamv = small("lamv", [P, 4, DIFF_DQ])
    g_col = small("g_col", [P, 4])
    row_max = small("row_max", [P, 16, 4])
    neg_max = small("neg_max", [P, 16, 4])
    den = small("den", [P, 16, 4])
    rden = small("rden", [P, 16, 4])
    lam_rden = small("lam_rden", [P, 4, 2])
    sumsq = small("sumsq", [P, T, 16])
    rms = small("rms", [P, T, 16])
    KB = 1024
    HT0 = ONEHOT0 + 8 * KB
    assert at[0] <= HT0, at[0] - HT0
    ident = cst[:, C_ID:C_ID + P]
    R0 = HT0 + 32 * KB
    hT = place("hT", [P, KT, 2 * S], F32R, HT0)
    h = place("h", [P, T, D], F32, R0)
    w_raw = place("w_raw", [P, 4, CHUNK_KT, GROUP], F32, R0 + 16 * KB)
    w_hi = place("w_hi", [P, 2, CHUNK_KT, GROUP], F32R, R0 + 48 * KB)
    w_lo = place("w_lo", [P, 2, CHUNK_KT, GROUP], F32R, R0 + 64 * KB)
    ln_gb = place("ln_gb", [P, 2, D], F32, R0 + 80 * KB)
    proj = place("proj", [P, T, IN_WIDTH], F32, R0 + 96 * KB)
    qkT = place("qkT", [P, 32, S], F32, R0 + 48 * KB)
    mixed = place("mixed", [P, T, D], F32, HT0)
    scores = place("scores", [P, 2, T, S], F32, HT0 + 16 * KB)
    probs = place("probs", [P, 2, 2, T, S], F32, HT0 + 20 * KB)
    probsT = place("probsT", [P, 2, T, S], F32, HT0 + 28 * KB)
    rope_tmp = place("rope_tmp", [P, 4, 2 * DIL_HEADS * HALF_DIL], F32, R0 + 144 * KB)
    square = place("square", [P, P], F32, R0 + 150 * KB)
    mixT = place("mixT", [P, KT, 2 * S], F32R, R0 + 96 * KB)
    query = place("query", [P, T, D], F32, R0 + 96 * KB)
    queryT = place("queryT", [P, KT, S], F32, R0 + 112 * KB)
    keys = place("keys", [P, 2 * PEER_HEADS, P], F32, R0 + 80 * KB)
    keysT = place("keysT", [P, 2 * PEER_HEADS, N_KEYS], F32, R0 + 88 * KB)
    UNITS = T * PEER_HEADS
    key_scores = place("key_scores", [P, UNITS, 2, N_KEYS], F32, R0 + 96 * KB)
    TK = R0 + 112 * KB
    unit_s = place("unit_s", [P, 2, N_KEYS], F32, TK)
    top_v = place("top_v", [P, 2, TOPK], F32, TK + 1024)
    top_i = place("top_i", [P, 2, TOPK], U32, TK + 1152)
    top_if = place("top_if", [P, 2, TOPK], F32, TK + 1280)
    cand = place("cand", [P, TOPK, TOPK], F32, TK + 2048)
    pick_eq = place("pick_eq", [P, 2, TOPK, TOPK], F32, TK + 3072)
    pick_pos = place("pick_pos", [P, TOPK], U32, TK + 5120)
    pick_ij = place("pick_ij", [P, 2, TOPK], U32, TK + 5184)
    pick_ijf = place("pick_ijf", [P, 2, TOPK], F32, TK + 5312)
    pick = place("pick", [P, 3, UNITS, TOPK], F32, TK + 6144)
    pick_sums = place("pick_sums", [P, UNITS, TOPK], F32, TK + 9216)
    gate_e = place("gate_e", [P, UNITS, TOPK], F32, TK + 10240)
    gate_s = place("gate_s", [P, 2, UNITS], F32, TK + 11264)
    gates = place("gates", [P, N_KEYS, S], F32, R0)
    onehot = place("onehot", [P, 2, 4, 2, P], F32, ONEHOT0)
    e_raw = place("e_raw", [P, 2, D], F32, R0 + 128 * KB)
    uT_hi = place("uT_hi", [P, 4, 4, P], F32R, R0 + 144 * KB)
    uT_lo = place("uT_lo", [P, 4, 4, P], F32R, R0 + 152 * KB)
    act_tmp = place("act_tmp", [P, 2, S], F32, R0 + 160 * KB)
    v_hi = place("v_hi", [P, 2, D], F32R, HT0)
    v_lo = place("v_lo", [P, 2, D], F32R, HT0 + 16 * KB)
    h1 = place("h1", [P, T, D], F32, R0 + 144 * KB)
    a_hi = place("a_hi", [P, 2, S], F32R, R0 + 160 * KB)
    a_lo = place("a_lo", [P, 2, S], F32R, ONEHOT0)
    final = place("final", [P, T, D], F32, R0)
    ln2_gb = place("ln2_gb", [P, 2, D], F32, R0 + 16 * KB)

    sem = nc.alloc_semaphore

    def banks(name, shape):
        return nc.psum_tensor(name, shape, F32)

    def wait_used(eng, s, n):
        if not (isinstance(n, int) and n == 0):
            eng.wait_ge(s, n)

    def broadcast_rows(v):
        return v.rearrange("o d -> (o d)").partition_broadcast(P)

    def f(ap):
        return ap.bitcast(F32)

    def norm_stats(dve, chain, src, ready):
        for t in range(T):
            for c in range(4):
                n = chain.step(nc.vector.bn_stats(stats[:, t, c, :], src[:, t, c * 512:(c + 1) * 512]))
        dve.wait_ge(chain.sem, n)
        for t in range(T):
            n = chain.step(nc.vector.bn_aggr(meanvar[:, t, :], stats[:, t, :, :]))
        dve.wait_ge(chain.sem, n)
        nc.vector.tensor_scalar(rstd[:, :, 0], meanvar[:, :, 1], LN_EPS, None, ALU.add).then_inc(ready, 1)

    def inverse_root(pool, ready, done):
        pool.wait_ge(ready, 1)
        nc.gpsimd.tensor_tensor(rstd[:, :, 1], rstd[:, :, 0], mhalf[:, 0:T], ALU.pow).then_inc(done, 1)

    def norm_apply(dve, chain, buf, gb, done, norm_done):
        dve.wait_ge(done, 1)
        for t in range(T):
            n = chain.step(nc.vector.tensor_scalar(buf[:, t, :], buf[:, t, :], meanvar[:, t, 0:1],
                                                   rstd[:, t, 1:2], ALU.subtract, ALU.mult))
            dve.wait_ge(chain.sem, n)
            n = chain.step(nc.vector.tensor_tensor(buf[:, t, :], buf[:, t, :], gb[:, 0, :], ALU.mult))
            dve.wait_ge(chain.sem, n)
            nc.vector.tensor_tensor(buf[:, t, :], buf[:, t, :], gb[:, 1, :], ALU.add).then_inc(norm_done, 1)

    def turn_pe(pe, tp, src, sem_turned, sem_lo, wait_src):
        for j in range(KT // 2):
            if j >= 2:
                pe.wait_ge(sem_lo, j - 1)
            for t in range(T):
                if j == 0:
                    wait_src(t)
                for k in range(2):
                    kt = 2 * j + k
                    last = nc.tensor.transpose(tp[:, j % 2, k * S + t * P:k * S + (t + 1) * P],
                                               src[:, t, kt * P:(kt + 1) * P], ident)
            last.then_inc(sem_turned, 1)

    def turn_act(act, tp, dst, sem_turned, sem_hi, gain):
        for j in range(KT // 2):
            act.wait_ge(sem_turned, j + 1)
            o = dst[:, 2 * j:2 * j + 2, 0:S]
            i = tp[:, j % 2, :].rearrange("p (k s) -> p k s", k=2)
            g = gain(2 * j)
            if g is None:
                nc.scalar.copy(o, i).then_inc(sem_hi, 1)
            else:
                nc.scalar.activation(o, i, ACT.Copy, scale=g).then_inc(sem_hi, 1)

    def turn_dve(dve, tp, dst, sem_hi, sem_lo, gain):
        for j in range(KT // 2):
            dve.wait_ge(sem_hi, j + 1)
            o = dst[:, 2 * j:2 * j + 2, S:2 * S]
            hi = f(dst[:, 2 * j:2 * j + 2, 0:S])
            i = tp[:, j % 2, :].rearrange("p (k s) -> p k s", k=2)
            g = gain(2 * j)
            if g is None:
                nc.vector.tensor_tensor(o, i, hi, ALU.subtract).then_inc(sem_lo, 1)
            else:
                nc.vector.scalar_tensor_tensor(o, i, g, hi, ALU.mult, ALU.subtract).then_inc(sem_lo, 1)

    class Stream:
        def __init__(self, name, w, groups, acc):
            self.w = w.rearrange("(c k p) (g n) -> p c k g n", k=CHUNK_KT, p=P, n=GROUP)
            self.steps, self.acc = groups // 2, acc
            self.loaded = [sem(f"{name}_loaded{c}") for c in range(CHUNKS)]
            self.hi = [sem(f"{name}_hi{s}") for s in range(2)]
            self.lo = [sem(f"{name}_lo{s}") for s in range(2)]
            self.used = [sem(f"{name}_used{s}") for s in range(2)]
            self.read_out = [sem(f"{name}_read_out{u}") for u in range(2)]

        def load(self, sp, g, c):
            sp.dma_start(w_raw[:, c, :, :].unsqueeze(2), self.w[:, c, :, ds(g, 1), :]).then_inc(self.loaded[c], 16)

        def prefetch(self, sp):
            for c in range(CHUNKS):
                self.load(sp, 0, c)

        def steps_of(self, eng, body):
            body(0, True, self.steps == 1)
            if self.steps > 2:
                with eng.Fori(1, self.steps - 1) as i:
                    body(i, False, False)
            if self.steps > 1:
                body(self.steps - 1, False, True)

        def sp(self, sp):
            def body(i, first, last):
                for u in range(1 if last else 2):
                    for c in range(CHUNKS):
                        sp.wait_ge(self.lo[c % 2], i * 4 + (2 * u + c // 2 + 1))
                        self.load(sp, i * 2 + (u + 1), c)
            self.steps_of(sp, body)

        def split_act(self, act, after_chunk):
            def body(i, first, last):
                for u in range(2):
                    for c in range(CHUNKS):
                        s = c % 2
                        act.wait_ge(self.loaded[c], i * 32 + 16 * (u + 1))
                        if not (first and u == 0 and c < 2):
                            act.wait_ge(self.used[s], i * 4 + (2 * u + c // 2))
                        nc.scalar.copy(w_hi[:, s, :, :], w_raw[:, c, :, :]).then_inc(self.hi[s], 1)
                        after_chunk(i, first, last, u, c)
            self.steps_of(act, body)

        def split_dve(self, dve, after_chunk):
            def body(i, first, last):
                for u in range(2):
                    for c in range(CHUNKS):
                        s = c % 2
                        dve.wait_ge(self.hi[s], i * 4 + (2 * u + c // 2 + 1))
                        nc.vector.tensor_tensor(w_lo[:, s, :, :], w_raw[:, c, :, :], f(w_hi[:, s, :, :]),
                                                ALU.subtract).then_inc(self.lo[s], 1)
                        after_chunk(i, first, last, u, c)
            self.steps_of(dve, body)

        def read_after(self, eng, read):
            def after_chunk(i, first, last, u, c):
                if c == 1 and not (first and u == 0):
                    ip, up = (i, 0) if u == 1 else (i - 1, 1)
                    eng.wait_ge(self.used[1], i * 4 + 2 * u)
                    read(ip * 2 + up, self.acc[:, up, :, :]).then_inc(self.read_out[up], 1)
                if last and u == 1 and c == CHUNKS - 1:
                    eng.wait_ge(self.used[1], i * 4 + 4)
                    read(i * 2 + 1, self.acc[:, 1, :, :]).then_inc(self.read_out[1], 1)
            return after_chunk

        def pe(self, pe, actT):
            def body(i, first, last):
                for u in range(2):
                    for c in range(CHUNKS):
                        s = c % 2
                        pe.wait_ge(self.lo[s], i * 4 + (2 * u + c // 2 + 1))
                        if c == 0 and not first:
                            pe.wait_ge(self.read_out[u], i)
                        for k in range(CHUNK_KT):
                            kt = c * CHUNK_KT + k
                            for t in range(T):
                                hi, lo = (actT[:, kt, b + t * P:b + (t + 1) * P] for b in (0, S))
                                o = self.acc[:, u, t, :]
                                nc.tensor.matmul(o, hi, w_hi[:, s, k, :], start=(kt == 0), stop=False)
                                nc.tensor.matmul(o, hi, w_lo[:, s, k, :], start=False, stop=False)
                                mm = nc.tensor.matmul(o, lo, w_hi[:, s, k, :], start=False, stop=(kt == KT - 1))
                        mm.then_inc(self.used[s], 1)
            self.steps_of(pe, body)

    stream_acc = nc.alloc_psum_tensor("stream_acc", [P, 2, T, GROUP], F32)
    turn_ps = nc.alloc_psum_tensor("turn_ps", [P, 2, 512], F32)
    spare_ps = nc.alloc_psum_tensor("spare_ps", [P, 2, 512], F32)
    in_stream = Stream("w_in", w_in, IN_WIDTH // GROUP, stream_acc)
    out_stream = Stream("w_out", w_out, D // GROUP, stream_acc)
    query_stream = Stream("w_query", w_query, D // GROUP, stream_acc)

    s_const, s_x, s_lng, s_lamv, s_gcol = (sem(n) for n in ("const_in", "x_in", "ln_emb_in", "lambda_in", "gain_in"))
    s_attc = sem("attention_const_in")
    s_pool = sem("minus_half")
    s_c1, s_var1, s_root1, s_n1 = sem("embed_chain"), sem("embed_var"), sem("embed_root"), sem("embed_normed")
    s_t1, s_h1, s_l1 = sem("embed_turned"), sem("embed_hi"), sem("embed_lo")
    s_lam, s_lame = sem("lambda_sums"), sem("lambda_exps")
    with nc.Block() as block:
        @block.sync
        def _(sp):
            sp.dma_start(h[:], x_v).then_inc(s_x, 16)
            sp.dma_start(cst[:], constants[:, 0:C_KEPT]).then_inc(s_const, 16)
            sp.dma_start(att_cst[:], constants[:, C_KEPT:C_END]).then_inc(s_attc, 16)
            for j, v in enumerate((ln_emb_g, ln_emb_b)):
                sp.dma_start(ln_gb[:, j, :], v.partition_broadcast(P)).then_inc(s_lng, 16)
            in_stream.prefetch(sp)
            for j, v in enumerate((lambda_q1, lambda_k1, lambda_q2, lambda_k2)):
                sp.dma_start(lamv[:, j, :], broadcast_rows(v)).then_inc(s_lamv, 16)
            for j, v in enumerate((dil_norm_g, subln_g)):
                sp.dma_start(g_col[:, j:j + 1], v.rearrange("o d -> d o")).then_inc(s_gcol, 16)

        @block.gpsimd
        def _(pool):
            nc.gpsimd.memset(mhalf[:], -0.5).then_inc(s_pool, 1)
            pool.wait_ge(s_pool, 1)
            inverse_root(pool, s_var1, s_root1)

        @block.vector
        def _(dve):
            chain = Chain(s_c1)
            dve.wait_ge(s_x, 16)
            norm_stats(dve, chain, h, s_var1)
            dve.wait_ge(s_lamv, 64)
            for m in range(2):
                n = chain.step(nc.vector.tensor_tensor(lamv[:, 2 * m, :], lamv[:, 2 * m, :],
                                                       lamv[:, 2 * m + 1, :], ALU.mult))
                dve.wait_ge(chain.sem, n)
                nc.vector.tensor_reduce(lams[:, m:m + 1], lamv[:, 2 * m, :], AX_X, ALU.add).then_inc(s_lam, 1)
            dve.wait_ge(s_gcol, 32)
            n = chain.step(nc.vector.tensor_scalar(g_col[:, 1:2], g_col[:, 1:2], 1.0 - LAM_INIT, None, ALU.mult))
            dve.wait_ge(s_lame, 1)
            n = chain.step(nc.vector.tensor_tensor(lams[:, 4:5], lams[:, 3:4], lams[:, 2:3], ALU.subtract))
            dve.wait_ge(chain.sem, n)
            n = chain.step(nc.vector.tensor_scalar(lams[:, 5:6], lams[:, 4:5], LAM_INIT, None, ALU.subtract))
            dve.wait_ge(s_lng, 32)
            norm_apply(dve, chain, h, ln_gb, s_root1, s_n1)
            turn_dve(dve, turn_ps, hT, s_h1, s_l1, lambda kt: None)

        @block.scalar
        def _(act):
            act.wait_ge(s_lam, 2)
            nc.scalar.activation(lams[:, 2:4], lams[:, 0:2], ACT.Exp).then_inc(s_lame, 1)
            turn_act(act, turn_ps, hT, s_t1, s_h1, lambda kt: None)

        @block.tensor
        def _(pe):
            pe.wait_ge(s_const, 16)
            turn_pe(pe, turn_ps, h, s_t1, s_l1, lambda t: pe.wait_ge(s_n1, t + 1))
    if blocks < 2:
        return

    with nc.Block() as block:
        @block.sync
        def _(sp):
            in_stream.sp(sp)

        @block.scalar
        def _(act):
            in_stream.split_act(act, in_stream.read_after(act, lambda g, acc: nc.scalar.copy(
                proj[:, :, ds(g * GROUP, GROUP)], acc)))

        @block.vector
        def _(dve):
            in_stream.split_dve(dve, lambda *a: None)

        @block.tensor
        def _(pe):
            in_stream.pe(pe, hT)
    if blocks < 3:
        return

    def block_col(b):
        return b * P if b < 24 else COL_QD + (b - 24) * P

    HEADS = DIL_HEADS + DIFF_HEADS
    turn_seq = [b for hd in range(DIL_HEADS) for b in (hd, 12 + hd)] + [b for hd in range(4) for b in (24 + hd, 28 + hd)]
    s_c3, s_rope = sem("rope_chain"), sem("rope_done")
    s_qt, s_qe, = sem("qk_turned"), sem("qk_copied")
    s_s, s_mx, s_e, s_nrm, s_pt, s_pte, s_o, s_oe, s_sq = (sem("att_" + n) for n in (
        "scores", "max", "exp", "normed", "turned", "turned_copied", "out", "out_copied", "squares"))
    s_eps, s_root3, s_rms = sem("rms_eps"), sem("rms_root"), sem("rms_done")
    sc_ps = stream_acc

    def is_diff(u):
        return u >= DIL_HEADS

    def v_col(u):
        return 2 * DIL_HEADS * DH + u * DH if not is_diff(u) else COL_VD + (u - DIL_HEADS) * DH

    with nc.Block() as block:
        @block.sync
        def _(sp):
            out_stream.prefetch(sp)

        @block.vector
        def _(dve):
            chain = Chain(s_c3)

            def rope(t, col, heads, width, half, tab):
                v = proj[:, t, col:col + heads * width].rearrange("p (a w) -> p a w", w=width)
                x1, x2 = v[:, :, 0:half], v[:, :, half:2 * half]
                base = C_ROPE - C_KEPT + t * ROPE_W + tab
                cos = att_cst[:, base:base + half].unsqueeze(1).broadcast_to([P, heads, half])
                sin = att_cst[:, base + half:base + 2 * half].unsqueeze(1).broadcast_to([P, heads, half])
                tmp = [rope_tmp[:, j, 0:heads * half].rearrange("p (a w) -> p a w", w=half) for j in range(4)]
                for o, a, b in ((tmp[0], x1, cos), (tmp[1], x2, sin), (tmp[2], x1, sin), (tmp[3], x2, cos)):
                    n = chain.step(nc.vector.tensor_tensor(o, a, b, ALU.mult))
                dve.wait_ge(chain.sem, n)
                chain.step(nc.vector.tensor_tensor(x1, tmp[0], tmp[1], ALU.subtract))
                n = chain.step(nc.vector.tensor_tensor(x2, tmp[2], tmp[3], ALU.add))
                dve.wait_ge(chain.sem, n)
                return n
            dve.wait_ge(s_attc, 16)
            for t in range(T):
                rope(t, 0, 2 * DIL_HEADS, DH, HALF_DIL, 0)
                rope(t, COL_QD, 4 * DIFF_HEADS, DIFF_DQ, HALF_DIFF, 2 * HALF_DIL)
            nc.vector.memset(lams[:, 6:7], 0.0).then_inc(s_rope, 1)

            def row_maxima(u):
                s = u % 2
                dve.wait_ge(s_s, u + 1)
                if not is_diff(u):
                    if u >= 2:
                        dve.wait_ge(s_e, u - 1)
                    for t in range(T):
                        n = chain.step(nc.vector.tensor_tensor_reduce(
                            scores[:, s, t, :], sc_ps[:, s, 0, t * S:(t + 1) * S],
                            att_cst[:, t * S:(t + 1) * S], DH ** -0.5, LOWEST, ALU.add, ALU.max,
                            row_max[:, u, t:t + 1]))
                    w, scale = 2, -1.0
                else:
                    n = chain.step(nc.vector.tensor_reduce(
                        row_max[:, u, :], sc_ps[:, s, :, :].rearrange("p m (t k) -> p (m t) k", t=T), AX_X, ALU.max))
                    w, scale = 4, -DIFF_DQ ** -0.5
                dve.wait_ge(chain.sem, n)
                nc.vector.tensor_scalar(neg_max[:, u, 0:w], row_max[:, u, 0:w], scale, None, ALU.mult).then_inc(s_mx, 1)

            def normalise(u):
                s = u % 2
                dve.wait_ge(s_e, u + 1)
                if not is_diff(u):
                    nc.vector.reciprocal(rden[:, u, 0:2], den[:, u, 0:2]).then_inc(s_nrm, 1)
                    return
                j = u - DIL_HEADS
                n = chain.step(nc.vector.reciprocal(rden[:, u, :], den[:, u, :]))
                dve.wait_ge(chain.sem, n)
                n = chain.step(nc.vector.tensor_scalar(lam_rden[:, j, :], rden[:, u, 2:4], lams[:, 5:6], None, ALU.mult))
                for t in range(T):
                    n = chain.step(nc.vector.tensor_scalar(probs[:, s, 0, t, :], probs[:, s, 0, t, :],
                                                           rden[:, u, t:t + 1], None, ALU.mult))
                dve.wait_ge(chain.sem, n)
                for t in range(T):
                    ins = nc.vector.scalar_tensor_tensor(probs[:, s, 0, t, :], probs[:, s, 1, t, :],
                                                         lam_rden[:, j, t:t + 1], probs[:, s, 0, t, :],
                                                         ALU.mult, ALU.add)
                ins.then_inc(s_nrm, 1)

            def outputs(u):
                dve.wait_ge(s_o, u + 1)
                o = mixed[:, :, u * DH:(u + 1) * DH]
                i = spare_ps[:, u % 2, 0:T * DH].rearrange("p (t d) -> p t d", t=T)
                if is_diff(u):
                    nc.vector.tensor_copy(o, i).then_inc(s_oe, 1)
                else:
                    nc.vector.tensor_tensor(o, i, rden[:, u, 0:2].unsqueeze(2).broadcast_to([P, T, DH]),
                                            ALU.mult).then_inc(s_oe, 1)

            for n in range(HEADS + 3):
                if n < HEADS:
                    row_maxima(n)
                if 1 <= n <= HEADS:
                    normalise(n - 1)
                if n >= 3:
                    outputs(n - 3)
            dve.wait_ge(s_sq, HEADS * T)
            nc.vector.tensor_scalar(sumsq[:], sumsq[:], 1.0 / DH, LN_EPS, ALU.mult, ALU.add).then_inc(s_eps, 1)
            dve.wait_ge(s_root3, 1)
            for t in range(T):
                v = mixed[:, t, :].rearrange("p (u d) -> p u d", d=DH)
                nc.vector.tensor_tensor(v, v, rms[:, t, :].unsqueeze(2).broadcast_to([P, HEADS, DH]),
                                        ALU.mult).then_inc(s_rms, 1)

        @block.gpsimd
        def _(pool):
            pool.wait_ge(s_eps, 1)
            nc.gpsimd.tensor_tensor(rms[:].rearrange("p t u -> p (t u)"), sumsq[:].rearrange("p t u -> p (t u)"),
                                    mhalf[:], ALU.pow).then_inc(s_root3, 1)

        @block.scalar
        def _(act):
            for j in range(16):
                act.wait_ge(s_qt, j + 1)
                for k in range(2):
                    ins = nc.scalar.copy(qkT[:, turn_seq[2 * j + k], :], turn_ps[:, j % 2, k * S:(k + 1) * S])
                ins.then_inc(s_qe, 1)

            def exponentials(u):
                s = u % 2
                act.wait_ge(s_mx, u + 1)
                if u >= 2:
                    act.wait_ge(s_pt, u - 1)
                maps = 2 if is_diff(u) else 1
                for m in range(maps):
                    for t in range(T):
                        src = sc_ps[:, s, m, t * S:(t + 1) * S] if is_diff(u) else scores[:, s, t, :]
                        j = m * T + t
                        ins = nc.scalar.activation(probs[:, s, m, t, :], src, ACT.Exp, bias=neg_max[:, u, j:j + 1],
                                                   scale=DIFF_DQ ** -0.5 if is_diff(u) else 1.0,
                                                   accum_out=den[:, u, j:j + 1])
                ins.then_inc(s_e, 1)

            def copy_turned(u):
                act.wait_ge(s_pt, u + 1)
                if u >= 2:
                    act.wait_ge(s_o, u - 1)
                nc.scalar.copy(probsT[:, u % 2, :, :], turn_ps[:, u % 2, :].rearrange("p (k q) -> p k q", k=T)
                               ).then_inc(s_pte, 1)

            def squares(u):
                act.wait_ge(s_oe, u + 1)
                for t in range(T):
                    if u + t > 0:
                        act.wait_ge(s_sq, u * T + t)
                    nc.scalar.activation(square[:], mixed[:, t, u * DH:(u + 1) * DH], ACT.Square,
                                         accum_out=sumsq[:, t, u:u + 1]).then_inc(s_sq, 1)

            for n in range(HEADS + 4):
                if n < HEADS:
                    exponentials(n)
                if 1 <= n <= HEADS:
                    copy_turned(n - 1)
                if n >= 4:
                    squares(n - 4)

        @block.tensor
        def _(pe):
            pe.wait_ge(s_rope, 1)
            for j in range(16):
                if j >= 2:
                    pe.wait_ge(s_qe, j - 1)
                for k in range(2):
                    c = block_col(turn_seq[2 * j + k])
                    for t in range(T):
                        ins = nc.tensor.transpose(turn_ps[:, j % 2, k * S + t * P:k * S + (t + 1) * P],
                                                  proj[:, t, c:c + P], ident)
                ins.then_inc(s_qt, 1)

            def score(u):
                s = u % 2
                if u >= 2:
                    pe.wait_ge(s_mx, u - 1)
                    if is_diff(u - 2):
                        pe.wait_ge(s_e, u - 1)
                if not is_diff(u):
                    for t in range(T):
                        ins = nc.tensor.matmul(sc_ps[:, s, 0, t * S:(t + 1) * S], qkT[:, u, t * P:(t + 1) * P],
                                               qkT[:, 12 + u, :], start=True, stop=True)
                else:
                    j = u - DIL_HEADS
                    for m in range(2):
                        r = slice(m * DIFF_DQ, (m + 1) * DIFF_DQ)
                        for t in range(T):
                            ins = nc.tensor.matmul(sc_ps[:, s, m, t * S:(t + 1) * S],
                                                   qkT[r, 24 + j, t * P:(t + 1) * P], qkT[r, 28 + j, :],
                                                   start=True, stop=True)
                ins.then_inc(s_s, 1)

            def turn(u):
                s = u % 2
                pe.wait_ge(s_nrm, u + 1)
                if u >= 2:
                    pe.wait_ge(s_pte, u - 1)
                for k in range(T):
                    for t in range(T):
                        ins = nc.tensor.transpose(turn_ps[:, s, k * S + t * P:k * S + (t + 1) * P],
                                                  probs[:, s, 0, t, k * P:(k + 1) * P], ident)
                ins.then_inc(s_pt, 1)

            def weigh(u):
                s = u % 2
                pe.wait_ge(s_pte, u + 1)
                if u >= 2:
                    pe.wait_ge(s_oe, u - 1)
                c = v_col(u)
                for t in range(T):
                    for k in range(T):
                        ins = nc.tensor.matmul(spare_ps[:, s, t * DH:(t + 1) * DH],
                                               probsT[:, s, k, t * P:(t + 1) * P], proj[:, k, c:c + DH],
                                               start=(k == 0), stop=(k == T - 1))
                ins.then_inc(s_o, 1)

            pe.wait_ge(s_qe, 16)
            for n in range(HEADS + 2):
                if n < HEADS:
                    score(n)
                if 1 <= n <= HEADS:
                    turn(n - 1)
                if n >= 2:
                    weigh(n - 2)
    if blocks < 4:
        return

    s_lng4, s_c4, s_var4, s_root4, s_n4 = (sem("ln1_" + n) for n in ("gb_in", "chain", "var", "root", "normed"))
    s_mt, s_mh, s_ml = sem("mix_turned"), sem("mix_hi"), sem("mix_lo")
    s_t4, s_h4, s_l4 = sem("h1_turned"), sem("h1_hi"), sem("h1_lo")
    s_spill, s_keys = sem("h1_spilled"), sem("keys_in")

    def mix_gain(kt):
        return g_col[:, 0:1] if kt < DIL_HEADS else g_col[:, 1:2]

    with nc.Block() as block:
        @block.sync
        def _(sp):
            for j, v in enumerate((ln1_g, ln1_b)):
                sp.dma_start(ln_gb[:, j, :], broadcast_rows(v)).then_inc(s_lng4, 16)
            out_stream.sp(sp)
            sp.wait_ge(out_stream.lo[0], 8)
            sp.wait_ge(out_stream.lo[1], 8)
            query_stream.prefetch(sp)
            sp.wait_ge(s_n4, 2)
            sp.dma_start(spill_v, h[:]).then_inc(s_spill, 16)

        @block.gpsimd
        def _(pool):
            inverse_root(pool, s_var4, s_root4)

        @block.scalar
        def _(act):
            turn_act(act, turn_ps, mixT, s_mt, s_mh, mix_gain)
            out_stream.split_act(act, lambda *a: None)
            turn_act(act, turn_ps, hT, s_t4, s_h4, lambda kt: None)

        @block.vector
        def _(dve):
            chain = Chain(s_c4)
            turn_dve(dve, turn_ps, mixT, s_mh, s_ml, mix_gain)
            out_stream.split_dve(dve, out_stream.read_after(dve, lambda g, acc: nc.vector.scalar_tensor_tensor(
                h[:, :, ds(g * GROUP, GROUP)], h[:, :, ds(g * GROUP, GROUP)], ALPHA, acc, ALU.mult, ALU.add)))
            dve.wait_ge(out_stream.read_out[0], 2)
            dve.wait_ge(out_stream.read_out[1], 2)
            norm_stats(dve, chain, h, s_var4)
            dve.wait_ge(s_lng4, 32)
            norm_apply(dve, chain, h, ln_gb, s_root4, s_n4)
            turn_dve(dve, turn_ps, hT, s_h4, s_l4, lambda kt: None)

        @block.tensor
        def _(pe):
            turn_pe(pe, turn_ps, mixed, s_mt, s_ml, lambda t: None)
            pe.wait_ge(s_ml, 8)
            out_stream.pe(pe, mixT)
            turn_pe(pe, turn_ps, h, s_t4, s_l4, lambda t: pe.wait_ge(s_n4, t + 1))
    if blocks < 5:
        return

    HC = 2 * PEER_HEADS
    s_kt, s_kte, s_qt5, s_qe5, s_ks, s_kse = (sem("choice_" + n) for n in (
        "keys_turned", "keys_copied", "q_turned", "q_copied", "scores", "scores_copied"))
    u_rows = peer_u.rearrange("(a b) d -> a b d", b=N_KEYS)
    v_rows = peer_v.rearrange("(a b) d -> a b d", b=N_KEYS)
    u_loaded = [sem(f"u_loaded{s}") for s in range(2)]
    keys_v = sub_keys.rearrange("h c n d -> n (h c) d")

    with nc.Block() as block:
        @block.sync
        def _(sp):
            sp.dma_start(keys[:], keys_v).then_inc(s_keys, 16)
            query_stream.sp(sp)
            for s in range(2):
                sp.dma_start(e_raw[:, s, :], u_rows[:, s, :]).then_inc(u_loaded[s], 16)
            sp.wait_ge(s_spill, 16)

        @block.scalar
        def _(act):
            for j in range(4):
                act.wait_ge(s_kt, j + 1)
                nc.scalar.copy(keysT[:, 4 * j:4 * j + 4, :], turn_ps[:, j % 2, :].rearrange("p (a n) -> p a n", a=4)
                               ).then_inc(s_kte, 1)
            query_stream.split_act(act, query_stream.read_after(act, lambda g, acc: nc.scalar.copy(
                query[:, :, ds(g * GROUP, GROUP)], acc)))
            for j in range(8):
                act.wait_ge(s_qt5, j + 1)
                nc.scalar.copy(queryT[:, 2 * j:2 * j + 2, :], turn_ps[:, j % 2, :].rearrange("p (k s) -> p k s", k=2)
                               ).then_inc(s_qe5, 1)
            for j in range(8):
                act.wait_ge(s_ks, j + 1)
                nc.scalar.copy(key_scores[:, 2 * j:2 * j + 2, :, :], spare_ps[:, j % 2, :].rearrange(
                    "p (u c n) -> p u c n", u=2, c=2)).then_inc(s_kse, 1)
        @block.vector
        def _(dve):
            query_stream.split_dve(dve, lambda *a: None)

        @block.tensor
        def _(pe):
            pe.wait_ge(s_keys, 16)
            for j in range(4):
                if j >= 2:
                    pe.wait_ge(s_kte, j - 1)
                for k in range(4):
                    ins = nc.tensor.transpose(turn_ps[:, j % 2, k * P:(k + 1) * P], keys[:, 4 * j + k, :], ident)
                ins.then_inc(s_kt, 1)
            query_stream.pe(pe, hT)
            pe.wait_ge(query_stream.read_out[0], 2)
            pe.wait_ge(query_stream.read_out[1], 2)
            for j in range(8):
                pe.wait_ge(s_kte, 4)
                if j >= 2:
                    pe.wait_ge(s_qe5, j - 1)
                for k in range(2):
                    kt = 2 * j + k
                    for t in range(T):
                        ins = nc.tensor.transpose(turn_ps[:, j % 2, k * S + t * P:k * S + (t + 1) * P],
                                                  query[:, t, kt * P:(kt + 1) * P], ident)
                ins.then_inc(s_qt5, 1)
            pe.wait_ge(s_qe5, 8)
            for j in range(8):
                t, a = j // 4, 4 * (j % 4)
                if j >= 2:
                    pe.wait_ge(s_kse, j - 1)
                for k in range(4):
                    ins = nc.tensor.matmul(spare_ps[:, j % 2, k * P:(k + 1) * P],
                                           queryT[:, a + k, t * P:(t + 1) * P], keysT[:, a + k, :],
                                           start=True, stop=True)
                ins.then_inc(s_ks, 1)
    if blocks < 6:
        return

    STEPS = N_KEYS // 2
    PREP = UNITS
    GATE0 = PREP + 1
    GATE_STEPS = S // 8
    GATE1 = GATE0 + GATE_STEPS
    up_turned = [sem(f"u_turned{s}") for s in range(4)]
    up_hi = [sem(f"u_hi{s}") for s in range(4)]
    up_lo = [sem(f"u_lo{s}") for s in range(4)]
    up_used = [sem(f"u_used{s}") for s in range(4)]
    h2_out = [sem(f"score_lo_copied{a}") for a in range(2)]
    h_sum = [sem(f"score_summed{a}") for a in range(2)]
    h_gelu = [sem(f"score_gelu{a}") for a in range(2)]
    h_gated = [sem(f"score_gated{a}") for a in range(2)]
    v_loaded = [sem(f"v_loaded{s}") for s in range(2)]
    s_prep, s_ge, s_gs, s_pick, s_pkt, s_pke, s_ones = (sem("pick_" + n) for n in (
        "gate_chain", "exps_in", "exps", "done", "turned", "copied", "ones"))
    oh_ready = [sem(f"onehot_ready{a}") for a in range(2)]
    g_made = [sem(f"gates_made{a}") for a in range(2)]
    g_mult = [sem(f"gates_multiplied{a}") for a in range(2)]
    tq = stream_acc[:].rearrange("p a t n -> p (a t) n")
    count_row = cst[:, C_IOTA:C_IOTA + P]
    FIRST, PICKS, TURN, GATE_FIRST, GATES, GATE_AFTER, PLAIN, LAST = range(8)

    def expert_steps(eng, body):
        body(0, FIRST)
        with eng.Fori(1, PREP) as i:
            body(i, PICKS)
        body(PREP, TURN)
        body(GATE0, GATE_FIRST)
        with eng.Fori(GATE0 + 1, GATE1) as i:
            body(i, GATES)
        body(GATE1, GATE_AFTER)
        with eng.Fori(GATE1 + 1, STEPS - 1) as i:
            body(i, PLAIN)
        body(STEPS - 1, LAST)

    with nc.Block() as block:
        @block.sync
        def _(sp):
            def body(i, kind):
                for a in range(2):
                    sp.wait_ge(up_turned[3], i * 2 + (a + 1))
                    if kind == LAST:
                        sp.dma_start(e_raw[:, a, :], v_rows[:, a, :]).then_inc(v_loaded[a], 16)
                    else:
                        sp.dma_start(e_raw[:, a, :].unsqueeze(1), u_rows[:, ds(i * 2 + (2 + a), 1), :]
                                     ).then_inc(u_loaded[a], 16)
            expert_steps(sp, body)

        @block.gpsimd
        def _(pool):
            nc.gpsimd.memset(gates[:, 2 * GATE0:96, :], 1.0).then_inc(s_ones, 1)
            pool.wait_ge(s_pkt, T)
            nc.gpsimd.memset(gates[:, 96:N_KEYS, :], 1.0).then_inc(s_ones, 1)

        @block.tensor
        def _(pe):
            def turn(i, k):
                s, a = k % 4, (k // 4) % 2
                if s == 0:
                    pe.wait_ge(u_loaded[a], i * 16 + 16 * (k // 8 + 1))
                wait_used(pe, up_lo[s], i * 2 + k // 4)
                for j in range(4):
                    c = (4 * s + j) * P
                    ins = nc.tensor.transpose(tq[:, s, j * P:(j + 1) * P], e_raw[:, a, c:c + P], ident)
                ins.then_inc(up_turned[s], 1)

            def score(i, k):
                s, a = k % 4, k // 4
                pe.wait_ge(up_lo[s], i * 2 + (k // 4 + 1))
                if s == 0:
                    wait_used(pe, h_sum[a], i)
                for j in range(4):
                    kt = 4 * s + j
                    nc.tensor.matmul(turn_ps[:, a, :], uT_hi[:, s, j, :], hT[:, kt, :],
                                     start=(kt == 0), stop=False)
                    ins = nc.tensor.matmul(turn_ps[:, a, 0:S], uT_lo[:, s, j, :], hT[:, kt, 0:S],
                                           start=False, stop=(kt == KT - 1))
                ins.then_inc(up_used[s], 1)

            def turn_picks():
                pe.wait_ge(s_pick, 1)
                for t in range(T):
                    for k in range(3):
                        ins = nc.tensor.transpose(
                            spare_ps[:, t, k * P:(k + 1) * P],
                            pick[:, k, t * PEER_HEADS:(t + 1) * PEER_HEADS, :].rearrange("p a k -> p (a k)"), ident)
                    ins.then_inc(s_pkt, 1)

            def gate_matrix(i, b):
                pe.wait_ge(oh_ready[b], i - (GATE0 - 1))
                if not (isinstance(i, int) and i == GATE0):
                    pe.wait_ge(g_mult[b], i - GATE0)
                for j in range(4):
                    ins = nc.tensor.matmul(spare_ps[:, b, j * P:(j + 1) * P], onehot[:, b, j, 0, :],
                                           onehot[:, b, j, 1, :], start=True, stop=True)
                ins.then_inc(g_made[b], 1)

            turn(0, 0)
            turn(0, 1)

            def body(i, kind):
                for k in range(8):
                    if not (kind == LAST and k >= 6):
                        turn(i, k + 2)
                    score(i, k)
                    if kind == TURN and k == 4:
                        turn_picks()
                    if kind in (GATE_FIRST, GATES) and k in (4, 7):
                        gate_matrix(i, 0 if k == 4 else 1)
            expert_steps(pe, body)

        @block.scalar
        def _(act):
            def finish(i, a, first):
                act.wait_ge(up_used[3], i * 2 + (a + 1))
                if not first:
                    act.wait_ge(h_sum[1 - a], i + a)
                nc.scalar.copy(act_tmp[:, a, :], turn_ps[:, a, S:2 * S]).then_inc(h2_out[a], 1)

            def gelu(i, a, gated):
                act.wait_ge(h_sum[a], i + 1)
                src = act_tmp[:, a, :]
                if gated:
                    nc.scalar.activation(src, src, ACT.Gelu).then_inc(h_gelu[a], 1)
                else:
                    nc.scalar.activation(gates[:, ds(i * 2 + a, 1), :], src.unsqueeze(1), ACT.Gelu
                                         ).then_inc(h_gelu[a], 1)

            def body(i, kind):
                for k in range(8):
                    s = k % 4
                    act.wait_ge(up_turned[s], i * 2 + (k // 4 + 1))
                    wait_used(act, up_used[s], i * 2 + k // 4)
                    nc.scalar.copy(uT_hi[:, s, :, :], tq[:, s, :].rearrange("p (j n) -> p j n", j=4)
                                   ).then_inc(up_hi[s], 1)
                    if k == 2 and kind != FIRST:
                        finish(i - 1, 1, False)
                    if k == 3 and kind != FIRST:
                        gelu(i - 1, 1, kind >= GATES)
                    if k == 6:
                        finish(i, 0, kind == FIRST)
                    if k == 7:
                        gelu(i, 0, kind >= GATE_FIRST)
                    if kind == TURN and k == 0:
                        act.wait_ge(s_ge, 1)
                        nc.scalar.activation(gate_e[:], gate_e[:], ACT.Exp).then_inc(s_gs, 1)
                    if kind == TURN and k == 7:
                        for t in range(T):
                            act.wait_ge(s_pkt, t + 1)
                            nc.scalar.copy(pickT[:, :, t * P:(t + 1) * P], spare_ps[:, t, 0:3 * P].rearrange(
                                "p (a k) -> p a k", a=3)).then_inc(s_pke, 1)
                if kind == LAST:
                    finish(i, 1, False)
                    gelu(i, 1, True)
            expert_steps(act, body)

        @block.vector
        def _(dve):
            def add(i, a):
                dve.wait_ge(h2_out[a], i + 1)
                nc.vector.tensor_tensor(act_tmp[:, a, :], turn_ps[:, a, 0:S], act_tmp[:, a, :], ALU.add
                                        ).then_inc(h_sum[a], 1)

            def gate(i, a):
                dve.wait_ge(h_gelu[a], i + 1)
                g = gates[:, ds(i * 2 + a, 1), :]
                nc.vector.tensor_tensor(g, g, act_tmp[:, a, :].unsqueeze(1), ALU.mult).then_inc(h_gated[a], 1)

            def one_hots(i, b, tokens):
                if 0 in tokens and not (isinstance(i, int) and i == GATE0):
                    dve.wait_ge(g_made[b], i - GATE0)
                for j in tokens:
                    tok = i * 8 + (4 * b + j - 8 * GATE0)
                    nc.vector.tensor_scalar(onehot[:, b, j, 0, :], count_row, pickT[:, 0, ds(tok, 1)], None,
                                            ALU.is_equal)
                    ins = nc.vector.tensor_scalar(onehot[:, b, j, 1, :], count_row, pickT[:, 1, ds(tok, 1)],
                                                  pickT[:, 2, ds(tok, 1)], ALU.is_equal, ALU.mult)
                    if j == 3:
                        ins.then_inc(oh_ready[b], 1)

            def multiply_in(i, b):
                dve.wait_ge(g_made[b], i - (GATE0 - 1))
                g = gates[:, :, ds(i * 8 + (4 * b - 8 * GATE0), 4)].rearrange("p n t -> p t n")
                nc.vector.tensor_tensor(g, g, spare_ps[:, b, :].rearrange("p (t n) -> p t n", t=4), ALU.mult
                                        ).then_inc(g_mult[b], 1)

            def picks(i, k):
                sv, tv, ti = unit_s, top_v, top_i
                flat = cand[:].rearrange("p a b -> p (a b)")
                if k == 0:
                    nc.vector.tensor_copy(unit_s[:].unsqueeze(1), key_scores[:, ds(i, 1), :, :])
                    dve.drain()
                    nc.vector.max(tv[:, 0, 0:8], sv[:, 0, :])
                    nc.vector.max(tv[:, 1, 0:8], sv[:, 1, :])
                    dve.drain()
                    nc.vector.max_index(ti[:, 0, 0:8], tv[:, 0, 0:8], sv[:, 0, :])
                elif k == 1:
                    nc.vector.max_index(ti[:, 1, 0:8], tv[:, 1, 0:8], sv[:, 1, :])
                    dve.drain()
                    nc.vector.match_replace(sv[:, 0, :], tv[:, 0, 0:8], sv[:, 0, :], LOWEST)
                    nc.vector.match_replace(sv[:, 1, :], tv[:, 1, 0:8], sv[:, 1, :], LOWEST)
                    dve.drain()
                    nc.vector.max(tv[:, 0, 8:16], sv[:, 0, :])
                elif k == 2:
                    nc.vector.max(tv[:, 1, 8:16], sv[:, 1, :])
                    dve.drain()
                    nc.vector.max_index(ti[:, 0, 8:16], tv[:, 0, 8:16], sv[:, 0, :])
                    nc.vector.max_index(ti[:, 1, 8:16], tv[:, 1, 8:16], sv[:, 1, :])
                    dve.drain()
                    nc.vector.tensor_copy(top_if[:], top_i[:])
                elif k == 3:
                    nc.vector.tensor_tensor(cand[:], tv[:, 0, :].unsqueeze(2).broadcast_to([P, TOPK, TOPK]),
                                                 tv[:, 1, :].unsqueeze(1).broadcast_to([P, TOPK, TOPK]), ALU.add)
                    dve.drain()
                    nc.vector.max(pick_v[:, 0:8], flat)
                elif k == 4:
                    dve.drain()
                    nc.vector.max_index(pick_pos[:, 0:8], pick_v[:, 0:8], flat)
                    dve.drain()
                    nc.vector.match_replace(flat, pick_v[:, 0:8], flat, LOWEST)
                elif k == 5:
                    dve.drain()
                    nc.vector.max(pick_v[:, 8:16], flat)
                    dve.drain()
                    nc.vector.max_index(pick_pos[:, 8:16], pick_v[:, 8:16], flat)
                elif k == 6:
                    dve.drain()
                    nc.vector.tensor_scalar(pick_ij[:, 0, :], pick_pos[:], 4, None, ALU.logical_shift_right)
                    nc.vector.tensor_scalar(pick_ij[:, 1, :], pick_pos[:], TOPK - 1, None, ALU.bitwise_and)
                    dve.drain()
                    nc.vector.tensor_copy(pick_ijf[:], pick_ij[:])
                    dve.drain()
                    nc.vector.tensor_tensor(
                        pick_eq[:], cst[:, C_IOTA16:C_IOTA16 + TOPK].unsqueeze(1).unsqueeze(1).broadcast_to(
                            [P, 2, TOPK, TOPK]),
                        pick_ijf[:].unsqueeze(3).broadcast_to([P, 2, TOPK, TOPK]), ALU.is_equal)
                elif k == 7:
                    dve.drain()
                    nc.vector.tensor_tensor(pick_eq[:], pick_eq[:], top_if[:].unsqueeze(2).broadcast_to(
                        [P, 2, TOPK, TOPK]), ALU.mult)
                    nc.vector.tensor_copy(pick_sums[:, ds(i, 1), :], pick_v[:].unsqueeze(1))
                    dve.drain()
                    nc.vector.tensor_reduce(pick[:, 0:2, ds(i, 1), :], pick_eq[:].unsqueeze(2), AX_X, ALU.add)
                    dve.drain()

            def softmax(k):
                if k == 0:
                    nc.vector.tensor_tensor(gate_e[:], pick_sums[:], pick_sums[:, :, 0:1].broadcast_to(
                        [P, UNITS, TOPK]), ALU.subtract).then_inc(s_ge, 1)
                if k == 2:
                    dve.wait_ge(s_gs, 1)
                    nc.vector.tensor_reduce(gate_s[:, 0, :], gate_e[:], AX_X, ALU.add).then_inc(s_prep, 1)
                    dve.wait_ge(s_prep, 1)
                    nc.vector.reciprocal(gate_s[:, 1, :], gate_s[:, 0, :]).then_inc(s_prep, 1)
                    dve.wait_ge(s_prep, 2)
                    nc.vector.tensor_tensor(pick[:, 2, :, :], gate_e[:], gate_s[:, 1, :].unsqueeze(2).broadcast_to(
                        [P, UNITS, TOPK]), ALU.mult).then_inc(s_pick, 1)

            def body(i, kind):
                for k in range(8):
                    s = k % 4
                    dve.wait_ge(up_hi[s], i * 2 + (k // 4 + 1))
                    nc.vector.tensor_tensor(uT_lo[:, s, :, :], tq[:, s, :].rearrange("p (j n) -> p j n", j=4),
                                            f(uT_hi[:, s, :, :]), ALU.subtract).then_inc(up_lo[s], 1)
                    if kind in (FIRST, PICKS):
                        picks(i, k)
                    if kind == TURN:
                        softmax(k)
                    if kind == GATE_FIRST and k == 0:
                        dve.wait_ge(s_pke, T)
                    if kind in (GATE_FIRST, GATES) and k < 6:
                        one_hots(i, k // 3, ((0,), (1, 2), (3,))[k % 3])
                    if k == 1 and kind in (GATES, GATE_AFTER):
                        dve.wait_ge(g_mult[0], i - GATE0)
                        multiply_in(i - 1, 1)
                    if k == 2 and kind != FIRST:
                        add(i - 1, 1)
                    if k == 3 and kind >= GATES:
                        if kind <= GATE_AFTER:
                            dve.wait_ge(g_mult[1], i - GATE0)
                        gate(i - 1, 1)
                    if k == 6:
                        add(i, 0)
                    if k == 7 and kind >= GATE_FIRST:
                        if kind == GATE_FIRST:
                            dve.wait_ge(s_ones, 2)
                        if kind in (GATES, GATE_AFTER):
                            dve.wait_ge(g_mult[1], i - GATE0)
                        gate(i, 0)
                        if kind == GATE_FIRST:
                            dve.wait_ge(h_gelu[1], GATE0)
                        if kind <= GATES:
                            dve.wait_ge(h_gated[0], i - (GATE0 - 1))
                            multiply_in(i, 0)
                if kind == LAST:
                    add(i, 1)
                    gate(i, 1)
            expert_steps(dve, body)
    if blocks < 8:
        return

    s_vhi, s_vlo, s_ahi, s_alo, s_vused = ([sem(f"{n}{s}") for s in range(2)] for n in (
        "v_hi", "v_lo", "a_hi", "a_lo", "v_used"))
    s_h1in, s_gb8, s_c8, s_var8, s_root8, s_n8, s_res, s_done = (sem("ln2_" + n) for n in (
        "h1_in", "gb_in", "chain", "var", "root", "normed", "residual", "stored"))

    def y_bank(t, q):
        if q < 2:
            return stream_acc[:, q, t, :]
        return (turn_ps if q == 2 else spare_ps)[:, t, :]

    STEPS = N_KEYS // 2

    def steps_of(eng, body):
        body(0, True, False)
        with eng.Fori(1, STEPS - 1) as i:
            body(i, False, False)
        body(STEPS - 1, False, True)

    with nc.Block() as block:
        @block.sync
        def _(sp):
            sp.dma_start(h1[:], spill_v).then_inc(s_h1in, 16)

            def body(i, first, last):
                for a in range(2):
                    sp.wait_ge(s_vlo[a], i + 1)
                    if not last:
                        sp.dma_start(e_raw[:, a, :].unsqueeze(1), v_rows[:, ds(i * 2 + (2 + a), 1), :]
                                     ).then_inc(v_loaded[a], 16)
            steps_of(sp, body)
            for j, v in enumerate((ln2_g, ln2_b)):
                sp.dma_start(ln2_gb[:, j, :], broadcast_rows(v)).then_inc(s_gb8, 16)
            for t in range(T):
                sp.wait_ge(s_n8, t + 1)
                sp.dma_start(out_v[:, t, :], final[:, t, :]).then_inc(s_done, 16)
            sp.wait_ge(s_done, 32)

        @block.gpsimd
        def _(pool):
            inverse_root(pool, s_var8, s_root8)

        @block.scalar
        def _(act):
            def body(i, first, last):
                for a in range(2):
                    act.wait_ge(v_loaded[a], i * 16 + 16)
                    wait_used(act, s_vused[a], i)
                    nc.scalar.copy(a_hi[:, a, :].unsqueeze(1), gates[:, ds(i * 2 + a, 1), :]).then_inc(s_ahi[a], 1)
                    nc.scalar.copy(v_hi[:, a, :], e_raw[:, a, :]).then_inc(s_vhi[a], 1)
            steps_of(act, body)

        @block.vector
        def _(dve):
            def body(i, first, last):
                for a in range(2):
                    dve.wait_ge(s_ahi[a], i + 1)
                    nc.vector.tensor_tensor(a_lo[:, a, :].unsqueeze(1), gates[:, ds(i * 2 + a, 1), :],
                                            f(a_hi[:, a, :]).unsqueeze(1), ALU.subtract).then_inc(s_alo[a], 1)
                    dve.wait_ge(s_vhi[a], i + 1)
                    nc.vector.tensor_tensor(v_lo[:, a, :], e_raw[:, a, :], f(v_hi[:, a, :]), ALU.subtract
                                            ).then_inc(s_vlo[a], 1)
            steps_of(dve, body)
            chain = Chain(s_c8)
            dve.wait_ge(s_h1in, 16)
            dve.wait_ge(s_vused[1], STEPS)
            for t in range(T):
                for q in range(4):
                    n = chain.step(nc.vector.scalar_tensor_tensor(
                        final[:, t, q * 512:(q + 1) * 512], h1[:, t, q * 512:(q + 1) * 512], ALPHA, y_bank(t, q),
                        ALU.mult, ALU.add))
            dve.wait_ge(chain.sem, n)
            norm_stats(dve, chain, final, s_var8)
            dve.wait_ge(s_gb8, 32)
            norm_apply(dve, chain, final, ln2_gb, s_root8, s_n8)

        @block.tensor
        def _(pe):
            def body(i, first, last):
                for a in range(2):
                    pe.wait_ge(s_vlo[a], i + 1)
                    pe.wait_ge(s_alo[a], i + 1)
                    for t in range(T):
                        hi, lo = a_hi[:, a, t * P:(t + 1) * P], a_lo[:, a, t * P:(t + 1) * P]
                        start, stop = first and a == 0, last and a == 1
                        for q in range(4):
                            nc.tensor.matmul(y_bank(t, q), hi, v_hi[:, a, q * 512:(q + 1) * 512],
                                             start=start, stop=False)
                        for q in range(4):
                            nc.tensor.matmul(y_bank(t, q), hi, v_lo[:, a, q * 512:(q + 1) * 512],
                                             start=False, stop=False)
                        for q in range(4):
                            ins = nc.tensor.matmul(y_bank(t, q), lo, v_hi[:, a, q * 512:(q + 1) * 512],
                                                   start=False, stop=stop)
                    ins.then_inc(s_vused[a], 1)
            steps_of(pe, body)


_INS = ["x", "ln_emb_g", "ln_emb_b", "w_in", "dil_norm_g", "lambda_q1", "lambda_k1", "lambda_q2", "lambda_k2",
        "subln_g", "w_out", "ln1_g", "ln1_b", "peer_w_query", "peer_sub_keys", "peer_u", "peer_v", "ln2_g", "ln2_b"]
_LAYERED = {"w_in", "w_out", "peer_w_query", "peer_sub_keys", "peer_u", "peer_v"}


def kernel(**inputs):
    import concourse.bacc as _bacc
    from concourse.bass_utils import run_bass_kernel_spmd as _run

    nc = _bacc.Bacc("TRN2", target_bir_lowering=False, num_devices=1)
    arrays, args = {}, []
    for name in _INS:
        a = np.ascontiguousarray(inputs[name])
        if name in _LAYERED:
            a = a[0]
        arrays[f"in_{name}_dram"] = a
        args.append(nc.dram_tensor(f"in_{name}_dram", a.shape, F32, kind="ExternalInput").ap())
    arrays["constants_dram"] = shape_constants()
    args.append(nc.dram_tensor("constants_dram", (P, C_END), F32, kind="ExternalInput").ap())
    args.append(nc.dram_tensor("h1_spill", (S, D), F32, kind="Internal").ap())
    args.append(nc.dram_tensor("out_0_dram", (1, S, D), F32, kind="ExternalOutput").ap())
    encoder_layer(nc, *args)
    r = _run(nc, [arrays], core_ids=[0])
    return r.results[0]["out_0_dram"]
```

```python
import math

import numpy as np

import concourse.bass as bass
from concourse import mybir
from concourse.alu_op_type import AluOpType as ALU

F32 = mybir.dt.float32
F32R = mybir.dt.float32r
BF16 = mybir.dt.bfloat16
U32 = mybir.dt.uint32
ACT = mybir.ActivationFunctionType
AX_X = mybir.AxisListType.X
ds = bass.ds

P = 128
D = 2048
S = 256
T = S // P
KT = D // P
DH = 128
DIL_HEADS = 12
DIFF_HEADS = 4
DIFF_DQ = 64
IN_WIDTH = 3 * DIL_HEADS * DH + 3 * DIFF_HEADS * 2 * DIFF_DQ
COL_QD = 2 * DIL_HEADS * DH
COL_KD = COL_QD + DIFF_HEADS * DH
COL_V = COL_KD + DIFF_HEADS * DH
HEADS = DIL_HEADS + DIFF_HEADS
QK_GROUPS = COL_V // 512
ROPE_THETA = 500000.0
HALF_DIL = DH // 4 // 2
HALF_DIFF = DIFF_DQ // 4 // 2
DIL_CONFIGS = ((128, 1), (512, 4), (2048, 16))
PEER_HEADS = 8
N_KEYS = 128
TOPK = 16
LN_EPS = 1e-5
ALPHA = 2.0 ** 0.25
LAM_INIT = 0.8 - 0.6 * math.exp(-0.0)
LOWEST = -3.0e38
GROUP = 512
CHUNK_KT = 4
CHUNKS = KT // CHUNK_KT

C_ID = 0
C_IOTA = C_ID + P
C_IOTA16 = C_IOTA + P
C_KEPT = C_IOTA16 + TOPK
C_MASK = C_KEPT
C_ROPE = C_MASK + T * S
ROPE_W = 2 * HALF_DIL + 2 * HALF_DIFF
C_END = C_ROPE + T * ROPE_W


def shape_constants():
    c = np.zeros((P, C_END), np.float32)
    c[:, C_ID:C_ID + P] = np.eye(P, dtype=np.float32)
    c[:, C_IOTA:C_IOTA + P] = np.arange(P, dtype=np.float32)
    c[:, C_IOTA16:C_IOTA16 + TOPK] = np.arange(TOPK, dtype=np.float32)
    q, k = np.arange(S)[:, None], np.arange(S)[None, :]
    count = np.zeros((S, S), np.int64)
    for window, dilation in DIL_CONFIGS:
        near = np.abs(q // dilation - k // dilation) <= window // (2 * dilation)
        count += near & (q % dilation == k % dilation)
    log_count = np.where(count > 0, np.log(np.maximum(count, 1)) * DH ** 0.5, -1e30)
    c[:, C_MASK:C_MASK + T * S] = log_count.reshape(T, P, S).transpose(1, 0, 2).reshape(P, T * S)
    rope = []
    for half in (HALF_DIL, HALF_DIFF):
        exponent = np.arange(0, 2 * half, 2, dtype=np.float32) / np.float32(2 * half)
        inv = np.float32(1.0) / np.power(np.float32(ROPE_THETA), exponent)
        angle = np.arange(S, dtype=np.float32)[:, None] * inv[None, :]
        rope += [np.cos(angle), np.sin(angle)]
    rope = np.concatenate(rope, axis=1).astype(np.float32)
    c[:, C_ROPE:] = rope.reshape(T, P, ROPE_W).transpose(1, 0, 2).reshape(P, T * ROPE_W)
    return c


class Chain:

    def __init__(self, sem):
        self.sem, self.n = sem, 0

    def step(self, ins):
        ins.then_inc(self.sem, 1)
        self.n += 1
        return self.n


def encoder_layer(nc, x, ln_emb_g, ln_emb_b, w_in, dil_norm_g, lambda_q1, lambda_k1, lambda_q2, lambda_k2,
                  subln_g, w_out, ln1_g, ln1_b, w_query, sub_keys, peer_u, peer_v, ln2_g, ln2_b,
                  constants, h1_spill, out):
    x_v = x.rearrange("o (t p) d -> p (o t) d", p=P)
    out_v = out.rearrange("o (t p) d -> p (o t) d", p=P)
    spill_v = h1_spill.rearrange("(t p) d -> p t d", p=P)

    BASE = 16512
    at = [BASE]

    def small(name, shape, dt=F32):
        size = 4 * int(np.prod(shape[1:]))
        size += -size % 32
        t = nc.alloc_sbuf_tensor_at(name, shape, dt, offset=at[0])
        at[0] += size
        return t

    def place(name, shape, dt, offset):
        return nc.alloc_sbuf_tensor_at(name, shape, dt, offset=offset)

    cst = small("cst", [P, C_KEPT])
    pickT = small("pickT", [P, 4, S], F32R)
    lams = small("lams", [P, 8])
    stats = small("stats", [P, T, 4, 6])
    meanvar = small("meanvar", [P, T, 2])
    rstd = small("rstd", [P, T, 2])
    mhalf = small("mhalf", [P, 32])
    pick_v = small("pick_v", [P, 16])
    ONEHOT0 = at[0]
    att_cst = small("att_cst", [P, C_END - C_KEPT])
    lamv = small("lamv", [P, 4, DIFF_DQ])
    g_col = small("g_col", [P, 4])
    row_max = small("row_max", [P, DIFF_HEADS, 4])
    neg_max = small("neg_max", [P, 16, 4])
    den = small("den", [P, 16, 4])
    rden = small("rden", [P, 16, 4])
    lam_rden = small("lam_rden", [P, 4, 2])
    sumsq = small("sumsq", [P, 16, T])
    rms = small("rms", [P, 16, T])
    square = small("square", [P, P])
    KB = 1024
    HT0 = ONEHOT0 + 8 * KB
    assert at[0] <= HT0, at[0] - HT0
    ident = cst[:, C_ID:C_ID + P]
    R0 = HT0 + 32 * KB
    hT = place("hT", [P, KT, 2 * S], F32R, HT0)
    h = place("h", [P, T, D], F32, R0)
    w_raw = place("w_raw", [P, 4, CHUNK_KT, GROUP], F32, R0 + 16 * KB)
    w_hi = place("w_hi", [P, 2, CHUNK_KT, GROUP], F32R, R0 + 48 * KB)
    w_lo = place("w_lo", [P, 2, CHUNK_KT, GROUP], F32R, R0 + 64 * KB)
    ln_gb = place("ln_gb", [P, 2, D], F32, R0 + 80 * KB)
    g_row = place("g_row", [1, D], F32, R0 + 96 * KB)
    one_row = place("one_row", [1, P], F32, R0 + 112 * KB)
    proj = place("proj", [P, T, IN_WIDTH], F32, R0 + 96 * KB)
    qkT_half = [place("qkT_a", [P, 8, 2, S], F32, R0 + 80 * KB), place("qkT_b", [P, 8, 2, S], F32, R0 + 144 * KB)]
    mixed = place("mixed", [P, T, D], F32, HT0)
    scores = place("scores", [P, 2, T, S], F32, HT0 + 16 * KB)
    probs = place("probs", [P, 2, 2, T, S], F32, HT0 + 20 * KB)
    probsT = place("probsT", [P, 2, T, S], F32, HT0 + 28 * KB)
    rope_tmp = place("rope_tmp", [P, 2, 256], F32, R0 + 160 * KB)
    mixT = place("mixT", [P, KT, 2 * S], F32R, R0 + 48 * KB)
    wo_hi = place("wo_hi", [P, 2, CHUNK_KT, GROUP], F32R, R0 + 96 * KB)
    wo_lo = place("wo_lo", [P, 2, CHUNK_KT, GROUP], F32R, R0 + 120 * KB)
    query = place("query", [P, T, D], F32, R0 + 96 * KB)
    queryT = place("queryT", [P, KT, S], F32, R0 + 112 * KB)
    keys = place("keys", [P, 2 * PEER_HEADS, P], F32, R0 + 144 * KB)
    keysT = place("keysT", [P, 2 * PEER_HEADS, N_KEYS], F32, R0 + 152 * KB)
    UNITS = T * PEER_HEADS
    key_scores = place("key_scores", [P, UNITS, 2, N_KEYS], F32, R0 + 96 * KB)
    TK = R0 + 112 * KB
    unit_s = place("unit_s", [P, 2, N_KEYS], F32, TK)
    top_v = place("top_v", [P, 2, TOPK], F32, TK + 1024)
    top_i = place("top_i", [P, 2, TOPK], U32, TK + 1152)
    top_if = place("top_if", [P, 2, TOPK], F32, TK + 1280)
    cand = place("cand", [P, TOPK, TOPK], F32, TK + 2048)
    pick_eq = place("pick_eq", [P, 2, TOPK, TOPK], F32, TK + 3072)
    pick_pos = place("pick_pos", [P, TOPK], U32, TK + 5120)
    pick_ij = place("pick_ij", [P, 2, TOPK], U32, TK + 5184)
    pick_ijf = place("pick_ijf", [P, 2, TOPK], F32, TK + 5312)
    pick = place("pick", [P, 3, UNITS, TOPK], F32, TK + 6144)
    pick_sums = place("pick_sums", [P, UNITS, TOPK], F32, TK + 9216)
    gate_e = place("gate_e", [P, UNITS, TOPK], F32, TK + 10240)
    gate_s = place("gate_s", [P, 2, UNITS], F32, TK + 11264)
    gates = place("gates", [P, N_KEYS, S], F32, R0)
    oh_first = place("oh_first", [P, 4, P], F32R, ONEHOT0)
    oh_gate = place("oh_gate", [P, 4, 2, P], F32R, ONEHOT0 + 2 * KB)
    oh_second = place("oh_second", [P, 4, P], BF16, ONEHOT0 + 6 * KB)
    gate_sum = place("gate_sum", [P, 2, P], F32, ONEHOT0 + 7 * KB)
    e_raw = place("e_raw", [P, 2, D], F32, R0 + 128 * KB)
    uT_hi = place("uT_hi", [P, 4, 4, P], F32R, R0 + 144 * KB)
    uT_lo = place("uT_lo", [P, 4, 4, P], F32R, R0 + 152 * KB)
    act_tmp = place("act_tmp", [P, 2, S], F32, R0 + 160 * KB)
    v_hi = place("v_hi", [P, 2, D], F32R, HT0)
    v_lo = place("v_lo", [P, 2, D], F32R, HT0 + 16 * KB)
    v_raw = place("v_raw", [P, 4, D], F32, R0 + 128 * KB)
    a_hi = place("a_hi", [P, 2, S], F32R, R0 + 160 * KB)
    a_lo = place("a_lo", [P, 2, S], F32R, ONEHOT0)
    final = place("final", [P, T, D], F32, R0)
    ln2_gb = place("ln2_gb", [P, 2, D], F32, R0 + 16 * KB)
    h1 = place("h1", [P, T, D], F32, R0 + 32 * KB)

    sem = nc.alloc_semaphore
    chain = Chain(sem("vector_chain"))

    def wait_used(eng, s, n):
        if not (isinstance(n, int) and n == 0):
            eng.wait_ge(s, n)

    def broadcast_rows(v):
        return v.rearrange("o d -> (o d)").partition_broadcast(P)

    def f(ap):
        return ap.bitcast(F32)

    def quarter_stats(chain, src, q):
        for t in range(T):
            n = chain.step(nc.vector.bn_stats(stats[:, t, q, :], src[:, t, q * 512:(q + 1) * 512]))
        return n

    def norm_variance(dve, chain, n, ready):
        dve.wait_ge(chain.sem, n)
        for t in range(T):
            n = chain.step(nc.vector.bn_aggr(meanvar[:, t, :], stats[:, t, :, :]))
        dve.wait_ge(chain.sem, n)
        nc.vector.tensor_scalar(rstd[:, :, 0], meanvar[:, :, 1], LN_EPS, None, ALU.add).then_inc(ready, 1)

    def inverse_root(pool, ready, done):
        pool.wait_ge(ready, 1)
        nc.gpsimd.tensor_tensor(rstd[:, :, 1], rstd[:, :, 0], mhalf[:, 0:T], ALU.pow).then_inc(done, 1)

    def norm_quarter(dve, chain, buf, gb, q, before_bias, normed):
        c = slice(q * 512, (q + 1) * 512)
        for t in range(T):
            n = chain.step(nc.vector.scalar_tensor_tensor(buf[:, t, c], buf[:, t, c], meanvar[:, t, 0:1],
                                                          gb[:, 0, c], ALU.subtract, ALU.mult))
        dve.wait_ge(chain.sem, n)
        if q == 0:
            for s, n in before_bias:
                dve.wait_ge(s, n)
        for t in range(T):
            nc.vector.scalar_tensor_tensor(buf[:, t, c], buf[:, t, c], rstd[:, t, 1:2], gb[:, 1, c],
                                           ALU.mult, ALU.add).then_inc(normed, 1)

    def turn_bank(j):
        return (turn_ps if j % 4 < 2 else spare_ps)[:, j % 2, :]

    def turn_pe(pe, src, normed, sem_turned, sem_lo):
        for j in range(KT // 2):
            if j % 2 == 0:
                pe.wait_ge(normed, T * (j // 2 + 1))
            if j >= 4:
                pe.wait_ge(sem_lo, j - 3)
            for t in range(T):
                for k in range(2):
                    kt = 2 * j + k
                    last = nc.tensor.transpose(turn_bank(j)[:, k * S + t * P:k * S + (t + 1) * P],
                                               src[:, t, kt * P:(kt + 1) * P], ident)
            last.then_inc(sem_turned, 1)

    def turn_act(act, dst, sem_turned, sem_hi, after={}):
        for j in range(KT // 2):
            act.wait_ge(sem_turned, j + 1)
            nc.scalar.copy(dst[:, 2 * j:2 * j + 2, 0:S], turn_bank(j).rearrange("p (k s) -> p k s", k=2)
                           ).then_inc(sem_hi, 1)
            if j in after:
                after[j]()

    def turn_dve(dve, dst, j, sem_hi, sem_lo):
        dve.wait_ge(sem_hi, j + 1)
        nc.vector.tensor_tensor(dst[:, 2 * j:2 * j + 2, S:2 * S], turn_bank(j).rearrange("p (k s) -> p k s", k=2),
                                f(dst[:, 2 * j:2 * j + 2, 0:S]), ALU.subtract).then_inc(sem_lo, 1)

    def norm_and_turn_dve(dve, chain, buf, gb, dst, before_bias, normed, sem_hi, sem_lo):
        for q in range(4):
            norm_quarter(dve, chain, buf, gb, q, before_bias, normed)
            if q >= 1:
                for j in (2 * q - 2, 2 * q - 1):
                    turn_dve(dve, dst, j, sem_hi, sem_lo)
        for j in (6, 7):
            turn_dve(dve, dst, j, sem_hi, sem_lo)

    class Stream:
        def __init__(self, name, w, groups, acc, w_hi, w_lo):
            self.w = w.rearrange("(c k p) (g n) -> p c k g n", k=CHUNK_KT, p=P, n=GROUP)
            self.steps, self.acc, self.w_hi, self.w_lo = groups // 2, acc, w_hi, w_lo
            self.loaded = [sem(f"{name}_loaded{c}") for c in range(CHUNKS)]
            self.hi = [sem(f"{name}_hi{s}") for s in range(2)]
            self.lo = [sem(f"{name}_lo{s}") for s in range(2)]
            self.used = [sem(f"{name}_used{s}") for s in range(2)]
            self.read_out = [sem(f"{name}_read_out{u}") for u in range(2)]

        def load(self, sp, g, c):
            sp.dma_start(w_raw[:, c, :, :].unsqueeze(2), self.w[:, c, :, ds(g, 1), :]).then_inc(self.loaded[c], 16)

        def prefetch(self, sp):
            for c in range(CHUNKS):
                self.load(sp, 0, c)

        def steps_of(self, eng, body):
            body(0, True, self.steps == 1)
            if self.steps > 2:
                with eng.Fori(1, self.steps - 1) as i:
                    body(i, False, False)
            if self.steps > 1:
                body(self.steps - 1, False, True)

        def sp(self, sp):
            def body(i, first, last):
                for u in range(1 if last else 2):
                    for c in range(CHUNKS):
                        sp.wait_ge(self.lo[c % 2], i * 4 + (2 * u + c // 2 + 1))
                        self.load(sp, i * 2 + (u + 1), c)
            self.steps_of(sp, body)

        def hi_part(self, c):
            return nc.scalar.copy(self.w_hi[:, c % 2, :, :], w_raw[:, c, :, :]).then_inc(self.hi[c % 2], 1)

        def lo_part(self, c, maker=nc.vector):
            s = c % 2
            return maker.tensor_tensor(self.w_lo[:, s, :, :], w_raw[:, c, :, :], f(self.w_hi[:, s, :, :]),
                                       ALU.subtract).then_inc(self.lo[s], 1)

        def presplit_act(self, act, c):
            act.wait_ge(self.loaded[c], 16)
            self.hi_part(c)

        def presplit_piece_act(self, act, c, k):
            if k == 0:
                act.wait_ge(self.loaded[c], 16)
            ins = nc.scalar.copy(self.w_hi[:, c, k, :], w_raw[:, c, k, :])
            if k == CHUNK_KT - 1:
                ins.then_inc(self.hi[c], 1)

        def presplit_piece_lo(self, eng, maker, c, k):
            if k == 0:
                eng.wait_ge(self.hi[c], 1)
            ins = maker.tensor_tensor(self.w_lo[:, c, k, :], w_raw[:, c, k, :], f(self.w_hi[:, c, k, :]), ALU.subtract)
            if k == CHUNK_KT - 1:
                ins.then_inc(self.lo[c], 1)

        def presplit_lo(self, eng, maker, c):
            eng.wait_ge(self.hi[c], 1)
            self.lo_part(c, maker)

        def split_act(self, act, after_chunk):
            def body(i, first, last):
                for u in range(2):
                    for c in range(CHUNKS):
                        if not (first and u == 0 and c < 2):
                            act.wait_ge(self.loaded[c], i * 32 + 16 * (u + 1))
                            act.wait_ge(self.used[c % 2], i * 4 + (2 * u + c // 2))
                            self.hi_part(c)
                        after_chunk(i, first, last, u, c)
            self.steps_of(act, body)

        def split_dve(self, dve, after_chunk):
            def body(i, first, last):
                for u in range(2):
                    for c in range(CHUNKS):
                        if not (first and u == 0 and c < 2):
                            dve.wait_ge(self.hi[c % 2], i * 4 + (2 * u + c // 2 + 1))
                            self.lo_part(c)
                        after_chunk(i, first, last, u, c)
            self.steps_of(dve, body)

        def read_after(self, eng, read):
            def after_chunk(i, first, last, u, c):
                if c == 1 and not (first and u == 0):
                    ip, up = (i, 0) if u == 1 else (i - 1, 1)
                    eng.wait_ge(self.used[1], i * 4 + 2 * u)
                    read(ip * 2 + up, self.acc[:, up, :, :]).then_inc(self.read_out[up], 1)
                if last and u == 1 and c == CHUNKS - 1:
                    eng.wait_ge(self.used[1], i * 4 + 4)
                    read(i * 2 + 1, self.acc[:, 1, :, :]).then_inc(self.read_out[1], 1)
            return after_chunk

        def pe(self, pe, actT, after_chunk=lambda i, first, last, u, c: None):
            def body(i, first, last):
                for u in range(2):
                    for c in range(CHUNKS):
                        s = c % 2
                        pe.wait_ge(self.lo[s], i * 4 + (2 * u + c // 2 + 1))
                        if c == 0 and not first:
                            pe.wait_ge(self.read_out[u], i)
                        for k in range(CHUNK_KT):
                            kt = c * CHUNK_KT + k
                            for t in range(T):
                                hi, lo = (actT[:, kt, b + t * P:b + (t + 1) * P] for b in (0, S))
                                o = self.acc[:, u, t, :]
                                nc.tensor.matmul(o, hi, self.w_hi[:, s, k, :], start=(kt == 0), stop=False)
                                nc.tensor.matmul(o, hi, self.w_lo[:, s, k, :], start=False, stop=False)
                                mm = nc.tensor.matmul(o, lo, self.w_hi[:, s, k, :], start=False,
                                                      stop=(kt == KT - 1))
                        mm.then_inc(self.used[s], 1)
                        after_chunk(i, first, last, u, c)
            self.steps_of(pe, body)

    stream_acc = nc.alloc_psum_tensor("stream_acc", [P, 2, T, GROUP], F32)
    turn_ps = nc.alloc_psum_tensor("turn_ps", [P, 2, 512], F32)
    spare_ps = nc.alloc_psum_tensor("spare_ps", [P, 2, 512], F32)
    in_stream = Stream("w_in", w_in, IN_WIDTH // GROUP, stream_acc, w_hi, w_lo)
    out_stream = Stream("w_out", w_out, D // GROUP, stream_acc, wo_hi, wo_lo)
    query_stream = Stream("w_query", w_query, D // GROUP, stream_acc, w_hi, w_lo)

    s_const, s_lng, s_lamv, s_gcol = (sem(n) for n in ("const_in", "ln_emb_in", "lambda_in", "gain_in"))
    s_x = [sem(f"x_in{q}") for q in range(4)]
    s_attc = sem("attention_const_in")
    s_pool = sem("fills")
    s_var1, s_root1, s_n1 = sem("embed_var"), sem("embed_root"), sem("embed_normed")
    s_t1, s_h1, s_l1 = sem("embed_turned"), sem("embed_hi"), sem("embed_lo")
    s_lam, s_lame = sem("lambda_sums"), sem("lambda_exps")
    s_gm, s_g1 = sem("embed_gain_spread"), sem("embed_gain")
    s_lnb = sem("ln_emb_bias_in")
    with nc.Block() as block:
        @block.sync
        def _(sp):
            sp.dma_start(g_row[:], ln_emb_g.rearrange("(o d) -> o d", o=1)).then_inc(s_lng, 16)
            for q in range(4):
                c = slice(q * 512, (q + 1) * 512)
                sp.dma_start(h[:, :, c], x_v[:, :, c]).then_inc(s_x[q], 16)
            sp.dma_start(ln_gb[:, 1, :], ln_emb_b.partition_broadcast(P)).then_inc(s_lnb, 16)
            sp.dma_start(cst[:], constants[:, 0:C_KEPT]).then_inc(s_const, 16)
            in_stream.prefetch(sp)
            for j, v in enumerate((lambda_q1, lambda_k1, lambda_q2, lambda_k2)):
                sp.dma_start(lamv[:, j, :], broadcast_rows(v)).then_inc(s_lamv, 16)
            for j, v in enumerate((dil_norm_g, subln_g)):
                sp.dma_start(g_col[:, j:j + 1], v.rearrange("o d -> d o")).then_inc(s_gcol, 16)
            sp.dma_start(att_cst[:], constants[:, C_KEPT:C_END]).then_inc(s_attc, 16)

        @block.gpsimd
        def _(pool):
            nc.gpsimd.memset(one_row[:], 1.0).then_inc(s_pool, 1)
            nc.gpsimd.memset(mhalf[:], -0.5).then_inc(s_pool, 1)
            pool.wait_ge(s_pool, 2)
            inverse_root(pool, s_var1, s_root1)
            in_stream.presplit_lo(pool, nc.gpsimd, 0)
            in_stream.presplit_lo(pool, nc.gpsimd, 1)

        @block.vector
        def _(dve):
            for q in range(4):
                dve.wait_ge(s_x[q], 16)
                n = quarter_stats(chain, h, q)
            norm_variance(dve, chain, n, s_var1)
            dve.wait_ge(s_g1, 4)
            norm_and_turn_dve(dve, chain, h, ln_gb, hT, [(s_root1, 1), (s_lnb, 16)], s_n1, s_h1, s_l1)
            dve.wait_ge(s_lamv, 64)
            for m in range(2):
                n = chain.step(nc.vector.tensor_tensor(lamv[:, 2 * m, :], lamv[:, 2 * m, :],
                                                       lamv[:, 2 * m + 1, :], ALU.mult))
                dve.wait_ge(chain.sem, n)
                nc.vector.tensor_reduce(lams[:, m:m + 1], lamv[:, 2 * m, :], AX_X, ALU.add).then_inc(s_lam, 1)
            dve.wait_ge(s_gcol, 32)
            chain.step(nc.vector.tensor_scalar(g_col[:, 1:2], g_col[:, 1:2], 1.0 - LAM_INIT, None, ALU.mult))

        @block.scalar
        def _(act):
            for q in range(4):
                act.wait_ge(s_gm, q + 1)
                nc.scalar.copy(ln_gb[:, 0, q * 512:(q + 1) * 512], stream_acc[:, q // 2, q % 2, :]).then_inc(s_g1, 1)
            turn_act(act, hT, s_t1, s_h1, {1: lambda: in_stream.presplit_act(act, 0),
                                           3: lambda: in_stream.presplit_act(act, 1)})

        @block.tensor
        def _(pe):
            pe.wait_ge(s_pool, 1)
            pe.wait_ge(s_lng, 16)
            for q in range(4):
                nc.tensor.matmul(stream_acc[:, q // 2, q % 2, :], one_row[:], g_row[:, q * 512:(q + 1) * 512],
                                 start=True, stop=True).then_inc(s_gm, 1)
            pe.wait_ge(s_const, 16)
            turn_pe(pe, h, s_n1, s_t1, s_l1)

    s_rope, s_qt, s_qe = sem("rope_done"), sem("qk_turned"), sem("qk_copied")
    with nc.Block() as block:
        @block.sync
        def _(sp):
            in_stream.sp(sp)

        def head_set(u, c):
            return {(0, 3): 0, (1, 0): 1, (1, 1): 2, (1, 2): 3}.get((u, c))

        @block.scalar
        def _(act):
            read = in_stream.read_after(act, lambda g, acc: nc.scalar.copy(proj[:, :, ds(g * GROUP, GROUP)], acc))

            def copy_heads(k):
                for hd in range(4 * k, 4 * k + 4):
                    act.wait_ge(s_qt, hd + 1)
                    nc.scalar.copy(qkT_half[hd // 8][:, hd % 8, :, :],
                                   turn_bank(hd).rearrange("p (a s) -> p a s", a=2)).then_inc(s_qe, 1)

            def after_chunk(i, first, last, u, c):
                if last and u == 1 and c >= 1:
                    copy_heads(c - 1)
                if last and u == 1 and c == 3:
                    copy_heads(3)
                read(i, first, last, u, c)
            act.wait_ge(s_lam, 2)
            nc.scalar.activation(lams[:, 2:4], lams[:, 0:2], ACT.Exp).then_inc(s_lame, 1)
            in_stream.split_act(act, after_chunk)

        @block.vector
        def _(dve):

            def rope(t, col, heads, width, half, tab):
                v = proj[:, t, col:col + heads * width].rearrange("p (a w) -> p a w", w=width)
                x1, x2 = v[:, :, 0:half], v[:, :, half:2 * half]
                base = C_ROPE - C_KEPT + t * ROPE_W + tab
                cos = att_cst[:, base:base + half].unsqueeze(1).broadcast_to([P, heads, half])
                sin = att_cst[:, base + half:base + 2 * half].unsqueeze(1).broadcast_to([P, heads, half])
                x1_sin, x2_sin = (rope_tmp[:, j, 0:heads * half].rearrange("p (a w) -> p a w", w=half)
                                  for j in range(2))
                chain.step(nc.vector.tensor_tensor(x1_sin, x1, sin, ALU.mult))
                n = chain.step(nc.vector.tensor_tensor(x2_sin, x2, sin, ALU.mult))
                dve.wait_ge(chain.sem, n)
                chain.step(nc.vector.tensor_tensor(x1, x1, cos, ALU.mult))
                n = chain.step(nc.vector.tensor_tensor(x2, x2, cos, ALU.mult))
                dve.wait_ge(chain.sem, n)
                chain.step(nc.vector.tensor_tensor(x1, x1, x2_sin, ALU.subtract))
                n = chain.step(nc.vector.tensor_tensor(x2, x2, x1_sin, ALU.add))
                dve.wait_ge(chain.sem, n)

            def after_chunk(i, first, last, u, c):
                if first and u == 0 and c == 0:
                    dve.wait_ge(s_lame, 1)
                    n = chain.step(nc.vector.tensor_tensor(lams[:, 4:5], lams[:, 3:4], lams[:, 2:3], ALU.subtract))
                    dve.wait_ge(chain.sem, n)
                    chain.step(nc.vector.tensor_scalar(lams[:, 5:6], lams[:, 4:5], LAM_INIT, None, ALU.subtract))
                if not (last and u == 0 and c < 3):
                    return
                if c == 0:
                    dve.wait_ge(s_attc, 16)
                    for r in in_stream.read_out:
                        dve.wait_ge(r, QK_GROUPS // 2)
                if c < 2:
                    for part in range(2):
                        rope(c, part * DIL_HEADS * DH, DIL_HEADS, DH, HALF_DIL, 0)
                else:
                    for t in range(T):
                        rope(t, COL_QD, 4 * DIFF_HEADS, DIFF_DQ, HALF_DIFF, 2 * HALF_DIL)
                    nc.vector.memset(lams[:, 6:7], 0.0).then_inc(s_rope, 1)
            in_stream.split_dve(dve, after_chunk)

        @block.tensor
        def _(pe):
            def after_chunk(i, first, last, u, c):
                k = head_set(u, c) if last else None
                if k is None:
                    return
                if k == 0:
                    pe.wait_ge(s_rope, 1)
                for hd in range(4 * k, 4 * k + 4):
                    if hd >= 4:
                        pe.wait_ge(s_qe, hd - 3)
                    q = hd * DH if hd < DIL_HEADS else COL_QD + (hd - DIL_HEADS) * DH
                    kk = (DIL_HEADS + hd) * DH if hd < DIL_HEADS else COL_KD + (hd - DIL_HEADS) * DH
                    for a, col in enumerate((q, kk)):
                        for t in range(T):
                            ins = nc.tensor.transpose(turn_bank(hd)[:, a * S + t * P:a * S + (t + 1) * P],
                                                      proj[:, t, col:col + P], ident)
                    ins.then_inc(s_qt, 1)
            in_stream.pe(pe, hT, after_chunk)

    s_s, s_mx, s_e, s_nrm, s_pt, s_pte, s_o, s_oe, s_sq, s_root3, s_rms, s_mt, s_mh, s_ml = (
        sem("att_" + n) for n in ("scores", "max", "exp", "normed", "turned", "turned_copied", "out", "out_copied",
                                  "squares", "roots", "rms_done", "mix_turned", "mix_hi", "mix_lo"))
    s_eps = sem("att_mean_squares")
    sc_ps = stream_acc

    def is_diff(u):
        return u >= DIL_HEADS

    def qT(u):
        return qkT_half[u // 8][:, u % 8, 0, :]

    def kT(u):
        return qkT_half[u // 8][:, u % 8, 1, :]

    def mix_gain(u):
        return g_col[:, 1:2] if is_diff(u) else g_col[:, 0:1]

    out_bank = spare_ps[:, 0, 0:T * DH]

    def mix_bank(u):
        j = u - (HEADS - 3)
        return sc_ps[:, j // 2, j % 2, 0:S] if j >= 0 else spare_ps[:, 1, 0:S]

    PIECE_HI, PIECE_LO = 4, 4
    with nc.Block() as block:
        @block.sync
        def _(sp):
            out_stream.prefetch(sp)

        @block.vector
        def _(dve):

            def row_maxima(u):
                s = u % 2
                dve.wait_ge(s_s, u + 1)
                if not is_diff(u):
                    if u >= 2:
                        dve.wait_ge(s_e, u - 1)
                    for t in range(T):
                        ins = nc.vector.tensor_tensor_reduce(
                            scores[:, s, t, :], sc_ps[:, s, 0, t * S:(t + 1) * S],
                            att_cst[:, t * S:(t + 1) * S], -DH ** -0.5, -LOWEST, ALU.add, ALU.min,
                            neg_max[:, u, t:t + 1])
                    ins.then_inc(s_mx, 1)
                    return
                n = chain.step(nc.vector.tensor_reduce(
                    row_max[:, u - DIL_HEADS, :], sc_ps[:, s, :, :].rearrange("p m (t k) -> p (m t) k", t=T),
                    AX_X, ALU.max))
                dve.wait_ge(chain.sem, n)
                nc.vector.tensor_scalar(neg_max[:, u, :], row_max[:, u - DIL_HEADS, :], -DIFF_DQ ** -0.5, None, ALU.mult
                                        ).then_inc(s_mx, 1)

            def normalise(u):
                s = u % 2
                dve.wait_ge(s_e, u + 1)
                if not is_diff(u):
                    nc.vector.reciprocal(rden[:, u, 0:2], den[:, u, 0:2]).then_inc(s_nrm, 1)
                    return
                j = u - DIL_HEADS
                n = chain.step(nc.vector.reciprocal(rden[:, u, :], den[:, u, :]))
                dve.wait_ge(chain.sem, n)
                n = chain.step(nc.vector.scalar_tensor_tensor(lam_rden[:, j, :], rden[:, u, 2:4], lams[:, 5:6],
                                                              den[:, u, 0:2], ALU.mult, ALU.mult))
                dve.wait_ge(chain.sem, n)
                for t in range(T):
                    ins = nc.vector.scalar_tensor_tensor(probs[:, s, 0, t, :], probs[:, s, 1, t, :],
                                                         lam_rden[:, j, t:t + 1], probs[:, s, 0, t, :],
                                                         ALU.mult, ALU.add)
                ins.then_inc(s_nrm, 1)

            def outputs(u):
                dve.wait_ge(s_o, u + 1)
                o = mixed[:, :, u * DH:(u + 1) * DH]
                i = out_bank.rearrange("p (t d) -> p t d", t=T)
                nc.vector.tensor_tensor(o, i, rden[:, u, 0:2].unsqueeze(2).broadcast_to([P, T, DH]),
                                        ALU.mult).then_inc(s_oe, 1)
                dve.wait_ge(s_oe, u + 1)
                for t in range(T):
                    if u + t > 0:
                        dve.wait_ge(s_sq, u * T + t)
                    nc.vector.tensor_tensor_reduce(square[:], mixed[:, t, u * DH:(u + 1) * DH],
                                                   mixed[:, t, u * DH:(u + 1) * DH], 1.0, 0.0, ALU.mult, ALU.add,
                                                   sumsq[:, u, t:t + 1]).then_inc(s_sq, 1)

            def mix_lo(u):
                dve.wait_ge(s_mh, u + 1)
                nc.vector.scalar_tensor_tensor(mixT[:, u, S:2 * S], mix_bank(u), mix_gain(u),
                                               f(mixT[:, u, 0:S]), ALU.mult, ALU.subtract).then_inc(s_ml, 1)

            for n in range(HEADS + 8):
                if 4 <= n < HEADS + 4:
                    outputs(n - 4)
                if n < HEADS:
                    row_maxima(n)
                if n >= 8:
                    mix_lo(n - 8)
                if 1 <= n <= HEADS:
                    normalise(n - 1)

        @block.gpsimd
        def _(pool):
            for u in range(HEADS):
                pool.wait_ge(s_sq, T * (u + 1))
                nc.gpsimd.tensor_scalar(rms[:, u, :], sumsq[:, u, :], 1.0 / DH, LN_EPS, ALU.mult, ALU.add
                                        ).then_inc(s_eps, 1)
                pool.wait_ge(s_eps, u + 1)
                nc.gpsimd.tensor_tensor(rms[:, u, :], rms[:, u, :], mhalf[:, 0:T], ALU.pow).then_inc(s_root3, 1)
                pool.wait_ge(s_root3, u + 1)
                v = mixed[:, :, u * DH:(u + 1) * DH]
                nc.gpsimd.tensor_tensor(v, v, rms[:, u, :].unsqueeze(2).broadcast_to([P, T, DH]), ALU.mult
                                        ).then_inc(s_rms, 1)
                if PIECE_LO <= u < PIECE_LO + 2 * CHUNK_KT:
                    out_stream.presplit_piece_lo(pool, nc.gpsimd, *divmod(u - PIECE_LO, CHUNK_KT))

        @block.scalar
        def _(act):
            def exponentials(u):
                s = u % 2
                act.wait_ge(s_mx, u + 1)
                if u >= 2:
                    act.wait_ge(s_pt, u - 1)
                maps = 2 if is_diff(u) else 1
                for m in range(maps):
                    for t in range(T):
                        src = sc_ps[:, s, m, t * S:(t + 1) * S] if is_diff(u) else scores[:, s, t, :]
                        j = m * T + t
                        ins = nc.scalar.activation(probs[:, s, m, t, :], src, ACT.Exp, bias=neg_max[:, u, j:j + 1],
                                                   scale=DIFF_DQ ** -0.5 if is_diff(u) else -1.0,
                                                   accum_out=den[:, u, j:j + 1])
                ins.then_inc(s_e, 1)

            def copy_turned(u):
                act.wait_ge(s_pt, u + 1)
                if u >= 2:
                    act.wait_ge(s_o, u - 1)
                nc.scalar.copy(probsT[:, u % 2, :, :], turn_ps[:, u % 2, :].rearrange("p (k q) -> p k q", k=T)
                               ).then_inc(s_pte, 1)

            def mix_hi(u):
                act.wait_ge(s_mt, u + 1)
                nc.scalar.activation(mixT[:, u, 0:S], mix_bank(u), ACT.Copy, scale=mix_gain(u)).then_inc(s_mh, 1)

            for n in range(HEADS + 8):
                if n >= 8:
                    mix_hi(n - 8)
                if 2 <= n < HEADS + 2:
                    copy_turned(n - 2)
                if n < HEADS:
                    exponentials(n)
                if PIECE_HI <= n < PIECE_HI + 2 * CHUNK_KT:
                    out_stream.presplit_piece_act(act, *divmod(n - PIECE_HI, CHUNK_KT))

        @block.tensor
        def _(pe):
            def score(u):
                s = u % 2
                if u >= 2:
                    pe.wait_ge(s_mx, u - 1)
                    if is_diff(u - 2):
                        pe.wait_ge(s_e, u - 1)
                if not is_diff(u):
                    for t in range(T):
                        ins = nc.tensor.matmul(sc_ps[:, s, 0, t * S:(t + 1) * S], qT(u)[:, t * P:(t + 1) * P], kT(u),
                                               start=True, stop=True)
                else:
                    for m in range(2):
                        r = slice(m * DIFF_DQ, (m + 1) * DIFF_DQ)
                        for t in range(T):
                            ins = nc.tensor.matmul(sc_ps[:, s, m, t * S:(t + 1) * S],
                                                   qT(u)[r, t * P:(t + 1) * P], kT(u)[r, :], start=True, stop=True)
                ins.then_inc(s_s, 1)

            def turn(u):
                s = u % 2
                pe.wait_ge(s_nrm, u + 1)
                if u >= 2:
                    pe.wait_ge(s_pte, u - 1)
                for k in range(T):
                    for t in range(T):
                        ins = nc.tensor.transpose(turn_ps[:, s, k * S + t * P:k * S + (t + 1) * P],
                                                  probs[:, s, 0, t, k * P:(k + 1) * P], ident)
                ins.then_inc(s_pt, 1)

            def weigh(u):
                s = u % 2
                pe.wait_ge(s_pte, u + 1)
                if u >= 1:
                    pe.wait_ge(s_oe, u)
                c = COL_V + u * DH
                for t in range(T):
                    for k in range(T):
                        ins = nc.tensor.matmul(out_bank[:, t * DH:(t + 1) * DH],
                                               probsT[:, s, k, t * P:(t + 1) * P], proj[:, k, c:c + DH],
                                               start=(k == 0), stop=(k == T - 1))
                ins.then_inc(s_o, 1)

            def turn_mix(u):
                pe.wait_ge(s_rms, u + 1)
                if 1 <= u < HEADS - 3:
                    pe.wait_ge(s_ml, u)
                for t in range(T):
                    ins = nc.tensor.transpose(mix_bank(u)[:, t * P:(t + 1) * P],
                                              mixed[:, t, u * DH:(u + 1) * DH], ident)
                ins.then_inc(s_mt, 1)

            for n in range(HEADS + 7):
                if n < HEADS:
                    score(n)
                if 2 <= n < HEADS + 2:
                    turn(n - 2)
                if 3 <= n < HEADS + 3:
                    weigh(n - 3)
                if n >= 7:
                    turn_mix(n - 7)

    s_lng4, s_var4, s_root4, s_n4 = (sem("ln1_" + n) for n in ("gb_in", "var", "root", "normed"))
    s_t4, s_h4, s_l4 = sem("h1_turned"), sem("h1_hi"), sem("h1_lo")
    s_spill, s_keys, s_kt, s_kte = sem("h1_spilled"), sem("keys_in"), sem("keys_turned"), sem("keys_copied")

    with nc.Block() as block:
        @block.sync
        def _(sp):
            sp.dma_start(keys[:], sub_keys.rearrange("h c n d -> n (h c) d")).then_inc(s_keys, 16)
            for j, v in enumerate((ln1_g, ln1_b)):
                sp.dma_start(ln_gb[:, j, :], broadcast_rows(v)).then_inc(s_lng4, 16)
            out_stream.sp(sp)
            sp.wait_ge(out_stream.lo[0], 8)
            sp.wait_ge(out_stream.lo[1], 8)
            query_stream.prefetch(sp)
            sp.wait_ge(s_n4, 4 * T)
            sp.dma_start(spill_v, h[:]).then_inc(s_spill, 16)

        @block.gpsimd
        def _(pool):
            inverse_root(pool, s_var4, s_root4)
            query_stream.presplit_lo(pool, nc.gpsimd, 0)
            query_stream.presplit_lo(pool, nc.gpsimd, 1)

        @block.scalar
        def _(act):
            out_stream.split_act(act, lambda *a: None)
            for j in range(4):
                act.wait_ge(s_kt, j + 1)
                nc.scalar.copy(keysT[:, 4 * j:4 * j + 4, :], turn_bank(j).rearrange("p (a n) -> p a n", a=4)
                               ).then_inc(s_kte, 1)
            act.wait_ge(out_stream.used[0], 8)
            act.wait_ge(out_stream.used[1], 8)
            query_stream.presplit_act(act, 0)
            query_stream.presplit_act(act, 1)
            turn_act(act, hT, s_t4, s_h4)

        @block.vector
        def _(dve):
            residual = out_stream.read_after(dve, lambda g, acc: nc.vector.scalar_tensor_tensor(
                h[:, :, ds(g * GROUP, GROUP)], h[:, :, ds(g * GROUP, GROUP)], ALPHA, acc, ALU.mult, ALU.add))
            stats_at = [0]

            def after_chunk(i, first, last, u, c):
                residual(i, first, last, u, c)
                g = 2 * i + u
                for q in ([g - 1] if c == 1 and g >= 1 else []) + ([g] if last and u == 1 and c == CHUNKS - 1 else []):
                    dve.wait_ge(out_stream.read_out[q % 2], q // 2 + 1)
                    stats_at[0] = quarter_stats(chain, h, q)
            out_stream.split_dve(dve, after_chunk)
            norm_variance(dve, chain, stats_at[0], s_var4)
            dve.wait_ge(s_lng4, 32)
            norm_and_turn_dve(dve, chain, h, ln_gb, hT, [(s_root4, 1)], s_n4, s_h4, s_l4)

        @block.tensor
        def _(pe):
            out_stream.pe(pe, mixT)
            pe.wait_ge(s_keys, 16)
            for j in range(4):
                for k in range(4):
                    ins = nc.tensor.transpose(turn_bank(j)[:, k * P:(k + 1) * P], keys[:, 4 * j + k, :], ident)
                ins.then_inc(s_kt, 1)
            pe.wait_ge(s_kte, 4)
            turn_pe(pe, h, s_n4, s_t4, s_l4)

    s_qt5, s_qe5, s_ks = (sem("choice_" + n) for n in ("q_turned", "q_copied", "scores"))
    u_rows = peer_u.rearrange("(a b) d -> a b d", b=N_KEYS)
    v_rows = peer_v.rearrange("(a b) d -> a b d", b=N_KEYS)
    s_kse = [sem(f"choice_scores_copied{a}") for a in range(2)]
    u_loaded = [[sem(f"u_loaded{half}_{s}") for s in range(2)] for half in range(2)]
    HALVES = [slice(0, D // 2), slice(D // 2, D)]

    with nc.Block() as block:
        @block.sync
        def _(sp):
            query_stream.sp(sp)
            for s in range(2):
                for half in range(2):
                    sp.dma_start(e_raw[:, s, HALVES[half]], u_rows[:, s, HALVES[half]]
                                 ).then_inc(u_loaded[half][s], 16)
            sp.wait_ge(s_spill, 16)

        def copy_scores(eng, copy, j):
            eng.wait_ge(s_ks, j + 1)
            copy(key_scores[:, 2 * j:2 * j + 2, :, :], spare_ps[:, j % 2, :].rearrange(
                "p (u c n) -> p u c n", u=2, c=2)).then_inc(s_kse[j % 2], 1)

        @block.scalar
        def _(act):
            read = query_stream.read_after(act, lambda g, acc: nc.scalar.copy(query[:, :, ds(g * GROUP, GROUP)], acc))

            def copy_query(g):
                for a in range(2):
                    act.wait_ge(s_qt5, 2 * g + a + 1)
                    nc.scalar.copy(queryT[:, 4 * g + 2 * a:4 * g + 2 * a + 2, :],
                                   turn_ps[:, a, :].rearrange("p (k s) -> p k s", k=2)).then_inc(s_qe5, 1)

            def after_chunk(i, first, last, u, c):
                read(i, first, last, u, c)
                if c == 0 and 2 * i + u >= 2:
                    copy_query(2 * i + u - 2)
            query_stream.split_act(act, after_chunk)
            copy_query(2)
            copy_query(3)
            for j in range(0, 8, 2):
                copy_scores(act, nc.scalar.copy, j)

        @block.vector
        def _(dve):
            query_stream.split_dve(dve, lambda *a: None)
            for j in range(1, 8, 2):
                copy_scores(dve, nc.vector.tensor_copy, j)

        @block.tensor
        def _(pe):
            def turn_query(g):
                pe.wait_ge(query_stream.read_out[g % 2], g // 2 + 1)
                if g >= 1:
                    pe.wait_ge(s_qe5, 2 * g)
                for a in range(2):
                    for k in range(2):
                        kt = 4 * g + 2 * a + k
                        for t in range(T):
                            ins = nc.tensor.transpose(turn_ps[:, a, k * S + t * P:k * S + (t + 1) * P],
                                                      query[:, t, kt * P:(kt + 1) * P], ident)
                    ins.then_inc(s_qt5, 1)

            def after_chunk(i, first, last, u, c):
                if c == 2 and 2 * i + u >= 1:
                    turn_query(2 * i + u - 1)
            query_stream.pe(pe, hT, after_chunk)
            turn_query(3)
            for j in range(8):
                t, a = j // 4, 4 * (j % 4)
                if j < 4:
                    pe.wait_ge(s_qe5, 2 * (j + 1))
                if j >= 2:
                    pe.wait_ge(s_kse[j % 2], j // 2)
                for k in range(4):
                    ins = nc.tensor.matmul(spare_ps[:, j % 2, k * P:(k + 1) * P],
                                           queryT[:, a + k, t * P:(t + 1) * P], keysT[:, a + k, :],
                                           start=True, stop=True)
                ins.then_inc(s_ks, 1)

    STEPS = N_KEYS // 2
    PREP = UNITS
    GATE0 = PREP + 1
    GATE_STEPS = S // 8
    GATE1 = GATE0 + GATE_STEPS
    up_turned = [sem(f"u_turned{s}") for s in range(4)]
    up_hi = [sem(f"u_hi{s}") for s in range(4)]
    up_lo = [sem(f"u_lo{s}") for s in range(4)]
    up_used = [sem(f"u_used{s}") for s in range(4)]
    h2_out = [sem(f"score_lo_copied{a}") for a in range(2)]
    h_sum = [sem(f"score_summed{a}") for a in range(2)]
    h_gelu = [sem(f"score_gelu{a}") for a in range(2)]
    h_gated = sem("score_gated")
    v_loaded = [sem(f"v_loaded{s}") for s in range(4)]
    unit_in, eq_made, numbers_out = (sem("pick_" + n) for n in ("unit_in", "positions", "numbers"))
    s_prep, s_ge, s_gs, s_pick, s_pkt, s_pke, s_ones = (sem("pick_" + n) for n in (
        "gate_chain", "exps_in", "exps", "done", "turned", "copied", "ones"))
    oh_ready, oh_scaled, g_made = (sem("token_" + n) for n in ("onehots", "scaled", "gates_made"))
    g_lo_out, g_sum, g_mult = (sem("pair_" + n) for n in ("lo_copied", "summed", "multiplied"))
    s_vhi, s_vlo, s_ahi, s_alo, s_vused = (sem(n) for n in ("v_hi", "v_lo", "a_hi", "a_lo", "v_used"))
    tq = stream_acc[:].rearrange("p a t n -> p (a t) n")
    count_row = cst[:, C_IOTA:C_IOTA + P]
    FIRST, PICKS, TURN, GATE_FIRST, GATES, GATE_AFTER, PLAIN, LAST = range(8)

    def token(i, k):
        return i * 8 + (k - 8 * GATE0)

    def pair(i, b):
        return i * 4 + (b - 4 * GATE0)

    def wait_past(eng, s, n):
        if not (isinstance(n, int) and n < 1):
            eng.wait_ge(s, n)

    def made(a):
        return spare_ps[:, a, :].rearrange("p (t h n) -> p t h n", t=2, h=2)

    def expert_steps(eng, body):
        body(0, FIRST)
        with eng.Fori(1, PREP) as i:
            body(i, PICKS)
        body(PREP, TURN)
        body(GATE0, GATE_FIRST)
        with eng.Fori(GATE0 + 1, GATE1) as i:
            body(i, GATES)
        body(GATE1, GATE_AFTER)
        with eng.Fori(GATE1 + 1, STEPS - 1) as i:
            body(i, PLAIN)
        body(STEPS - 1, LAST)

    with nc.Block() as block:
        @block.sync
        def _(sp):
            def body(i, kind):
                for a in range(2):
                    if kind == LAST:
                        sp.wait_ge(up_turned[3], i * 2 + (a + 1))
                        sp.dma_start(v_raw[:, a, :], v_rows[:, a, :]).then_inc(v_loaded[a], 16)
                        continue
                    for half in range(2):
                        sp.wait_ge(up_turned[2 * half + 1], i * 2 + (a + 1))
                        sp.dma_start(e_raw[:, a, HALVES[half]].unsqueeze(1),
                                     u_rows[:, ds(i * 2 + (2 + a), 1), HALVES[half]]).then_inc(u_loaded[half][a], 16)
            expert_steps(sp, body)

        @block.gpsimd
        def _(pool):
            nc.gpsimd.memset(gates[:, 2 * GATE0:96, :], 1.0).then_inc(s_ones, 1)

            def key_numbers(i):
                pool.wait_ge(eq_made, i + 1)
                nc.gpsimd.tensor_tensor(pick_eq[:], pick_eq[:], top_if[:].unsqueeze(2).broadcast_to(
                    [P, 2, TOPK, TOPK]), ALU.mult).then_inc(numbers_out, 1)
            key_numbers(0)
            with pool.Fori(1, UNITS) as i:
                key_numbers(i)
            pool.wait_ge(s_pkt, T)
            nc.gpsimd.memset(gates[:, 96:N_KEYS, :], 1.0).then_inc(s_ones, 1)

        @block.tensor
        def _(pe):
            def turn(i, k):
                s, a = k % 4, (k // 4) % 2
                if s % 2 == 0:
                    pe.wait_ge(u_loaded[s // 2][a], i * 16 + 16 * (k // 8 + 1))
                wait_used(pe, up_lo[s], i * 2 + k // 4)
                for j in range(4):
                    c = (4 * s + j) * P
                    ins = nc.tensor.transpose(tq[:, s, j * P:(j + 1) * P], e_raw[:, a, c:c + P], ident)
                ins.then_inc(up_turned[s], 1)

            def score(i, k):
                s, a = k % 4, k // 4
                pe.wait_ge(up_lo[s], i * 2 + (k // 4 + 1))
                if s == 0:
                    wait_used(pe, h_sum[a], i)
                for j in range(4):
                    kt = 4 * s + j
                    nc.tensor.matmul(turn_ps[:, a, :], uT_hi[:, s, j, :], hT[:, kt, :],
                                     start=(kt == 0), stop=False)
                    ins = nc.tensor.matmul(turn_ps[:, a, 0:S], uT_lo[:, s, j, :], hT[:, kt, 0:S],
                                           start=False, stop=(kt == KT - 1))
                ins.then_inc(up_used[s], 1)

            def turn_picks():
                pe.wait_ge(s_pick, 1)
                for t in range(T):
                    for k in range(3):
                        ins = nc.tensor.transpose(
                            spare_ps[:, t, k * P:(k + 1) * P],
                            pick[:, k, t * PEER_HEADS:(t + 1) * PEER_HEADS, :].rearrange("p a k -> p (a k)"), ident)
                    ins.then_inc(s_pkt, 1)

            def gate_matrix(i, k):
                a, j = (k // 2) % 2, k % 2
                pe.wait_ge(oh_scaled, token(i, k) + 1)
                if j == 0:
                    wait_past(pe, g_sum, pair(i, k // 2) - 1)
                nc.tensor.matmul(spare_ps[:, a, j * 2 * P:(j + 1) * 2 * P], oh_first[:, k % 4, :],
                                 oh_gate[:, k % 4, :, :].rearrange("p h n -> p (h n)"), start=True, stop=True
                                 ).then_inc(g_made, 1)

            turn(0, 0)
            turn(0, 1)

            def body(i, kind):
                for k in range(8):
                    if not (kind == LAST and k >= 6):
                        turn(i, k + 2)
                    score(i, k)
                    if kind == TURN and k == 4:
                        turn_picks()
                    if kind in (GATE_FIRST, GATES):
                        gate_matrix(i, k)
            expert_steps(pe, body)

        @block.scalar
        def _(act):
            def finish(i, a, first):
                act.wait_ge(up_used[3], i * 2 + (a + 1))
                if not first:
                    act.wait_ge(h_sum[1 - a], i + a)
                nc.scalar.copy(act_tmp[:, a, :], turn_ps[:, a, S:2 * S]).then_inc(h2_out[a], 1)

            def gelu(i, a, gated):
                act.wait_ge(h_sum[a], i + 1)
                src = act_tmp[:, a, :]
                if gated:
                    nc.scalar.activation(src, src, ACT.Gelu).then_inc(h_gelu[a], 1)
                else:
                    nc.scalar.activation(gates[:, ds(i * 2 + a, 1), :], src.unsqueeze(1), ACT.Gelu
                                         ).then_inc(h_gelu[a], 1)

            def copy_unit(i):
                nc.scalar.copy(unit_s[:].unsqueeze(1), key_scores[:, ds(i, 1), :, :]).then_inc(unit_in, 1)

            def scale(i, k):
                act.wait_ge(oh_ready, token(i, k) + 1)
                for part in range(2):
                    ins = nc.scalar.activation(oh_gate[:, k % 4, part, :], oh_second[:, k % 4, :], ACT.Copy,
                                               scale=f(pickT[:, 2 + part, ds(token(i, k), 1)]))
                ins.then_inc(oh_scaled, 1)

            def copy_lo(i, b):
                act.wait_ge(g_made, pair(i, b) * 2 + 2)
                wait_past(act, g_mult, pair(i, b))
                nc.scalar.copy(gate_sum[:], made(b % 2)[:, :, 1, :]).then_inc(g_lo_out, 1)

            def body(i, kind):
                if kind in (FIRST, PICKS):
                    wait_used(act, up_lo[0], i * 2)
                    copy_unit(i)
                for k in range(8):
                    s = k % 4
                    act.wait_ge(up_turned[s], i * 2 + (k // 4 + 1))
                    wait_used(act, up_used[s], i * 2 + k // 4)
                    nc.scalar.copy(uT_hi[:, s, :, :], tq[:, s, :].rearrange("p (j n) -> p j n", j=4)
                                   ).then_inc(up_hi[s], 1)
                    if kind == GATE_FIRST and k == 1:
                        act.wait_ge(s_prep, 3)
                    if k == 0 and kind in (GATES, GATE_AFTER):
                        scale(i - 1, 7)
                    if k >= 1 and kind in (GATE_FIRST, GATES):
                        scale(i, k - 1)
                    if k in (0, 2) and kind in (GATES, GATE_AFTER):
                        copy_lo(i - 1, 2 + k // 2)
                    if k in (4, 6) and kind in (GATE_FIRST, GATES):
                        copy_lo(i, k // 2 - 2)
                    if k == 2 and kind != FIRST:
                        finish(i - 1, 1, False)
                    if k == 3 and kind != FIRST:
                        gelu(i - 1, 1, kind >= GATES)
                    if k == 6:
                        finish(i, 0, kind == FIRST)
                    if k == 7:
                        gelu(i, 0, kind >= GATE_FIRST)
                    if kind == TURN and k == 0:
                        act.wait_ge(s_ge, 1)
                        nc.scalar.activation(gate_e[:], gate_e[:], ACT.Exp).then_inc(s_gs, 1)
                    if kind == TURN and k == 7:
                        for t in range(T):
                            act.wait_ge(s_pkt, t + 1)
                            nc.scalar.copy(pickT[:, 0:3, t * P:(t + 1) * P], spare_ps[:, t, 0:3 * P].rearrange(
                                "p (a k) -> p a k", a=3)).then_inc(s_pke, 1)
                if kind == LAST:
                    finish(i, 1, False)
                    act.wait_ge(h_gated, 2 * (STEPS - GATE0) - 1)
                    nc.scalar.copy(a_hi[:, 0, :], gates[:, 0, :]).then_inc(s_ahi, 1)
                    act.wait_ge(v_loaded[0], 16)
                    nc.scalar.copy(v_hi[:, 0, :], v_raw[:, 0, :]).then_inc(s_vhi, 1)
                    gelu(i, 1, True)
            expert_steps(act, body)

        @block.vector
        def _(dve):
            def add(i, a):
                dve.wait_ge(h2_out[a], i + 1)
                nc.vector.tensor_tensor(act_tmp[:, a, :], turn_ps[:, a, 0:S], act_tmp[:, a, :], ALU.add
                                        ).then_inc(h_sum[a], 1)

            def gate(i, a):
                dve.wait_ge(h_gelu[a], i + 1)
                g = gates[:, ds(i * 2 + a, 1), :]
                nc.vector.tensor_tensor(g, g, act_tmp[:, a, :].unsqueeze(1), ALU.mult).then_inc(h_gated, 1)

            def one_hots(i, k):
                wait_past(dve, g_made, token(i, k) - 3)
                nc.vector.tensor_scalar(oh_first[:, k % 4, :], count_row, f(pickT[:, 0, ds(token(i, k), 1)]), None,
                                        ALU.is_equal)
                nc.vector.tensor_scalar(oh_second[:, k % 4, :], count_row, f(pickT[:, 1, ds(token(i, k), 1)]), None,
                                        ALU.is_equal).then_inc(oh_ready, 1)

            def sum_parts(i, b):
                dve.wait_ge(g_lo_out, pair(i, b) + 1)
                nc.vector.tensor_tensor(gate_sum[:], made(b % 2)[:, :, 0, :], gate_sum[:], ALU.add).then_inc(g_sum, 1)

            def multiply_in(i, b):
                dve.wait_ge(g_sum, pair(i, b) + 1)
                g = gates[:, :, ds(i * 8 + (2 * b - 8 * GATE0), 2)].rearrange("p n t -> p t n")
                nc.vector.tensor_tensor(g, g, gate_sum[:], ALU.mult).then_inc(g_mult, 1)

            def picks(i, k):
                sv, tv, ti = unit_s, top_v, top_i
                flat = cand[:].rearrange("p a b -> p (a b)")
                if k == 0:
                    nc.vector.max(tv[:, 0, 0:8], sv[:, 0, :])
                    nc.vector.max(tv[:, 1, 0:8], sv[:, 1, :])
                    dve.drain()
                    nc.vector.max_index(ti[:, 0, 0:8], tv[:, 0, 0:8], sv[:, 0, :])
                elif k == 1:
                    nc.vector.max_index(ti[:, 1, 0:8], tv[:, 1, 0:8], sv[:, 1, :])
                    dve.drain()
                    nc.vector.match_replace(sv[:, 0, :], tv[:, 0, 0:8], sv[:, 0, :], LOWEST)
                    nc.vector.match_replace(sv[:, 1, :], tv[:, 1, 0:8], sv[:, 1, :], LOWEST)
                    dve.drain()
                    nc.vector.max(tv[:, 0, 8:16], sv[:, 0, :])
                elif k == 2:
                    nc.vector.max(tv[:, 1, 8:16], sv[:, 1, :])
                    dve.drain()
                    nc.vector.max_index(ti[:, 0, 8:16], tv[:, 0, 8:16], sv[:, 0, :])
                    nc.vector.max_index(ti[:, 1, 8:16], tv[:, 1, 8:16], sv[:, 1, :])
                    dve.drain()
                    nc.vector.tensor_copy(top_if[:], top_i[:])
                elif k == 3:
                    nc.vector.tensor_tensor(cand[:], tv[:, 0, :].unsqueeze(2).broadcast_to([P, TOPK, TOPK]),
                                                 tv[:, 1, :].unsqueeze(1).broadcast_to([P, TOPK, TOPK]), ALU.add)
                    dve.drain()
                    nc.vector.max(pick_v[:, 0:8], flat)
                elif k == 4:
                    dve.drain()
                    nc.vector.max_index(pick_pos[:, 0:8], pick_v[:, 0:8], flat)
                    dve.drain()
                    nc.vector.match_replace(flat, pick_v[:, 0:8], flat, LOWEST)
                elif k == 5:
                    dve.drain()
                    nc.vector.max(pick_v[:, 8:16], flat)
                    dve.drain()
                    nc.vector.max_index(pick_pos[:, 8:16], pick_v[:, 8:16], flat)
                elif k == 6:
                    dve.drain()
                    nc.vector.tensor_scalar(pick_ij[:, 0, :], pick_pos[:], 4, None, ALU.logical_shift_right)
                    nc.vector.tensor_scalar(pick_ij[:, 1, :], pick_pos[:], TOPK - 1, None, ALU.bitwise_and)
                    dve.drain()
                    nc.vector.tensor_copy(pick_ijf[:], pick_ij[:])
                elif k == 7:
                    dve.drain()
                    nc.vector.tensor_tensor(
                        pick_eq[:], cst[:, C_IOTA16:C_IOTA16 + TOPK].unsqueeze(1).unsqueeze(1).broadcast_to(
                            [P, 2, TOPK, TOPK]),
                        pick_ijf[:].unsqueeze(3).broadcast_to([P, 2, TOPK, TOPK]), ALU.is_equal).then_inc(eq_made, 1)
                    nc.vector.tensor_copy(pick_sums[:, ds(i, 1), :], pick_v[:].unsqueeze(1))
                    dve.drain()

            def sum_numbers(i):
                nc.vector.tensor_reduce(pick[:, 0:2, ds(i, 1), :], pick_eq[:].unsqueeze(2), AX_X, ALU.add)
                dve.drain()

            def softmax(k):
                if k == 0:
                    nc.vector.tensor_tensor(gate_e[:], pick_sums[:], pick_sums[:, :, 0:1].broadcast_to(
                        [P, UNITS, TOPK]), ALU.subtract).then_inc(s_ge, 1)
                if k == 2:
                    dve.wait_ge(s_gs, 1)
                    nc.vector.tensor_reduce(gate_s[:, 0, :], gate_e[:], AX_X, ALU.add).then_inc(s_prep, 1)
                    dve.wait_ge(s_prep, 1)
                    nc.vector.reciprocal(gate_s[:, 1, :], gate_s[:, 0, :]).then_inc(s_prep, 1)
                    dve.wait_ge(s_prep, 2)
                    nc.vector.tensor_tensor(pick[:, 2, :, :], gate_e[:], gate_s[:, 1, :].unsqueeze(2).broadcast_to(
                        [P, UNITS, TOPK]), ALU.mult).then_inc(s_pick, 1)

            def body(i, kind):
                for k in range(8):
                    s = k % 4
                    dve.wait_ge(up_hi[s], i * 2 + (k // 4 + 1))
                    if k == 0 and kind in (FIRST, PICKS):
                        dve.wait_ge(unit_in, i + 1)
                    if k == 2 and kind in (PICKS, TURN):
                        dve.wait_ge(numbers_out, i)
                    nc.vector.tensor_tensor(uT_lo[:, s, :, :], tq[:, s, :].rearrange("p (j n) -> p j n", j=4),
                                            f(uT_hi[:, s, :, :]), ALU.subtract).then_inc(up_lo[s], 1)
                    if k == 2 and kind in (PICKS, TURN):
                        sum_numbers(i - 1)
                    if kind in (FIRST, PICKS):
                        picks(i, k)
                    if kind == TURN:
                        softmax(k)
                    if kind == GATE_FIRST and k == 0:
                        dve.wait_ge(s_pke, T)
                        nc.vector.tensor_tensor(
                            pickT[:, 3, :].rearrange("p (t n) -> p t n", t=T), spare_ps[:, :, 2 * P:3 * P],
                            f(pickT[:, 2, :]).rearrange("p (t n) -> p t n", t=T), ALU.subtract).then_inc(s_prep, 1)
                    if kind in (GATE_FIRST, GATES):
                        one_hots(i, k)
                    if k in (0, 2) and kind in (GATES, GATE_AFTER):
                        sum_parts(i - 1, 2 + k // 2)
                    if k in (1, 3) and kind in (GATES, GATE_AFTER):
                        if k == 1:
                            dve.wait_ge(h_gated, i * 2 - (2 * GATE0 + 1))
                        multiply_in(i - 1, 2 + k // 2)
                    if k in (4, 6) and kind in (GATE_FIRST, GATES):
                        sum_parts(i, k // 2 - 2)
                    if k in (5, 7) and kind in (GATE_FIRST, GATES):
                        if kind == GATE_FIRST and k == 5:
                            dve.wait_ge(s_ones, 2)
                            dve.wait_ge(h_gelu[1], GATE0)
                        if kind == GATES and k == 5:
                            dve.wait_ge(h_gated, i * 2 - 2 * GATE0)
                        multiply_in(i, k // 2 - 2)
                    if k == 2 and kind != FIRST:
                        add(i - 1, 1)
                    if k == 3 and kind >= GATES:
                        if kind <= GATE_AFTER:
                            dve.wait_ge(g_mult, pair(i, 0))
                        gate(i - 1, 1)
                    if k == 6:
                        add(i, 0)
                    if k == 7 and kind >= GATE_FIRST:
                        if kind <= GATES:
                            dve.wait_ge(g_mult, pair(i, 2))
                        gate(i, 0)
                if kind == LAST:
                    add(i, 1)
                    gate(i, 1)
            expert_steps(dve, body)

    s_h1in, s_gb8, s_var8, s_root8, s_shift, s_unit, s_gain, s_done = (sem("ln2_" + n) for n in (
        "h1_in", "gb_in", "var", "root", "shift", "unit", "gain", "stored"))
    s_n8 = [sem(f"ln2_normed{t}") for t in range(T)]

    s_y0 = sem("y_of_first_tokens")

    def y_bank(t, q):
        if q < 2:
            return stream_acc[:, q, t, :]
        return (turn_ps if q == 2 else spare_ps)[:, t, :]

    PER_STEP = 4
    STEPS = N_KEYS // PER_STEP

    def steps_of(eng, body):
        body(0, True, False)
        with eng.Fori(1, STEPS - 1) as i:
            body(i, False, False)
        body(STEPS - 1, False, True)

    with nc.Block() as block:
        @block.sync
        def _(sp):
            for a in (2, 3):
                sp.dma_start(v_raw[:, a, :].unsqueeze(1), v_rows[:, ds(a, 1), :]).then_inc(v_loaded[a], 16)

            def body(i, first, last):
                if not last:
                    for a in range(PER_STEP):
                        sp.wait_ge(s_vlo, i * PER_STEP + (a + 1))
                        sp.dma_start(v_raw[:, a, :].unsqueeze(1), v_rows[:, ds(i * PER_STEP + (PER_STEP + a), 1), :]
                                     ).then_inc(v_loaded[a], 16)
            steps_of(sp, body)
            sp.dma_start(h1[:], spill_v).then_inc(s_h1in, 16)
            for j, v in enumerate((ln2_g, ln2_b)):
                sp.dma_start(ln2_gb[:, j, :], broadcast_rows(v)).then_inc(s_gb8, 16)
            for q in range(4):
                for t in range(T):
                    sp.wait_ge(s_n8[t], q + 1)
                    sp.dma_start(out_v[:, t, q * 512:(q + 1) * 512], final[:, t, q * 512:(q + 1) * 512]
                                 ).then_inc(s_done, 16)
            sp.wait_ge(s_done, 16 * 4 * T)

        @block.gpsimd
        def _(pool):
            def inverse_root(t):
                pool.wait_ge(s_var8, t + 1)
                nc.gpsimd.tensor_tensor(rstd[:, t, 1:2], rstd[:, t, 0:1], mhalf[:, 0:1], ALU.pow).then_inc(s_root8, 1)

            inverse_root(0)
            pool.wait_ge(s_gb8, 32)
            for q in range(4):
                c = slice(q * 512, (q + 1) * 512)
                pool.wait_ge(s_unit, q + 1)
                nc.gpsimd.tensor_tensor(final[:, 0, c], final[:, 0, c], ln2_gb[:, 0, c], ALU.mult).then_inc(s_gain, 1)
                if q == 1:
                    inverse_root(1)
                if q < 3:
                    pool.wait_ge(s_gain, q + 1)
                    nc.gpsimd.tensor_tensor(final[:, 0, c], final[:, 0, c], ln2_gb[:, 1, c], ALU.add
                                            ).then_inc(s_n8[0], 1)

        @block.scalar
        def _(act):
            def body(i, first, last):
                for a in range(1 if first else 0, PER_STEP):
                    s, n = a % 2, i * PER_STEP + a
                    act.wait_ge(v_loaded[a], i * 16 + 16)
                    wait_past(act, s_vused, n - 1)
                    nc.scalar.copy(a_hi[:, s, :].unsqueeze(1), gates[:, ds(n, 1), :]).then_inc(s_ahi, 1)
                    nc.scalar.copy(v_hi[:, s, :], v_raw[:, a, :]).then_inc(s_vhi, 1)
            steps_of(act, body)
            act.wait_ge(s_shift, 1)
            for q in range(4):
                c = slice(q * 512, (q + 1) * 512)
                nc.scalar.activation(final[:, 0, c], final[:, 0, c], ACT.Identity, bias=rstd[:, 0, 0:1],
                                     scale=rstd[:, 0, 1:2]).then_inc(s_unit, 1)

        @block.vector
        def _(dve):
            def body(i, first, last):
                for a in range(PER_STEP):
                    s, n = a % 2, i * PER_STEP + a
                    dve.wait_ge(s_ahi, n + 1)
                    nc.vector.tensor_tensor(a_lo[:, s, :].unsqueeze(1), gates[:, ds(n, 1), :],
                                            f(a_hi[:, s, :]).unsqueeze(1), ALU.subtract).then_inc(s_alo, 1)
                    dve.wait_ge(s_vhi, n + 1)
                    nc.vector.tensor_tensor(v_lo[:, s, :], v_raw[:, a, :], f(v_hi[:, s, :]), ALU.subtract
                                            ).then_inc(s_vlo, 1)
            steps_of(dve, body)
            dve.wait_ge(s_h1in, 16)
            for t in range(T):
                if t == 0:
                    dve.wait_ge(s_y0, 1)
                else:
                    dve.wait_ge(s_vused, N_KEYS)
                for q in range(4):
                    c = slice(q * 512, (q + 1) * 512)
                    n = chain.step(nc.vector.scalar_tensor_tensor(final[:, t, c], h1[:, t, c], ALPHA, y_bank(t, q),
                                                                  ALU.mult, ALU.add))
                    if q >= 1:
                        dve.wait_ge(chain.sem, n - (1 if q == 1 else 2))
                        p = slice((q - 1) * 512, q * 512)
                        n = chain.step(nc.vector.bn_stats(stats[:, t, q - 1, :], final[:, t, p]))
                    if t == 1 and q == 0:
                        dve.wait_ge(s_root8, 1)
                        nc.vector.tensor_scalar(rstd[:, 0, 0:1], rstd[:, 0, 1:2], meanvar[:, 0, 0:1], -1.0,
                                                ALU.mult, ALU.mult).then_inc(s_shift, 1)
                dve.wait_ge(chain.sem, n)
                dve.wait_ge(chain.sem, chain.step(nc.vector.bn_stats(stats[:, t, 3, :], final[:, t, c])))
                dve.wait_ge(chain.sem, chain.step(nc.vector.bn_aggr(meanvar[:, t, :], stats[:, t, :, :])))
                nc.vector.tensor_scalar(rstd[:, t, 0:1], meanvar[:, t, 1:2], LN_EPS, None, ALU.add).then_inc(s_var8, 1)
            dve.wait_ge(s_gb8, 32)
            last = None
            for q in range(5):
                if q < 4:
                    c = slice(q * 512, (q + 1) * 512)
                    n = chain.step(nc.vector.scalar_tensor_tensor(
                        final[:, 1, c], final[:, 1, c], meanvar[:, 1, 0:1], ln2_gb[:, 0, c],
                        ALU.subtract, ALU.mult))
                if q == 1:
                    dve.wait_ge(s_root8, 2)
                if q >= 1:
                    dve.wait_ge(chain.sem, last)
                    c = slice((q - 1) * 512, q * 512)
                    nc.vector.scalar_tensor_tensor(final[:, 1, c], final[:, 1, c], rstd[:, 1, 1:2],
                                                   ln2_gb[:, 1, c], ALU.mult, ALU.add).then_inc(s_n8[1], 1)
                if q == 3:
                    dve.wait_ge(s_gain, 4)
                    f0 = final[:, 0, 3 * 512:4 * 512]
                    nc.vector.tensor_tensor(f0, f0, ln2_gb[:, 1, 3 * 512:4 * 512], ALU.add).then_inc(s_n8[0], 1)
                last = n

        @block.tensor
        def _(pe):
            def hi_v_hi(s, t, start):
                for q in range(4):
                    nc.tensor.matmul(y_bank(t, q), a_hi[:, s, t * P:(t + 1) * P], v_hi[:, s, q * 512:(q + 1) * 512],
                                     start=start, stop=False)

            def hi_v_lo(s, t, stop=False):
                for q in range(4):
                    ins = nc.tensor.matmul(y_bank(t, q), a_hi[:, s, t * P:(t + 1) * P],
                                           v_lo[:, s, q * 512:(q + 1) * 512], start=False, stop=stop)
                return ins

            def lo_v_hi(s, t, stop=False):
                for q in range(4):
                    ins = nc.tensor.matmul(y_bank(t, q), a_lo[:, s, t * P:(t + 1) * P],
                                           v_hi[:, s, q * 512:(q + 1) * 512], start=False, stop=stop)
                return ins

            def wait_tile(i, a):
                pe.wait_ge(s_vlo, i * PER_STEP + (a + 1))
                pe.wait_ge(s_alo, i * PER_STEP + (a + 1))

            def as_parts_come(i, a, t, start, stop):
                s, n = a % 2, i * PER_STEP + a
                pe.wait_ge(s_ahi, n + 1)
                pe.wait_ge(s_vhi, n + 1)
                hi_v_hi(s, t, start)
                pe.wait_ge(s_alo, n + 1)
                lo_v_hi(s, t)
                pe.wait_ge(s_vlo, n + 1)
                return hi_v_lo(s, t, stop)

            def body(i, first, last):
                for a in range(PER_STEP - 2 if last else PER_STEP):
                    s = a % 2
                    if first and a == 0:
                        for t in range(T):
                            ins = as_parts_come(i, a, t, True, False)
                    else:
                        wait_tile(i, a)
                        for t in range(T):
                            hi_v_hi(s, t, False)
                            hi_v_lo(s, t)
                            ins = lo_v_hi(s, t)
                    ins.then_inc(s_vused, 1)
                if last:
                    for t in range(T):
                        for a in (PER_STEP - 2, PER_STEP - 1):
                            ins = as_parts_come(i, a, t, False, a == PER_STEP - 1)
                            if t == 1:
                                ins.then_inc(s_vused, 1)
                        if t == 0:
                            ins.then_inc(s_y0, 1)
            steps_of(pe, body)


_INS = ["x", "ln_emb_g", "ln_emb_b", "w_in", "dil_norm_g", "lambda_q1", "lambda_k1", "lambda_q2", "lambda_k2",
        "subln_g", "w_out", "ln1_g", "ln1_b", "peer_w_query", "peer_sub_keys", "peer_u", "peer_v", "ln2_g", "ln2_b"]
_LAYERED = {"w_in", "w_out", "peer_w_query", "peer_sub_keys", "peer_u", "peer_v"}


def kernel(**inputs):
    import concourse.bacc as _bacc
    from concourse.bass_utils import run_bass_kernel_spmd as _run

    nc = _bacc.Bacc("TRN2", target_bir_lowering=False, num_devices=1)
    arrays, args = {}, []
    for name in _INS:
        a = np.ascontiguousarray(inputs[name])
        if name in _LAYERED:
            a = a[0]
        if name == "w_in":
            dil, diff = DIL_HEADS * DH, DIFF_HEADS * DH
            cuts = np.split(a, np.cumsum([dil, dil, dil, diff, diff]), axis=1)
            a = np.concatenate([cuts[0], cuts[1], cuts[3], cuts[4], cuts[2], cuts[5]], axis=1)
        arrays[f"in_{name}_dram"] = a
        args.append(nc.dram_tensor(f"in_{name}_dram", a.shape, F32, kind="ExternalInput").ap())
    arrays["constants_dram"] = shape_constants()
    args.append(nc.dram_tensor("constants_dram", (P, C_END), F32, kind="ExternalInput").ap())
    args.append(nc.dram_tensor("h1_spill", (S, D), F32, kind="Internal").ap())
    args.append(nc.dram_tensor("out_0_dram", (1, S, D), F32, kind="ExternalOutput").ap())
    encoder_layer(nc, *args)
    r = _run(nc, [arrays], core_ids=[0])
    return r.results[0]["out_0_dram"]
```
